# Optimizing a Trainium2 kernel written in Bass

```python
import jax
import jax.numpy as jnp
from jax import lax
import numpy as np

D_MODEL = 1024
BATCH = 1
SEQ = 512
DEPTH = 2
DEC_BATCH = 8
DEC_SEQ = 16
PAST_LEN = 256

CHUNK = 64
N_HEADS = 8
N_KV_HEADS = 2
HEAD_DIM = 64
GQA_GROUP = N_HEADS // N_KV_HEADS
ATT_WIDTH = N_HEADS * HEAD_DIM
KV_WIDTH = N_KV_HEADS * HEAD_DIM
IDX_HEADS = 8
IDX_DIM = 32
TOPK_MAX = 256
Q_BLOCK = 128
SGU_GROUPS = 4
SGU_CHUNK = 128
SGU_WIDTH = 512
SGU_GDIM = SGU_WIDTH // SGU_GROUPS
N_GROUPS = 4
EXP_PER_GROUP = 8
EXP_TOPK = 2
EXP_HIDDEN = 128
ROPE_THETA = 10000.0
EPS = 1e-6
IN_SPLITS = (ATT_WIDTH, KV_WIDTH, KV_WIDTH, IDX_HEADS * IDX_DIM, IDX_DIM, IDX_HEADS, SGU_WIDTH, SGU_WIDTH, D_MODEL, D_MODEL)
IN_OFFSETS = tuple(int(o) for o in np.cumsum(IN_SPLITS)[:-1])
IN_COLS = int(sum(IN_SPLITS))

kernel_name = 'hybrid_dsa_sgu_hmoe_stream_step'

def rms_norm(x, g):
    xf = x.astype(jnp.float32)
    y = xf * lax.rsqrt(jnp.mean(xf * xf, axis=-1, keepdims=True) + EPS)
    return (y * g.astype(jnp.float32)).astype(x.dtype)

def layer_norm(x, g, b):
    xf = x.astype(jnp.float32)
    mu = jnp.mean(xf, axis=-1, keepdims=True)
    var = jnp.mean(jnp.square(xf - mu), axis=-1, keepdims=True)
    y = (xf - mu) * lax.rsqrt(var + EPS)
    return (y * g.astype(jnp.float32) + b.astype(jnp.float32)).astype(x.dtype)

def rope(x, pos):
    d = x.shape[-1]
    inv = ROPE_THETA ** (-jnp.arange(0, d, 2, dtype=jnp.float32) / d)
    ang = pos[:, None] * inv[None, :]
    cos = jnp.cos(ang)[:, None, :]
    sin = jnp.sin(ang)[:, None, :]
    xf = x.astype(jnp.float32)
    x1, x2 = xf[..., : d // 2], xf[..., d // 2:]
    return jnp.concatenate([x1 * cos - x2 * sin, x2 * cos + x1 * sin], axis=-1).astype(x.dtype)

def attn_inputs(q, k, v, qi, ki, wi, pos):
    b, t = q.shape[:2]
    q = rope(q.reshape(b, t, N_HEADS, HEAD_DIM), pos).reshape(b, t, N_KV_HEADS, GQA_GROUP, HEAD_DIM)
    k = rope(k.reshape(b, t, N_KV_HEADS, HEAD_DIM), pos)
    v = v.reshape(b, t, N_KV_HEADS, HEAD_DIM)
    qi = rope(qi.reshape(b, t, IDX_HEADS, IDX_DIM), pos)
    ki = rope(ki[:, :, None, :], pos)[:, :, 0, :]
    wi = wi * (IDX_HEADS ** -0.5)
    return q, k, v, qi, ki, wi

def dsa_attend(q, qi, wi, limit, keys, vals, kidx, topk):
    b, tq = q.shape[:2]
    n_keys = keys.shape[1]
    rel = jax.nn.relu(jnp.einsum('bqhd,bsd->bqhs', qi, kidx).astype(jnp.float32))
    score = jnp.einsum('bqh,bqhs->bqs', wi.astype(jnp.float32), rel)
    admissible = jnp.arange(n_keys, dtype=jnp.int32)[None, :] < limit[:, None]
    score = jnp.where(admissible[None], score, -jnp.inf)
    _, sel = lax.top_k(score, topk)
    valid = sel < limit[None, :, None]
    gather = jax.vmap(lambda a, i: a[i])
    k_sel = gather(keys, sel)
    v_sel = gather(vals, sel)
    logits = jnp.einsum('bqhgd,bqkhd->bqhgk', q, k_sel).astype(jnp.float32) * (HEAD_DIM ** -0.5)
    logits = jnp.where(valid[:, :, None, None, :], logits, -jnp.inf)
    p = jax.nn.softmax(logits, axis=-1).astype(v_sel.dtype)
    o = jnp.einsum('bqhgk,bqkhd->bqhgd', p, v_sel)
    return o.reshape(b, tq, ATT_WIDTH)

def dsa_prompt(q, k, v, qi, ki, wi):
    b, t = q.shape[:2]
    n_blk = t // Q_BLOCK
    topk = min(TOPK_MAX, t // 4)
    limit = (jnp.arange(t, dtype=jnp.int32) // CHUNK + 1) * CHUNK

    def to_blocks(a):
        return jnp.moveaxis(a.reshape((b, n_blk, Q_BLOCK) + a.shape[2:]), 1, 0)

    xs = (to_blocks(q), to_blocks(qi), to_blocks(wi), limit.reshape(n_blk, Q_BLOCK))
    out = lax.map(lambda blk: dsa_attend(blk[0], blk[1], blk[2], blk[3], k, v, ki, topk), xs)
    return jnp.moveaxis(out, 0, 1).reshape(b, t, ATT_WIDTH)

def dsa_sample(q, k, v, qi, ki, wi, k_past, v_past, ki_past):
    t = q.shape[1]
    keys = jnp.concatenate([k_past, k], axis=1)
    vals = jnp.concatenate([v_past, v], axis=1)
    kidx = jnp.concatenate([ki_past, ki], axis=1)
    n_keys = keys.shape[1]
    limit = jnp.full((t,), n_keys, dtype=jnp.int32)
    return dsa_attend(q, qi, wi, limit, keys, vals, kidx, min(TOPK_MAX, n_keys // 4))

def sgu(u, v, ln_g, ln_b, w_s, b_s):
    b, t, _ = u.shape
    u = jax.nn.gelu(u)
    v = layer_norm(jax.nn.gelu(v), ln_g, ln_b)
    pad = (-t) % SGU_CHUNK
    n_chunk = (t + pad) // SGU_CHUNK
    vc = jnp.pad(v, ((0, 0), (0, pad), (0, 0))).reshape(b, n_chunk, SGU_CHUNK, SGU_GROUPS, SGU_GDIM)
    w = w_s * jnp.tril(jnp.ones((SGU_CHUNK, SGU_CHUNK), w_s.dtype))[None]
    s = jnp.einsum('gij,bnjgc->bnigc', w, vc) + b_s.T[None, None, :, :, None]
    s = s.reshape(b, t + pad, SGU_WIDTH)[:, :t]
    return u * s, v

def hier_moe(x, w_rg, b_rg, w_re, b_re, w_eg, w_eu, w_ed):
    b, t, d = x.shape
    xf = x.reshape(b * t, d)
    pg = jax.nn.softmax((xf @ w_rg + b_rg).astype(jnp.float32), axis=-1)
    g_w, g_idx = lax.top_k(pg, 1)
    g_hot = jax.nn.one_hot(g_idx[:, 0], N_GROUPS, dtype=jnp.float32)
    le = (xf @ w_re + b_re).astype(jnp.float32).reshape(-1, N_GROUPS, EXP_PER_GROUP)
    pe = jax.nn.softmax(jnp.einsum('ng,nge->ne', g_hot, le), axis=-1)
    e_w, e_idx = lax.top_k(pe, EXP_TOPK)
    e_w = e_w / jnp.sum(e_w, axis=-1, keepdims=True)
    in_group = jnp.einsum('nk,nke->ne', e_w, jax.nn.one_hot(e_idx, EXP_PER_GROUP, dtype=jnp.float32))
    gate = ((g_hot * g_w)[:, :, None] * in_group[:, None, :]).astype(x.dtype)
    out = jnp.zeros_like(xf)
    for g in range(N_GROUPS):
        h = jax.nn.silu(jnp.einsum('nd,edf->nef', xf, w_eg[g])) * jnp.einsum('nd,edf->nef', xf, w_eu[g])
        out = out + jnp.einsum('nef,efd->nd', h * gate[:, g, :, None], w_ed[g])
    return out.reshape(b, t, d)

def trunk_layer(x, pos, past, norm1, w_in, sgu_ln_g, sgu_ln_b, sgu_w, sgu_b, w_pa, w_pb, w_out,
                norm2, w_rg, b_rg, w_re, b_re, w_eg, w_eu, w_ed):
    xn = rms_norm(x, norm1)
    q, k, v, qi, ki, wi, u_b, v_b, g_a, g_b = jnp.split(jnp.einsum('btd,dc->btc', xn, w_in), IN_OFFSETS, axis=-1)
    q, k, v, qi, ki, wi = attn_inputs(q, k, v, qi, ki, wi, pos)
    if past is None:
        att = dsa_prompt(q, k, v, qi, ki, wi)
    else:
        att = dsa_sample(q, k, v, qi, ki, wi, past[0], past[1], past[2])
    sg, v_rows = sgu(u_b, v_b, sgu_ln_g, sgu_ln_b, sgu_w, sgu_b)
    merged = jax.nn.sigmoid(g_a) * (att @ w_pa) + jax.nn.sigmoid(g_b) * (sg @ w_pb)
    h = x + merged @ w_out
    h = h + hier_moe(rms_norm(h, norm2), w_rg, b_rg, w_re, b_re, w_eg, w_eu, w_ed)
    return h, k, v, ki, v_rows

def setup_inputs(seed: int = 0) -> dict:
    key = jax.random.key(seed)
    ks = jax.random.split(key, 23)

    def nrm(k, shape, scale):
        return scale * jax.random.normal(k, shape, jnp.float32)

    L, D = DEPTH, D_MODEL
    return {
        'x_prompt': nrm(ks[0], (BATCH, SEQ, D), 1.0),
        'x_sample': nrm(ks[1], (DEC_BATCH, DEC_SEQ, D), 1.0),
        'cache_k': nrm(ks[2], (L, DEC_BATCH, PAST_LEN, N_KV_HEADS, HEAD_DIM), 1.0),
        'cache_v': nrm(ks[3], (L, DEC_BATCH, PAST_LEN, N_KV_HEADS, HEAD_DIM), 1.0),
        'cache_kidx': nrm(ks[4], (L, DEC_BATCH, PAST_LEN, IDX_DIM), 1.0),
        'norm1': 1.0 + nrm(ks[5], (L, D), 0.02),
        'w_in': nrm(ks[6], (L, D, IN_COLS), D ** -0.5),
        'sgu_ln_g': 1.0 + nrm(ks[7], (L, SGU_WIDTH), 0.02),
        'sgu_ln_b': nrm(ks[8], (L, SGU_WIDTH), 0.02),
        'sgu_w': nrm(ks[9], (L, SGU_GROUPS, SGU_CHUNK, SGU_CHUNK), SGU_CHUNK ** -0.5),
        'sgu_b': 1.0 + nrm(ks[10], (L, SGU_GROUPS, SGU_CHUNK), 0.1),
        'w_pa': nrm(ks[11], (L, ATT_WIDTH, D), ATT_WIDTH ** -0.5),
        'w_pb': nrm(ks[12], (L, SGU_WIDTH, D), SGU_WIDTH ** -0.5),
        'w_out': nrm(ks[13], (L, D, D), D ** -0.5),
        'norm2': 1.0 + nrm(ks[14], (L, D), 0.02),
        'w_rg': nrm(ks[15], (L, D, N_GROUPS), D ** -0.5),
        'b_rg': nrm(ks[16], (L, N_GROUPS), 0.01),
        'w_re': nrm(ks[17], (L, D, N_GROUPS * EXP_PER_GROUP), D ** -0.5),
        'b_re': nrm(ks[18], (L, N_GROUPS * EXP_PER_GROUP), 0.01),
        'w_eg': nrm(ks[19], (L, N_GROUPS, EXP_PER_GROUP, D, EXP_HIDDEN), D ** -0.5),
        'w_eu': nrm(ks[20], (L, N_GROUPS, EXP_PER_GROUP, D, EXP_HIDDEN), D ** -0.5),
        'w_ed': nrm(ks[21], (L, N_GROUPS, EXP_PER_GROUP, EXP_HIDDEN, D), EXP_HIDDEN ** -0.5),
        'final_norm': 1.0 + nrm(ks[22], (D,), 0.02),
    }

def reference(x_prompt, x_sample, cache_k, cache_v, cache_kidx, norm1, w_in, sgu_ln_g, sgu_ln_b, sgu_w, sgu_b,
              w_pa, w_pb, w_out, norm2, w_rg, b_rg, w_re, b_re, w_eg, w_eu, w_ed, final_norm):
    pos_p = jnp.arange(x_prompt.shape[1], dtype=jnp.float32)
    pos_s = PAST_LEN + jnp.arange(x_sample.shape[1], dtype=jnp.float32)
    hp, hs = x_prompt, x_sample
    kp, vp, kip, ksm, vsm, kism, svsm = [], [], [], [], [], [], []
    for l in range(DEPTH):
        w = (norm1[l], w_in[l], sgu_ln_g[l], sgu_ln_b[l], sgu_w[l], sgu_b[l], w_pa[l], w_pb[l], w_out[l],
             norm2[l], w_rg[l], b_rg[l], w_re[l], b_re[l], w_eg[l], w_eu[l], w_ed[l])
        hp, k1, v1, ki1, _ = trunk_layer(hp, pos_p, None, *w)
        hs, k2, v2, ki2, sv2 = trunk_layer(hs, pos_s, (cache_k[l], cache_v[l], cache_kidx[l]), *w)
        kp.append(k1)
        vp.append(v1)
        kip.append(ki1)
        ksm.append(k2)
        vsm.append(v2)
        kism.append(ki2)
        svsm.append(sv2)
    y_prompt = rms_norm(hp, final_norm)
    y_sample = rms_norm(hs, final_norm)
    return (y_prompt, y_sample, jnp.stack(kp), jnp.stack(vp), jnp.stack(kip),
            jnp.stack(ksm), jnp.stack(vsm), jnp.stack(kism), jnp.stack(svsm))


_drawn_inputs = setup_inputs


def setup_inputs(seed=0):
    import zlib

    import numpy as np

    out = dict(_drawn_inputs(seed))
    spreads = {}
    factors = {'sgu_ln_b': 2.982, 'b_rg': 2.946, 'final_norm': 2.816}
    for name, (base, spread) in spreads.items():
        noise = np.random.default_rng([zlib.crc32(name.encode()), seed]).standard_normal(out[name].shape)
        drawn = base * np.exp(spread * noise) if base else spread * noise
        out[name] = jnp.asarray(drawn.astype(out[name].dtype))
    for name, factor in factors.items():
        out[name] = (out[name] * factor).astype(out[name].dtype)
    return out
```

```python
from contextlib import ExitStack

import numpy as np

import concourse.bass as bass
from concourse import mybir

F32 = mybir.dt.float32
ALU = mybir.AluOpType
ACT = mybir.ActivationFunctionType
AX = mybir.AxisListType

P = 128
DEPTH, D = 2, 1024
SEQ, STREAMS, FRAMES, PAST = 512, 8, 16, 256
PT = SEQ // P
NT = PT + 1
ROWS = NT * P
KD = D // P
HEADS, KV, HD = 8, 2, 64
GQ = HEADS // KV
IH, ID = 8, 32
SG, SW = 4, 512
NG, NE = 4, 8
EXPERTS, HID = NG * NE, 128
EPS = 1e-6
ATT_SCALE = HD ** -0.5
COLS = 4136
K0, V0, QI0, KI0, WI0 = 512, 640, 768, 1024, 1056
QKV_W = 1064
Q_REP = 272
U0, VS0, GA0, GB0 = 1064, 1576, 2088, 3112
BLK = 512
TOPK_P, TOPK_S = 128, 68
KEYS = [P * (t + 1) for t in range(PT)] + [PAST + FRAMES]
MB_AT = [sum(KEYS[:t]) for t in range(NT)]
MB_W = sum(KEYS)
NEG = -3.3e38
SEL = -3.4e38
OFF = -1e30
SLOTS = 4
SLOT_W = KD * BLK
UNITS = 16 + EXPERTS
(QU, KU, IU, UU, VU, KCU, VCU, SU) = range(8)
GAU, GBU, PABU = (8, 11), (9, 12), (10, 13)
OUTU = (14, 15)
IDX_TILES = (3, 2, 1, 4)
UNIT_DMAS = {u: 1 for u in range(16)} | {IU: 3, KCU: 4, VCU: 2, PABU[0]: 4, PABU[1]: 4}


def landed(u):
    return 16 * sum(UNIT_DMAS[v] for v in range(u + 1) if v % SLOTS == u % SLOTS)


PROMPT_UNITS = [(t, j, g) for t in range(PT) for j in range(GQ) for g in range(KV)]
STREAM_UNITS = [(PT, j, g) for g in range(KV) for j in range(GQ)]
ATT_UNITS = PROMPT_UNITS + STREAM_UNITS
NPU, NAU = len(PROMPT_UNITS), len(ATT_UNITS)
PREP_AT = {NPU: 0, NPU + GQ: 1}


def over(ap, n, axis, shape):
    return ap.unsqueeze(axis).broadcast_to(shape)


def build(nc, a, o):
    ctx = ExitStack()
    with ctx:
        def sb(name, shape):
            return ctx.enter_context(nc.sbuf_tensor(name, shape, F32))

        def sem(name):
            return ctx.enter_context(nc.semaphore(name))

        ctx.enter_context(nc.allow_non_contiguous_dma("small parameters"))
        x = sb("x", [P, NT, D])
        xt = sb("xt", [P, KD, ROWS])
        qkv = sb("qkv", [P, NT, QKV_W])
        uv = sb("uv", [P, 2, NT, BLK])
        ring = sb("ring", [P, SLOTS, SLOT_W])
        att = sb("att", [P, GQ, ROWS])
        sgt = sb("sgt", [P, SG, ROWS])
        mb = sb("mb", [P, MB_W])
        kt = sb("kt", [P, SEQ])
        scr = sb("scr", [P, 2048])
        ident = sb("ident", [P, P])
        tril = sb("tril", [P, P])
        rope_t = sb("rope_t", [P, NT, HD + ID])
        quad = sb("quad", [P, 2, P])
        pair = sb("pair", [P, 4, P])
        own = sb("own", [P, STREAMS])
        gain = sb("gain", [P, 2, KD])
        rbias = sb("rbias", [P, NG + EXPERTS])
        sbias = sb("sbias", [P, 2, SG])
        corner = sb("corner", [P, SG, FRAMES])
        stat = sb("stat", [P, 64])
        ss, rs = stat[:, 0:5], stat[:, 5:10]
        mx, nmx, den, rden = (stat[:, 10 + 2 * i:12 + 2 * i] for i in range(4))
        moments = stat[:, 18:28].rearrange("p (t c) -> p t c", c=2)
        lrs = stat[:, 28:33]
        half = stat[:, 33:38]
        bns = stat[:, 38:44]
        best = stat[:, 44:52]
        var_e = stat[:, 52:57]

        qit = att[:, :, :].rearrange("p a b -> p (a b)")[:, 0:1024].rearrange("p (j r) -> p j r", j=2)
        kit = att[:, :, :].rearrange("p a b -> p (a b)")[:, 1024:1536]
        kis = att[:, :, :].rearrange("p a b -> p (a b)")[:, 1536:1536 + 2 * KEYS[PT]].rearrange(
            "p (s k) -> p s k", s=2)
        sgt_flat = sgt[:, :, :].rearrange("p a b -> p (a b)")
        qis = sgt_flat[:, 0:2048].rearrange("p (s h q) -> p s h q", s=2, h=IH)
        qt = sgt_flat[:, 0:2048].rearrange("p (j r) -> p j r", j=GQ)
        qts = sgt_flat[:, 0:2048].rearrange("p (s j q) -> p s j q", s=4, j=GQ)

        ki_rep = kt[:, :]
        qis_rep = mb[:, 0:1024].rearrange("p (h c d) -> p h c d", h=IH, c=4)
        kis_rep = mb[:, 1024:1152]
        ks_rep = [sgt_flat[:, 2048:2176], sgt_flat[:, 2176:2304]]

        def score(t):
            return mb[:, MB_AT[t]:MB_AT[t] + KEYS[t]]

        probs = [scr[:, 0:512], scr[:, 512:1024]]
        probs_t = [scr[:, 1024:1536], scr[:, 1536:2048]]
        relu_b = [scr[:, 0:512], scr[:, 512:1024]]
        ln_g, ln_b = scr[:, 1024:1536], scr[:, 1536:2048]
        xn = [scr[:, 0:1024], scr[:, 1024:2048]]
        sgw_t = [scr[:, 0:512].rearrange("p (g i) -> p g i", g=SG),
                 scr[:, 512:1024].rearrange("p (g i) -> p g i", g=SG)]
        hid = scr[:, 0:ROWS]
        fin_gain = uv[:, 0, 0:2, :].rearrange("p t c -> p (t c)")

        def mbv(at, w):
            return mb[:, at:at + w]
        logit = mbv(0, 180).rearrange("p (t c) -> p t c", t=NT)
        w16 = mbv(180, 80).rearrange("p (t c) -> p t c", t=NT)
        m8 = mbv(260, 40).rearrange("p (t c) -> p t c", t=NT)
        r8 = mbv(300, 40).rearrange("p (t c) -> p t c", t=NT)
        hot = mbv(340, 20).rearrange("p (t c) -> p t c", t=NT)
        eg = mbv(360, 20).rearrange("p (t c) -> p t c", t=NT)
        gsum, gw, esum, escale = (mbv(380 + 5 * i, 5) for i in range(4))
        picked = mbv(400, 160).rearrange("p (t g e) -> p t g e", t=NT, g=NG)
        l8 = mbv(560, 40).rearrange("p (t c) -> p t c", t=NT)
        e8 = mbv(600, 40).rearrange("p (t c) -> p t c", t=NT)
        gate = mbv(640, 160).rearrange("p (t e) -> p t e", t=NT)
        w16e = mbv(800, 80).rearrange("p (t c) -> p t c", t=NT)
        m8e = mbv(880, 40).rearrange("p (t c) -> p t c", t=NT)
        r8e = mbv(920, 40).rearrange("p (t c) -> p t c", t=NT)
        wr = kt[:, 0:KD * 36].rearrange("p (k c) -> p k c", k=KD)

        banks = [ctx.enter_context(nc.psum_tensor(f"bank{i}", [P, BLK], F32)) for i in range(8)]

        s_const = sem("s_const")
        s_pool = sem("s_pool")
        s_rope = sem("s_rope")
        s_x = sem("s_x")
        s_out = sem("s_out")
        s_fin = sem("s_fin")
        s_fin_ss = sem("s_fin_ss")
        s_fin_rs = sem("s_fin_rs")
        s_fin_x = sem("s_fin_x")
        s_go = {e: sem(f"s_go_{e}") for e in ("pe", "act", "dve", "pool")}
        params, ln_loaded, wr_loaded = sem("params"), sem("ln_loaded"), sem("wr_loaded")
        kv_out, sguv_out = sem("kv_out"), sem("sguv_out")
        first = sem("arrived")
        arrived = first
        slot = [sem(f"slot{i}") for i in range(SLOTS)]
        names = ("unit_done rows_sent ss_ready rs_ready xn_ready "
                 "xt_psum xt_done proj_psum proj_free rope_done rep_done kx_psum kx_done qis_done idx_psum "
                 "idx_relu idx_used qk_psum qk_done s_psum p_raw p_exp p_ready pt_psum pt_done "
                 "pv_done o_psum o_done ks_psum ks_done qts_done ln_stat ln_rs ln_done swm_ready "
                 "sw_psum sw_done sg_psum sg_used sgt_psum sgt_done mg_gate mg_proj mg_sig mg_done "
                 "mt_psum mt_done xo_psum xo_done r_psum r_exp r_sub gu_psum silu_done h_done "
                 "y_psum y_free dve_chain act_chain").split()
        (unit_done, rows_sent, ss_ready, rs_ready, xn_ready,
         xt_psum, xt_done, proj_psum, proj_free, rope_done, rep_done, kx_psum, kx_done, qis_done, idx_psum,
         idx_relu, idx_used, qk_psum, qk_done, s_psum, p_raw, p_exp, p_ready, pt_psum, pt_done,
         pv_done, o_psum, o_done, ks_psum, ks_done, qts_done, ln_stat, ln_rs, ln_done, swm_ready,
         sw_psum, sw_done, sg_psum, sg_used, sgt_psum, sgt_done, mg_gate, mg_proj, mg_sig, mg_done,
         mt_psum, mt_done, xo_psum, xo_done, r_psum, r_exp, r_sub, gu_psum, silu_done, h_done,
         y_psum, y_free, dve_chain, act_chain) = made = [sem(n) for n in names]
        layer_sems = [first, *slot, *made]

        block = ctx.enter_context(nc.Block())

        def next_layer(eng, key):
            eng.drain().then_inc(arrived, 1)
            eng.wait_ge(s_go[key], 1)
            eng.sem_clear(s_go[key])

        @block.sync
        def _(sp):
            for t in range(PT):
                sp.dma_start(x[:, t, :], a["x_prompt"][0, t * P:(t + 1) * P, :]).then_inc(s_x, 16)
            sp.dma_start(x[:, PT, :], a["x_sample"].rearrange("b t d -> (b t) d")).then_inc(s_x, 16)
            with sp.Fori(0, DEPTH) as L:
                w_in = a["w_in"][L].rearrange("(p k) c -> p k c", k=KD)

                def load(u, dst, src):
                    sp.dma_start(dst, src).then_inc(slot[u % SLOTS], 16)

                def at(u):
                    return ring[:, u % SLOTS, :]

                def cols(u, c0, w=BLK):
                    load(u, at(u)[:, 0:KD * w].rearrange("p (k c) -> p k c", k=KD), w_in[:, :, c0:c0 + w])

                for u in range(16):
                    if u >= SLOTS:
                        sp.wait_ge(unit_done, u - SLOTS + 1)
                    if u in (QU, KU):
                        cols(u, u * BLK)
                    elif u == IU:
                        cols(u, KI0, QKV_W - KI0)
                        for h in range(2):
                            load(u, at(u)[:, 512 + 256 * h:768 + 256 * h].rearrange("p (b d) -> p b d", b=STREAMS),
                                 a["cache_kidx"][L].rearrange("b (t p) d -> t p b d", p=P)[h])
                    elif u == UU:
                        cols(u, U0)
                    elif u == VU:
                        cols(u, VS0)
                    elif u == KCU:
                        for h in range(2):
                            for g in range(KV):
                                c0 = 512 * (2 * h + g)
                                load(u, at(u)[:, c0:c0 + 512].rearrange("p (b d) -> p b d", b=STREAMS),
                                     a["cache_k"][L].rearrange("b (t p) g d -> t g p b d", p=P)[h, g])
                    elif u == VCU:
                        for hf in range(2):
                            load(u, at(u)[:, 1024 * hf:1024 * hf + 1024].rearrange("p (n c) -> p n c", n=8),
                                 a["cache_v"][L].rearrange("b (t p) g d -> p (b t) (g d)", p=P)[:, 8 * hf:8 * hf + 8, :])
                    elif u == SU:
                        load(u, at(u)[:, 0:512].rearrange("p (g j) -> p g j", g=SG),
                             a["sgu_w"][L].rearrange("g i j -> i g j"))
                    elif u in GAU:
                        cols(u, GA0 + BLK * GAU.index(u))
                    elif u in GBU:
                        cols(u, GB0 + BLK * GBU.index(u))
                    elif u in PABU:
                        c0 = BLK * PABU.index(u)
                        for g in range(KV):
                            load(u, at(u)[64 * g:64 * g + 64, 0:2048].rearrange("p (j c) -> p j c", j=GQ),
                                 a["w_pa"][L].rearrange("(g j p) c -> g p j c", g=KV, p=HD)[g, :, :, c0:c0 + BLK])
                        for hf in range(2):
                            load(u, at(u)[:, 2048 + 1024 * hf:3072 + 1024 * hf].rearrange("p (j c) -> p j c", j=2),
                                 a["w_pb"][L].rearrange("(j p) c -> p j c", p=P)[:, 2 * hf:2 * hf + 2, c0:c0 + BLK])
                    else:
                        c0 = BLK * OUTU.index(u)
                        load(u, at(u).rearrange("p (k c) -> p k c", k=KD),
                             a["w_out"][L].rearrange("(k p) c -> p k c", p=P)[:, :, c0:c0 + BLK])
                with sp.Fori(0, EXPERTS // SLOTS) as i:
                    for q in range(SLOTS):
                        e = SLOTS * i + q
                        row = EXPERTS * L + e
                        sp.wait_ge(unit_done, e + 16 - SLOTS + 1)
                        for n, w in enumerate(("w_eg", "w_eu")):
                            sp.dma_start(ring[:, q, 1024 * n:1024 * n + 1024],
                                         a[w].rearrange("l g e (p k) f -> (l g e) p (k f)", k=KD)[row]
                                         ).then_inc(slot[q], 16)
                        sp.dma_start(ring[:, q, 2048:3072],
                                     a["w_ed"].rearrange("l g e f d -> (l g e) f d")[row]
                                     ).then_inc(slot[q], 16)
                sp.wait_ge(arrived, 4)
                for s in layer_sems:
                    sp.sem_clear(s)
                for key in s_go:
                    sp.sem_inc(s_go[key], 1)
            for t in range(PT):
                sp.wait_ge(s_fin, t + 1)
                sp.dma_start(o[0][0, t * P:(t + 1) * P, :], x[:, t, :]).then_inc(s_out, 16)
            sp.wait_ge(s_fin, NT)
            sp.dma_start(o[1].rearrange("b t d -> (b t) d"), x[:, PT, :]).then_inc(s_out, 16)
            sp.wait_ge(s_out, 16 * NT)

        @block.gpsimd
        def _(pool):
            pool.dma_start(rope_t[:, :, :], a["rope"].rearrange("t p c -> p t c")).then_inc(s_rope, 16)
            pool.memset(ident[:, :], 0.0)
            pool.memset(tril[:, :], 1.0)
            pool.memset(quad[:, :, :], 0.0)
            pool.memset(pair[:, :, :], 0.0)
            pool.memset(own[:, :], 1.0)
            pool.memset(half, -0.5)
            pool.memset(mb[:, 0:P], 0.0).then_inc(s_pool, 1)
            pool.wait_ge(s_pool, 1)
            pool.affine_select(out=ident[:, :], in_=ident[:, :], compare_op=ALU.not_equal, fill=1.0,
                               base=0, pattern=[[-1, P]], channel_multiplier=1)
            pool.affine_select(out=tril[:, :], in_=tril[:, :], compare_op=ALU.is_ge, fill=0.0,
                               base=0, pattern=[[-1, P]], channel_multiplier=1)
            pool.affine_select(out=own[:, :], in_=own[:, :], compare_op=ALU.is_ge, fill=0.0,
                               base=0, pattern=[[-FRAMES, STREAMS]], channel_multiplier=1).then_inc(s_pool, 1)
            pool.wait_ge(s_pool, 2)
            pool.affine_select(out=own[:, :], in_=own[:, :], compare_op=ALU.is_ge, fill=0.0,
                               base=FRAMES - 1, pattern=[[FRAMES, STREAMS]], channel_multiplier=-1)
            for b in range(STREAMS):
                q = slice(FRAMES * b, FRAMES * (b + 1))
                pool.memset(quad[32 * (b % 4):32 * (b % 4) + 32, b // 4, q], 1.0).then_inc(s_pool, 1)
                pool.wait_ge(s_pool, 3 + 2 * b)
                pool.memset(pair[64 * (b % 2):64 * (b % 2) + 64, b // 2, q], 1.0).then_inc(s_pool, 1)
                pool.wait_ge(s_pool, 4 + 2 * b)
            pool.drain().then_inc(s_const, 1)

            def power(dst, src, scale, ready, n, out_sem):
                pool.wait_ge(ready, n)
                pool.tensor_scalar(dst, src, scale, EPS, ALU.mult, ALU.add).then_inc(s_pool, 1)
                pool.wait_ge(s_pool, 1)
                pool.sem_clear(s_pool)
                pool.tensor_tensor(dst, dst, half, ALU.pow).then_inc(out_sem, 1)

            pool.sem_clear(s_pool)
            with pool.Fori(0, DEPTH) as L:
                pool.dma_start(gain[:, 0, :], a["norm1"][L].rearrange("(p k) -> p k", k=KD)).then_inc(params, 16)
                pool.dma_start(gain[:, 1, :], a["norm2"][L].rearrange("(p k) -> p k", k=KD)).then_inc(params, 16)
                power(rs, ss, 1.0 / D, ss_ready, 1, rs_ready)
                pool.dma_start(rbias[:, 0:NG], a["b_rg"][L].partition_broadcast(P)).then_inc(params, 16)
                pool.dma_start(rbias[:, NG:], a["b_re"][L].partition_broadcast(P)).then_inc(params, 16)
                pool.dma_start(sbias[:, 0, :], a["sgu_b"][L].rearrange("g i -> i g")).then_inc(params, 16)
                for b in range(STREAMS):
                    q = slice(FRAMES * b, FRAMES * (b + 1))
                    pool.dma_start(sbias[q, 1, :], a["sgu_b"][L][:, 0:FRAMES].rearrange("g i -> i g")).then_inc(params, 16)
                    pool.dma_start(corner[q, :, :], a["sgu_w"][L][:, 0:FRAMES, 0:FRAMES].rearrange("g i j -> i g j")).then_inc(params, 16)
                for t in range(NT):
                    pool.wait_ge(rope_done, t + 1)
                    for c0, w, n in ((K0, P, 0), (V0, P, 1), (KI0, ID, 2)):
                        if t < PT:
                            dst = o[2 + n][L][0, t * P:(t + 1) * P]
                            dst = dst if n == 2 else dst.rearrange("t g d -> t (g d)")
                        else:
                            dst = o[5 + n][L]
                            dst = dst.rearrange("b t d -> (b t) d") if n == 2 else dst.rearrange("b t g d -> (b t) (g d)")
                        pool.dma_start(dst, qkv[:, t, c0:c0 + w]).then_inc(kv_out, 16)
                    dst = ki_rep[:, t * P:(t + 1) * P] if t < PT else kis_rep
                    if t == PT:
                        pool.tensor_copy(qis_rep[:, :, :, :],
                                         qkv[:, t, QI0:KI0].rearrange("p (h d) -> p h d", h=IH).unsqueeze(2).broadcast_to([P, IH, 4, ID]))
                    pool.tensor_copy(dst.rearrange("p (c d) -> p c d", c=4),
                                     over(qkv[:, t, KI0:KI0 + ID], 4, 1, [P, 4, ID])).then_inc(rep_done, 1)
                pool.dma_start(ln_g, a["sgu_ln_g"][L].partition_broadcast(P)).then_inc(ln_loaded, 16)
                pool.dma_start(ln_b, a["sgu_ln_b"][L].partition_broadcast(P)).then_inc(ln_loaded, 16)
                pool.wait_ge(qk_psum, 1 + GQ)
                for g in range(KV):
                    if g:
                        power(lrs, moments[:, :, 1], 1.0, ln_stat, 1, ln_rs)
                        pool.wait_ge(ln_done, NT)
                        pool.dma_start(o[8][L].rearrange("b t c -> (b t) c"), uv[:, 1, PT, :]).then_inc(sguv_out, 16)
                        pool.wait_ge(ks_psum, 4)
                    q = qkv[:, PT, 0:512].rearrange("p (j g d) -> p j g d", g=KV, j=GQ)[:, :, g, :]
                    c0 = K0 + HD * g
                    pool.tensor_copy(qkv[:, 0:GQ, Q_REP:Q_REP + P].rearrange("p j (c d) -> p j c d", c=2),
                                     q.unsqueeze(2).broadcast_to([P, GQ, 2, HD]))
                    pool.tensor_copy(ks_rep[g].rearrange("p (c d) -> p c d", c=2),
                                     over(qkv[:, PT, c0:c0 + HD], 2, 1, [P, 2, HD])).then_inc(rep_done, 1)
                pool.wait_ge(kv_out, 48 * NT * L + 48 * NT)
                pool.wait_ge(sguv_out, 16 * L + 16)
                pool.sem_inc(rows_sent, 1)
                pool.wait_ge(s_psum, NAU)
                pool.dma_start(wr[:, :, 0:NG], a["w_rg"][L].rearrange("(p k) c -> p k c", k=KD)).then_inc(wr_loaded, 16)
                pool.dma_start(wr[:, :, NG:], a["w_re"][L].rearrange("(p k) c -> p k c", k=KD)).then_inc(wr_loaded, 16)
                power(rs, ss, 1.0 / D, ss_ready, 2, rs_ready)
                next_layer(pool, "pool")
            pool.dma_start(fin_gain, a["final_norm"].partition_broadcast(P)).then_inc(s_rope, 16)
            power(rs, ss, 1.0 / D, s_fin_ss, 1, s_fin_rs)

        @block.tensor
        def _(pe):
            pe.wait_ge(s_const, 1)
            idm = ident[:, :]

            def norm_transposes(phase):
                for t in range(NT):
                    pe.wait_ge(xn_ready, NT * phase + t + 1)
                    for hf in range(2):
                        n = 2 * t + hf
                        if n >= 4:
                            pe.wait_ge(xt_done, 2 * NT * phase + n - 3)
                        for k in range(4):
                            mm = pe.transpose(banks[n % 4][:, k * P:(k + 1) * P],
                                              xn[t % 2][:, 4 * hf + k:D:KD], idm)
                        mm.then_inc(xt_psum, 1)

            with pe.Fori(0, DEPTH) as L:
                def unit(u):
                    return ring[:, u % SLOTS, :]

                def wait_unit(u):
                    pe.wait_ge(slot[u % SLOTS], landed(u))

                def project(u, t, out, w=BLK):
                    rhs = unit(u)[:, 0:KD * w].rearrange("p (k c) -> p k c", k=KD)
                    for k in range(KD):
                        mm = pe.matmul(out, xt[:, k, t * P:(t + 1) * P], rhs[:, k, :],
                                       start=(k == 0), stop=(k == KD - 1))
                    return mm

                jobs = [(u, t) for u in (QU, KU, IU, UU, VU) for t in range(NT)]

                def proj_job(n):
                    u, t = jobs[n]
                    if t == 0:
                        wait_unit(u)
                    if u == QU:
                        pe.wait_ge(xt_done, 2 * t + 2)
                    if n >= 4:
                        pe.wait_ge(proj_free, n - 3)
                    w = QKV_W - KI0 if u == IU else BLK
                    mm = project(u, t, banks[4 + n % 4][:, 0:w], w)
                    mm.then_inc(proj_psum, 1)
                    if t == NT - 1 and u != IU:
                        pe.drain().then_inc(unit_done, 1)

                norm_transposes(0)
                for n in range(3 * NT):
                    proj_job(n)
                pe.wait_ge(xt_done, 2 * NT)
                kidx = unit(IU)[:, 512:1024].rearrange("p (h s c) -> p h s c", h=2, s=2)
                for s in range(2):
                    for h in range(2):
                        mm = pe.transpose(banks[0][:, 256 * s + 128 * h:256 * s + 128 * h + 128],
                                          kidx[:, h, s, :], idm)
                mm.then_inc(kx_psum, 1)
                pe.drain().then_inc(unit_done, 1)
                for n in range(3 * NT, 4 * NT):
                    proj_job(n)
                pe.wait_ge(rope_done, NT)
                pe.wait_ge(rep_done, NT)
                for t in range(PT):
                    mm = pe.transpose(banks[1][:, t * P:(t + 1) * P],
                                      ki_rep[:, t * P:(t + 1) * P], idm)
                mm.then_inc(kx_psum, 1)
                for j in range(2):
                    for t in range(PT):
                        mm = pe.transpose(banks[2 + j][:, t * P:(t + 1) * P],
                                          qkv[:, t, QI0 + P * j:QI0 + P * (j + 1)], idm)
                    mm.then_inc(kx_psum, 1)
                pe.wait_ge(kx_done, 1)
                pe.transpose(banks[0][:, 0:P], kis_rep, idm).then_inc(kx_psum, 1)
                for j in range(2):
                    pe.wait_ge(kx_done, 2 + j)
                    for h in range(4):
                        mm = pe.transpose(banks[1 + j][:, h * P:(h + 1) * P],
                                          qis_rep[:, 4 * j + h, :, :].rearrange("p c d -> p (c d)"), idm)
                    mm.then_inc(kx_psum, 1)
                pe.wait_ge(kx_done, 5)
                pe.wait_ge(qis_done, 2)
                for at, t in enumerate(IDX_TILES):
                    for h in range(IH):
                        m = IH * at + h
                        if m >= 4:
                            pe.wait_ge(idx_relu, m - 3)
                        out = banks[m % 4][:, 0:KEYS[t]]
                        if t < PT:
                            r = slice(ID * (h % 4), ID * (h % 4) + ID)
                            mm = pe.matmul(out, qit[r, h // 4, t * P:(t + 1) * P], kit[r, 0:KEYS[t]],
                                           start=True, stop=True)
                        else:
                            for s in range(2):
                                mm = pe.matmul(out, qis[:, s, h, :], kis[:, s, :], start=(s == 0), stop=(s == 1))
                        mm.then_inc(idx_psum, 1)
                    if at == 0:
                        for n in range(4 * NT, 5 * NT):
                            proj_job(n)
                pe.wait_ge(idx_relu, IH * len(IDX_TILES))
                for t in range(PT):
                    mm = pe.transpose(banks[0][:, t * P:(t + 1) * P], qkv[:, t, K0:K0 + P], idm)
                mm.then_inc(qk_psum, 1)
                pe.wait_ge(proj_free, 5 * NT)
                for j in range(GQ):
                    for t in range(PT):
                        mm = pe.transpose(banks[4 + j][:, t * P:(t + 1) * P], qkv[:, t, j * P:(j + 1) * P], idm)
                    mm.then_inc(qk_psum, 1)
                pe.wait_ge(qk_done, 1 + GQ)

                def stream_layout(g):
                    kc = unit(KCU)[:, 0:2048].rearrange("p (h g s c) -> p h g s c", h=2, g=KV, s=4)
                    for s2 in range(2):
                        if g:
                            pe.wait_ge(ks_done, 3)
                            pe.wait_ge(qts_done, 1)
                        for s in range(2):
                            for h in range(2):
                                mm = pe.transpose(banks[6 + s2][:, 256 * s + 128 * h:256 * s + 128 * h + 128],
                                                  kc[:, h, g, 2 * s2 + s, :], idm)
                        mm.then_inc(ks_psum, 1)
                    pe.wait_ge(ks_done, 3 * g + 1)
                    pe.wait_ge(rep_done, NT + 1 + g)
                    pe.transpose(banks[6][:, 0:P], ks_rep[g], idm).then_inc(ks_psum, 1)
                    pe.wait_ge(ks_done, 3 * g + 2)
                    for j in range(GQ):
                        mm = pe.transpose(banks[7][:, j * P:(j + 1) * P], qkv[:, j, Q_REP:Q_REP + P], idm)
                    mm.then_inc(ks_psum, 1)
                    if g:
                        pe.drain().then_inc(unit_done, 1)
                    pe.wait_ge(ks_done, 3 * g + 3)
                    pe.wait_ge(qts_done, g + 1)

                def logits(n):
                    t, j, g = ATT_UNITS[n]
                    if n in PREP_AT:
                        if g == 0:
                            wait_unit(KCU)
                        stream_layout(g)
                    out = banks[n % 2][:, 0:KEYS[t]]
                    if t < PT:
                        r = slice(HD * g, HD * g + HD)
                        mm = pe.matmul(out, qt[r, j, t * P:(t + 1) * P], kt[r, 0:KEYS[t]], start=True, stop=True)
                    else:
                        for s in range(4):
                            mm = pe.matmul(out, qts[:, s, j, :], qkv[:, s, 0:KEYS[t]], start=(s == 0), stop=(s == 3))
                    mm.then_inc(s_psum, 1)

                def probs_transposes(n):
                    t, j, g = ATT_UNITS[n]
                    pe.wait_ge(p_ready, n + 1)
                    if n >= 2:
                        pe.wait_ge(pt_done, n - 1)
                    blocks = range(t + 1) if t < PT else (0, 1, 3)
                    for i, c in enumerate(blocks):
                        mm = pe.transpose(banks[2 + n % 2][:, i * P:(i + 1) * P],
                                          probs[n % 2][:, c * P:(c + 1) * P], idm)
                    mm.then_inc(pt_psum, 1)

                def values(n):
                    t, j, g = ATT_UNITS[n]
                    pe.wait_ge(pt_done, n + 1)
                    if t >= 2 and (j, g) == (0, 0):
                        pe.wait_ge(o_done, t - 1)
                    o_b = banks[4 + t % 2]
                    v = slice(V0 + HD * g, V0 + HD * g + HD)
                    r = slice(HD * g, HD * g + HD)
                    pt = probs_t[n % 2]
                    if t < PT:
                        for c in range(t + 1):
                            mm = pe.matmul(o_b[r, j * P:(j + 1) * P], qkv[:, c, v], pt[:, c * P:(c + 1) * P],
                                           start=(c == 0), stop=(c == t))
                    else:
                        if n == NPU:
                            wait_unit(VCU)
                        vc = unit(VCU)[:, 0:2048].rearrange("p (b t c) -> p b t c", b=STREAMS, t=2)
                        pe.matmul(o_b[r, j * P:(j + 1) * P], qkv[:, PT, v], pt[:, 2 * P:3 * P], start=True, stop=False)
                        for b in range(STREAMS):
                            for h in range(2):
                                q0 = FRAMES * b
                                mm = pe.matmul(o_b[r, j * P + q0:j * P + q0 + FRAMES], vc[:, b, h, r],
                                               pt[:, h * P + q0:h * P + q0 + FRAMES], start=False,
                                               stop=(b == STREAMS - 1 and h == 1))
                    mm.then_inc(pv_done, 1)
                    if n == NAU - 1 or ATT_UNITS[n + 1][0] != t:
                        pe.drain().then_inc(o_psum, 1)

                logits(0)
                logits(1)
                for n in range(NAU):
                    probs_transposes(n)
                    if n + 2 < NAU:
                        logits(n + 2)
                    if n >= 1:
                        values(n - 1)
                values(NAU - 1)
                pe.drain().then_inc(unit_done, 1)

                for m in range(2):
                    pe.wait_ge(swm_ready, m + 1)
                    if m == 0:
                        src = unit(SU)[:, 0:512]
                    else:
                        src = unit(SU)[:, 1024:1536]
                    for g in range(SG):
                        mm = pe.transpose(banks[6 + m][:, g * P:(g + 1) * P], src[:, g * P:(g + 1) * P], idm)
                    mm.then_inc(sw_psum, 1)
                pe.drain().then_inc(unit_done, 1)
                pe.wait_ge(sw_done, 2)
                for t in range(NT):
                    pe.wait_ge(ln_done, t + 1)
                    if t == 4:
                        pe.wait_ge(sg_used, 1)
                    for g in range(SG):
                        mm = pe.matmul(banks[t % 4][:, g * P:(g + 1) * P], sgw_t[t // PT][:, g, :],
                                       uv[:, 1, t, g * P:(g + 1) * P], start=True, stop=True)
                    mm.then_inc(sg_psum, 1)
                pe.wait_ge(o_done, NT)
                for t in range(NT):
                    pe.wait_ge(sg_used, t + 1)
                    if t == 4:
                        pe.wait_ge(sgt_done, 1)
                    for g in range(SG):
                        mm = pe.transpose(banks[4 + t % 4][:, g * P:(g + 1) * P], uv[:, 0, t, g * P:(g + 1) * P], idm)
                    mm.then_inc(sgt_psum, 1)

                pe.wait_ge(sgt_done, NT)
                for n in range(2 * NT):
                    c, t = divmod(n, NT)
                    b = banks[4 * (n % 2):4 * (n % 2) + 4]
                    if n >= 2:
                        pe.wait_ge(mg_done, n - 1)
                    if t == 0:
                        wait_unit(GAU[c])
                        wait_unit(GBU[c])
                    project(GAU[c], t, b[0][:, :])
                    project(GBU[c], t, b[1][:, :]).then_inc(mg_gate, 1)
                    if t == 0:
                        wait_unit(PABU[c])
                    w = unit(PABU[c]).rearrange("p (n c) -> p n c", n=8)
                    for half_, src in ((0, att), (1, sgt)):
                        for j in range(4):
                            mm = pe.matmul(b[2 + half_][:, :], src[:, j, t * P:(t + 1) * P], w[:, 4 * half_ + j, :],
                                           start=(j == 0), stop=(j == 3))
                    mm.then_inc(mg_proj, 1)
                    if t == NT - 1:
                        pe.drain().then_inc(unit_done, 3)
                pe.wait_ge(mg_done, 2 * NT)
                for n in range(2 * NT):
                    t, hf = divmod(n, 2)
                    if n >= 4:
                        pe.wait_ge(mt_done, n - 3)
                    for k in range(4):
                        mm = pe.transpose(banks[n % 4][:, k * P:(k + 1) * P], uv[:, hf, t, k * P:(k + 1) * P], idm)
                    mm.then_inc(mt_psum, 1)
                for n in range(2 * NT):
                    c, t = divmod(n, NT)
                    if t == 0:
                        wait_unit(OUTU[c])
                    if c == 0:
                        pe.wait_ge(mt_done, 2 * t + 2)
                    if n >= 4:
                        pe.wait_ge(xo_done, n - 3)
                    project(OUTU[c], t, banks[4 + n % 4][:, :]).then_inc(xo_psum, 1)
                    if t == NT - 1:
                        pe.drain().then_inc(unit_done, 1)

                norm_transposes(1)
                pe.wait_ge(xt_done, 4 * NT)
                pe.wait_ge(xo_done, 2 * NT)
                pe.wait_ge(wr_loaded, 32 * L + 32)
                for t in range(NT):
                    for k in range(KD):
                        mm = pe.matmul(banks[4][:, 36 * t:36 * t + 36], xt[:, k, t * P:(t + 1) * P], wr[:, k, :],
                                       start=(k == 0), stop=(k == KD - 1))
                mm.then_inc(r_psum, 1)

                with pe.Fori(0, EXPERTS // SLOTS) as i:
                    for q in range(SLOTS):
                        e = SLOTS * i + q
                        pe.wait_ge(slot[q], 48 * i + (landed(12 + q) + 48))
                        pe.wait_ge(h_done, e + 1)
                        for m in range(2):
                            w = ring[:, q, 1024 * m:1024 * m + 1024].rearrange("p (k f) -> p k f", k=KD)
                            for c in range(2):
                                for k in range(KD):
                                    mm = pe.matmul(banks[2 * m + c][:, 0:320], w[:, k, :], xt[:, k, 320 * c:320 * c + 320],
                                                   start=(k == 0), stop=(k == KD - 1))
                            mm.then_inc(gu_psum, 1)
                        pe.wait_ge(h_done, e + 2)
                        for n in range(2 * NT):
                            t, c = divmod(n, 2)
                            pe.wait_ge(y_free, 2 * NT * e + n + 1)
                            mm = pe.matmul(banks[4 + n % 4][:, :], hid[:, t * P:(t + 1) * P],
                                           ring[:, q, 2048 + BLK * c:2048 + BLK * c + BLK], start=True, stop=True)
                            mm.then_inc(y_psum, 1)
                        pe.drain().then_inc(unit_done, 1)
                next_layer(pe, "pe")

        @block.scalar
        def _(act):
            with act.Fori(0, DEPTH) as L:
                def proj_out(n):
                    u, t = divmod(n, NT)
                    act.wait_ge(proj_psum, n + 1)
                    b = banks[4 + n % 4]
                    if u == 0:
                        ins = act.activation(qkv[:, t, 0:BLK].rearrange("p (j g d) -> p g j d", g=KV, j=GQ),
                                             b[:, :].rearrange("p (g j d) -> p g j d", g=KV, j=GQ), ACT.Copy)
                    elif u == 1:
                        ins = act.activation(qkv[:, t, BLK * u:BLK * u + BLK], b[:, :], ACT.Copy)
                    elif u == 2:
                        ins = act.activation(qkv[:, t, KI0:QKV_W], b[:, 0:QKV_W - KI0], ACT.Copy)
                    else:
                        ins = act.activation(uv[:, u - 3, t, :], b[:, :], ACT.Gelu_apprx_tanh)
                    ins.then_inc(proj_free, 1)

                for n in range(3 * NT):
                    proj_out(n)
                act.wait_ge(kx_psum, 1)
                act.activation(kis[:, :, 0:PAST], banks[0][:, :].rearrange("p (s k) -> p s k", s=2), ACT.Copy).then_inc(kx_done, 1)
                for n in range(3 * NT, 4 * NT):
                    proj_out(n)
                for i, dst in enumerate((kit, qit[:, 0, :], qit[:, 1, :])):
                    act.wait_ge(kx_psum, i + 2)
                    act.activation(dst, banks[1 + i][:, :], ACT.Copy).then_inc(kx_done, 1)
                act.wait_ge(kx_psum, 5)
                for c in range(4):
                    r = slice(ID * c, ID * c + ID)
                    src = banks[0][r, 0:P].rearrange("p (s q) -> p s q", s=2)[:, :, FRAMES * c:FRAMES * c + FRAMES]
                    ins = act.activation(kis[r, :, PAST:PAST + FRAMES], src, ACT.Copy)
                ins.then_inc(kx_done, 1)
                for at, t in enumerate(IDX_TILES):
                    for h in range(IH):
                        m = IH * at + h
                        act.wait_ge(idx_psum, m + 1)
                        if m >= 2:
                            act.wait_ge(idx_used, m - 1)
                        act.activation(relu_b[m % 2][:, 0:KEYS[t]], banks[m % 4][:, 0:KEYS[t]], ACT.Relu).then_inc(idx_relu, 1)
                    if at == 0:
                        for n in range(4 * NT, 5 * NT):
                            proj_out(n)
                for i, dst in enumerate([kt[:, :]] + [qt[:, j, :] for j in range(GQ)]):
                    act.wait_ge(qk_psum, i + 1)
                    act.activation(dst, banks[0 if i == 0 else 3 + i][:, :], ACT.Copy).then_inc(qk_done, 1)

                def stream_keys(g):
                    for s2 in range(2):
                        act.wait_ge(ks_psum, 4 * g + s2 + 1)
                        act.activation(qkv[:, 2 * s2:2 * s2 + 2, 0:PAST],
                                       banks[6 + s2][:, :].rearrange("p (s k) -> p s k", s=2), ACT.Copy).then_inc(ks_done, 1)
                    act.wait_ge(ks_psum, 4 * g + 3)
                    for c in range(2):
                        r = slice(HD * c, HD * c + HD)
                        src = banks[6][r, 0:P].rearrange("p (s q) -> p s q", s=4)[:, :, FRAMES * c:FRAMES * c + FRAMES]
                        ins = act.activation(qkv[r, 0:4, PAST:PAST + FRAMES], src, ACT.Copy)
                    ins.then_inc(ks_done, 1)

                def probs_out(n):
                    t = ATT_UNITS[n][0]
                    act.wait_ge(pt_psum, n + 1)
                    if n >= 2:
                        act.wait_ge(pv_done, n - 1)
                    w = KEYS[t] if t < PT else 3 * P
                    act.activation(probs_t[n % 2][:, 0:w], banks[2 + n % 2][:, 0:w], ACT.Copy).then_inc(pt_done, 1)

                def tile_out(t):
                    act.wait_ge(o_psum, t + 1)
                    act.activation(att[:, :, t * P:(t + 1) * P],
                                   banks[4 + t % 2][:, :].rearrange("p (j q) -> p j q", j=GQ), ACT.Copy).then_inc(o_done, 1)

                for n in range(NAU):
                    t = ATT_UNITS[n][0]
                    if n in PREP_AT:
                        stream_keys(PREP_AT[n])
                    act.wait_ge(p_raw, n + 1)
                    k = n % 2
                    act.activation(probs[k][:, 0:KEYS[t]], probs[k][:, 0:KEYS[t]], ACT.Exp,
                                   bias=nmx[:, k:k + 1], scale=ATT_SCALE, accum_out=den[:, k:k + 1]).then_inc(p_exp, 1)
                    if n >= 1:
                        probs_out(n - 1)
                    if n >= 2 and ATT_UNITS[n - 2][0] != ATT_UNITS[n - 1][0]:
                        tile_out(ATT_UNITS[n - 2][0])
                probs_out(NAU - 1)
                tile_out(PT)
                for m in range(2):
                    act.wait_ge(sw_psum, m + 1)
                    act.activation(scr[:, 512 * m:512 * m + 512], banks[6 + m][:, :], ACT.Copy).then_inc(sw_done, 1)
                for t in range(NT):
                    act.wait_ge(sgt_psum, t + 1)
                    act.activation(sgt[:, :, t * P:(t + 1) * P],
                                   banks[4 + t % 4][:, :].rearrange("p (g q) -> p g q", g=SG), ACT.Copy).then_inc(sgt_done, 1)
                for n in range(2 * NT):
                    act.wait_ge(mg_gate, n + 1)
                    if n >= 2:
                        act.wait_ge(mg_done, n - 1)
                    for m in range(2):
                        c0 = 1024 * (n % 2) + 512 * m
                        ins = act.activation(scr[:, c0:c0 + 512], banks[4 * (n % 2) + m][:, :], ACT.Sigmoid)
                    ins.then_inc(mg_sig, 1)
                for n in range(2 * NT):
                    t, hf = divmod(n, 2)
                    act.wait_ge(mt_psum, n + 1)
                    act.activation(xt[:, 4 * hf:4 * hf + 4, t * P:(t + 1) * P],
                                   banks[n % 4][:, :].rearrange("p (k q) -> p k q", k=4), ACT.Copy).then_inc(mt_done, 1)
                for m in range(2):
                    act.wait_ge(r_sub, m + 1)
                    v = (eg, e8)[m]
                    act.activation(v, v, ACT.Exp).then_inc(r_exp, 1)
                with act.Fori(0, EXPERTS // SLOTS) as i:
                    for q in range(SLOTS):
                        e = SLOTS * i + q
                        act.wait_ge(gu_psum, 2 * e + 1)
                        for c in range(2):
                            ins = act.activation(hid[:, 320 * c:320 * c + 320], banks[c][:, 0:320], ACT.Silu)
                        ins.then_inc(silu_done, 1)
                next_layer(act, "act")

        @block.vector
        def _(dve):
            V = nc.vector
            count = [0]

            def then(ins):
                count[0] += 1
                ins.then_inc(dve_chain, 1)
                dve.wait_ge(dve_chain, count[0])

            def square_sums(done):
                for t in range(NT):
                    then(V.tensor_tensor_reduce(out=xn[t % 2], in0=x[:, t, :], in1=x[:, t, :], scale=1.0, scalar=0.0,
                                                op0=ALU.mult, op1=ALU.add, accum_out=ss[:, t:t + 1]))
                V.nop().then_inc(done, 1)

            def norm(phase, L):
                square_sums(ss_ready)
                dve.wait_ge(rs_ready, phase + 1)
                if phase == 0:
                    dve.wait_ge(params, 16 * 21 * L + 16 * 21)

                def rows(t):
                    if t >= 2:
                        dve.wait_ge(xt_psum, 2 * NT * phase + 2 * (t - 1))
                    V.tensor_scalar(xn[t % 2], x[:, t, :], rs[:, t:t + 1], None, ALU.mult).then_inc(xn_ready, 1)

                rows(0)
                rows(1)
                for t in range(NT):
                    for hf in range(2):
                        n = 2 * t + hf
                        dve.wait_ge(xt_psum, 2 * NT * phase + n + 1)
                        V.tensor_tensor(xt[:, 4 * hf:4 * hf + 4, t * P:(t + 1) * P],
                                        banks[n % 4][:, :].rearrange("p (k q) -> p k q", k=4),
                                        gain[:, phase, 4 * hf:4 * hf + 4].unsqueeze(2).broadcast_to([P, 4, P]),
                                        ALU.mult).then_inc(xt_done, 1)
                    if t + 2 < NT:
                        rows(t + 2)

            def rotate(t, c0, heads, d, table):
                h2 = d // 2
                src = qkv[:, t, c0:c0 + heads * d].rearrange("p (h a i) -> p h a i", a=2, i=h2)
                cos, sin = table[:, 0:h2], table[:, h2:d]
                w = heads * d
                t1 = scr[:, 0:w].rearrange("p (h a i) -> p h a i", a=2, i=h2)
                t2 = scr[:, 1024:1024 + w].rearrange("p (h a i) -> p h a i", a=2, i=h2)
                bc = [P, heads, h2]
                for z in range(2):
                    V.tensor_tensor(t1[:, :, z, :], src[:, :, z, :], over(cos, heads, 1, bc), ALU.mult)
                    ins = V.tensor_tensor(t2[:, :, z, :], src[:, :, 1 - z, :], over(sin, heads, 1, bc), ALU.mult)
                then(ins)
                V.tensor_tensor(src[:, :, 0, :], t1[:, :, 0, :], t2[:, :, 0, :], ALU.subtract)
                then(V.tensor_tensor(src[:, :, 1, :], t1[:, :, 1, :], t2[:, :, 1, :], ALU.add))

            def select(t):
                s = score(t)
                k = TOPK_P if t < PT else TOPK_S
                for r in range(-(-k // 8)):
                    then(V.max(best, s))
                    if k - 8 * r < 8:
                        then(V.memset(best[:, k - 8 * r:8], SEL))
                    then(V.match_replace(out=s, in_to_replace=best, in_values=s, imm_value=SEL))
                then(V.tensor_scalar(s, s, SEL, OFF, ALU.not_equal, ALU.mult))

            dve.wait_ge(s_const, 1)
            dve.wait_ge(s_rope, 16)
            dve.wait_ge(s_x, 16 * NT)
            with dve.Fori(0, DEPTH) as L:
                count[0] = 0
                norm(0, L)
                for t in range(NT):
                    dve.wait_ge(proj_free, 2 * NT + t + 1)
                    dve.wait_ge(xt_psum, 2 * NT)
                    k_all = HEADS + KV
                    rotate(t, 0, k_all, HD, rope_t[:, t, 0:HD])
                    rotate(t, QI0, IH + 1, ID, rope_t[:, t, HD:HD + ID])
                    V.tensor_scalar(qkv[:, t, WI0:QKV_W], qkv[:, t, WI0:QKV_W], IH ** -0.5, None,
                                    ALU.mult).then_inc(rope_done, 1)
                for j in range(2):
                    dve.wait_ge(kx_psum, 6 + j)
                    for s in range(2):
                        ins = V.tensor_tensor(qis[:, s, 4 * j:4 * j + 4, :],
                                              banks[1 + j][:, :].rearrange("p (h q) -> p h q", h=4),
                                              over(quad[:, s, :], 4, 1, [P, 4, P]), ALU.mult)
                    ins.then_inc(qis_done, 1)
                V.memset(score(0)[:, :], 0.0).then_inc(dve_chain, 1)
                count[0] += 1
                dve.wait_ge(dve_chain, count[0])
                then(V.memset(score(0)[0:64, 64:P], OFF))
                dve.wait_ge(rope_done, NT)
                for at, t in enumerate(IDX_TILES):
                    s = score(t)
                    for h in range(IH):
                        m = IH * at + h
                        dve.wait_ge(idx_relu, m + 1)
                        w = qkv[:, t, WI0 + h:WI0 + h + 1]
                        r = relu_b[m % 2][:, 0:KEYS[t]]
                        if h == 0:
                            ins = V.tensor_scalar(s, r, w, None, ALU.mult)
                        else:
                            ins = V.scalar_tensor_tensor(s, r, w, s, ALU.mult, ALU.add)
                        ins.then_inc(idx_used, 1)
                        dve.wait_ge(idx_used, m + 1)
                    if t < PT:
                        then(V.memset(s[0:64, KEYS[t] - 64:KEYS[t]], NEG))
                    select(t)

                dve.wait_ge(proj_free, 5 * NT)
                for t in range(NT):
                    then(V.bn_stats(bns, uv[:, 1, t, :]))
                    then(V.bn_aggr(moments[:, t, :], bns))
                V.nop().then_inc(ln_stat, 1)
                dve.wait_ge(ln_rs, 1)
                dve.wait_ge(ln_loaded, 32 * L + 32)
                for t in range(NT):
                    v = uv[:, 1, t, :]
                    then(V.tensor_scalar(v, v, moments[:, t, 0:1], lrs[:, t:t + 1], ALU.subtract, ALU.mult))
                    then(V.tensor_tensor(v, v, ln_g, ALU.mult))
                    V.tensor_tensor(v, v, ln_b, ALU.add).then_inc(ln_done, 1)
                dve.wait_ge(ln_done, NT)

                def masked_logits(n):
                    t = ATT_UNITS[n][0]
                    if n in PREP_AT:
                        g = PREP_AT[n]
                        dve.wait_ge(ks_psum, 4 * g + 4)
                        for s in range(4):
                            ins = V.tensor_tensor(qts[:, s, :, :], banks[7][:, :].rearrange("p (j q) -> p j q", j=GQ),
                                                  over(pair[:, s, :], GQ, 1, [P, GQ, P]), ALU.mult)
                        ins.then_inc(qts_done, 1)
                    k = n % 2
                    dve.wait_ge(s_psum, n + 1)
                    if n >= 2:
                        dve.wait_ge(pt_psum, n - 1)
                    then(V.tensor_tensor_reduce(out=probs[k][:, 0:KEYS[t]], in0=banks[n % 2][:, 0:KEYS[t]], in1=score(t),
                                                scale=1.0, scalar=NEG, op0=ALU.add, op1=ALU.max,
                                                accum_out=mx[:, k:k + 1]))
                    V.tensor_scalar(nmx[:, k:k + 1], mx[:, k:k + 1], -ATT_SCALE, None, ALU.mult).then_inc(p_raw, 1)

                def normalise(n):
                    t = ATT_UNITS[n][0]
                    k = n % 2
                    p = probs[k][:, 0:KEYS[t]]
                    dve.wait_ge(p_exp, n + 1)
                    then(V.reciprocal(rden[:, k:k + 1], den[:, k:k + 1]))
                    ins = V.tensor_scalar(p, p, rden[:, k:k + 1], None, ALU.mult)
                    if t == PT:
                        then(ins)
                        ins = V.tensor_tensor(probs[k][:, 3 * P:4 * P].rearrange("p (b i) -> p b i", b=STREAMS),
                                              over(p[:, PAST:PAST + FRAMES], STREAMS, 1, [P, STREAMS, FRAMES]),
                                              own[:, :].unsqueeze(2).broadcast_to([P, STREAMS, FRAMES]), ALU.mult)
                    ins.then_inc(p_ready, 1)

                masked_logits(0)
                for n in range(NAU):
                    if n + 1 < NAU and n + 1 not in PREP_AT:
                        masked_logits(n + 1)
                    normalise(n)
                    if n + 1 in PREP_AT:
                        masked_logits(n + 1)

                dve.wait_ge(slot[SU % SLOTS], landed(SU))
                sw = ring[:, SU % SLOTS, :]
                w4 = sw[:, 0:512].rearrange("p (g j) -> p g j", g=SG)
                low = over(tril[:, :], SG, 1, [P, SG, P])
                V.tensor_tensor(w4, w4, low, ALU.mult).then_inc(swm_ready, 1)
                ws = sw[:, 1024:1536].rearrange("p (g b j) -> p g b j", g=SG, b=STREAMS)
                for g in range(SG):
                    ins = V.tensor_tensor(ws[:, g, :, :], over(corner[:, g, :], STREAMS, 1, [P, STREAMS, FRAMES]),
                                          own[:, :].unsqueeze(2).broadcast_to([P, STREAMS, FRAMES]), ALU.mult)
                then(ins)
                ws4 = sw[:, 1024:1536].rearrange("p (g j) -> p g j", g=SG)
                V.tensor_tensor(ws4, ws4, low, ALU.mult).then_inc(swm_ready, 1)
                for t in range(NT):
                    dve.wait_ge(sg_psum, t + 1)
                    for g in range(SG):
                        u = uv[:, 0, t, g * P:(g + 1) * P]
                        ins = V.scalar_tensor_tensor(u, banks[t % 4][:, g * P:(g + 1) * P],
                                                     sbias[:, t // PT, g:g + 1], u, ALU.add, ALU.mult)
                    ins.then_inc(sg_used, 1)
                for n in range(2 * NT):
                    c, t = divmod(n, NT)
                    dve.wait_ge(mg_sig, n + 1)
                    dve.wait_ge(mg_proj, n + 1)
                    b = banks[4 * (n % 2):4 * (n % 2) + 4]
                    t1 = scr[:, 1024 * (n % 2):1024 * (n % 2) + 512]
                    t2 = scr[:, 1024 * (n % 2) + 512:1024 * (n % 2) + 1024]
                    V.tensor_tensor(t1, t1, b[2][:, :], ALU.mult)
                    then(V.tensor_tensor(t2, t2, b[3][:, :], ALU.mult))
                    if n == 2 * NT - 1:
                        dve.wait_ge(rows_sent, 1)
                    V.tensor_tensor(uv[:, c, t, :], t1, t2, ALU.add).then_inc(mg_done, 1)
                for n in range(2 * NT):
                    c, t = divmod(n, NT)
                    dve.wait_ge(xo_psum, n + 1)
                    xs = x[:, t, BLK * c:BLK * c + BLK]
                    V.tensor_tensor(xs, xs, banks[4 + n % 4][:, :], ALU.add).then_inc(xo_done, 1)
                dve.wait_ge(xo_done, 2 * NT)
                norm(1, L)

                dve.wait_ge(r_psum, 1)
                then(V.tensor_tensor(logit, banks[4][:, 0:36 * NT].rearrange("p (t c) -> p t c", t=NT),
                                     over(rbias[:, :], NT, 1, [P, NT, 36]), ALU.add))
                for w_, r_ in ((w16, r8), (w16e, r8e)):
                    V.memset(w_, NEG)
                    then(V.memset(r_, NEG))
                then(V.tensor_copy(w16[:, :, 0:NG], logit[:, :, 0:NG]))
                for t in range(NT):
                    ins = V.max(m8[:, t, :], w16[:, t, :])
                then(ins)
                V.tensor_tensor(eg, logit[:, :, 0:NG], m8[:, :, 0:1].broadcast_to([P, NT, NG]),
                                ALU.subtract).then_inc(r_sub, 1)
                then(V.tensor_copy(r8[:, :, 0:1], m8[:, :, 0:1]))
                for t in range(NT):
                    ins = V.match_replace(out=w16[:, t, :], in_to_replace=r8[:, t, :], in_values=w16[:, t, :], imm_value=SEL)
                then(ins)
                then(V.tensor_scalar(hot, w16[:, :, 0:NG], SEL, None, ALU.is_equal))
                for t in range(NT):
                    ins = V.tensor_tensor(picked[:, t, :, :], logit[:, t, NG:].rearrange("p (g e) -> p g e", g=NG),
                                          hot[:, t, :].unsqueeze(2).broadcast_to([P, NG, NE]), ALU.mult)
                then(ins)
                then(V.tensor_reduce(l8, picked.rearrange("p t g e -> p t e g"), AX.X, ALU.add))
                then(V.tensor_copy(w16e[:, :, 0:NE], l8))
                for t in range(NT):
                    ins = V.max(m8e[:, t, :], w16e[:, t, :])
                then(ins)
                V.tensor_tensor(e8, l8, m8e[:, :, 0:1].broadcast_to([P, NT, NE]), ALU.subtract).then_inc(r_sub, 1)
                then(V.tensor_copy(r8e[:, :, 0:2], m8e[:, :, 0:2]))
                for t in range(NT):
                    ins = V.match_replace(out=w16e[:, t, :], in_to_replace=r8e[:, t, :], in_values=w16e[:, t, :], imm_value=SEL)
                then(ins)
                then(V.tensor_scalar(w16e[:, :, 0:NE], w16e[:, :, 0:NE], SEL, None, ALU.is_equal))
                dve.wait_ge(r_exp, 2)
                then(V.tensor_reduce(gsum, eg, AX.X, ALU.add))
                then(V.tensor_tensor(e8, e8, w16e[:, :, 0:NE], ALU.mult))
                then(V.tensor_reduce(esum, e8, AX.X, ALU.add))
                then(V.tensor_tensor(escale, gsum, esum, ALU.mult))
                then(V.reciprocal(gw, escale))
                then(V.tensor_tensor(e8, e8, gw.unsqueeze(2).broadcast_to([P, NT, NE]), ALU.mult))
                for t in range(NT):
                    ins = V.tensor_tensor(gate[:, t, :].rearrange("p (g e) -> p g e", g=NG),
                                          over(e8[:, t, :], NG, 1, [P, NG, NE]),
                                          hot[:, t, :].unsqueeze(2).broadcast_to([P, NG, NE]), ALU.mult)
                then(ins)
                V.nop().then_inc(y_free, 4)
                V.nop().then_inc(h_done, 1)

                with dve.Fori(0, EXPERTS // SLOTS) as i:
                    for q in range(SLOTS):
                        e = SLOTS * i + q
                        dve.wait_ge(silu_done, e + 1)
                        dve.wait_ge(gu_psum, 2 * e + 2)
                        for c in range(2):
                            h = hid[:, 320 * c:320 * c + 320]
                            ins = V.tensor_tensor(h, h, banks[2 + c][:, 0:320], ALU.mult)
                        ins.then_inc(h_done, 1)
                        for n in range(2 * NT):
                            t, c = divmod(n, 2)
                            xs = x[:, t, BLK * c:BLK * c + BLK]
                            dve.wait_ge(y_psum, 2 * NT * e + n + 1)
                            V.scalar_tensor_tensor(xs, banks[4 + n % 4][:, :], gate[:, t, bass.ds(e, 1)], xs,
                                                   ALU.mult, ALU.add).then_inc(y_free, 1)
                next_layer(dve, "dve")

            count[0] = 0
            square_sums(s_fin_ss)
            dve.wait_ge(s_fin_rs, 1)
            dve.wait_ge(s_rope, 32)
            for t in range(NT):
                dve.wait_ge(s_fin, t)
                V.tensor_scalar(x[:, t, :], x[:, t, :], rs[:, t:t + 1], None, ALU.mult).then_inc(s_fin_x, 1)
                dve.wait_ge(s_fin_x, t + 1)
                V.tensor_tensor(x[:, t, :], x[:, t, :], fin_gain, ALU.mult).then_inc(s_fin, 1)


_INS = ("x_prompt x_sample cache_k cache_v cache_kidx norm1 w_in sgu_ln_g sgu_ln_b sgu_w sgu_b w_pa w_pb w_out "
        "norm2 w_rg b_rg w_re b_re w_eg w_eu w_ed final_norm").split()
_OUTS = [(1, SEQ, D), (STREAMS, FRAMES, D), (DEPTH, 1, SEQ, KV, HD), (DEPTH, 1, SEQ, KV, HD), (DEPTH, 1, SEQ, ID),
         (DEPTH, STREAMS, FRAMES, KV, HD), (DEPTH, STREAMS, FRAMES, KV, HD), (DEPTH, STREAMS, FRAMES, ID),
         (DEPTH, STREAMS, FRAMES, SW)]


def _rope_table():
    pos = np.concatenate([np.arange(SEQ), PAST + np.tile(np.arange(FRAMES), STREAMS)]).astype(np.float32)
    parts = []
    for d in (HD, ID):
        inv = np.float32(10000.0) ** (-np.arange(0, d, 2, dtype=np.float32) / np.float32(d))
        ang = pos[:, None] * inv[None, :].astype(np.float32)
        parts += [np.cos(ang), np.sin(ang)]
    return np.concatenate(parts, axis=1).astype(np.float32).reshape(NT, P, HD + ID)


def kernel(**inputs):
    import concourse.bacc as bacc
    from concourse.bass_utils import run_bass_kernel_spmd

    nc = bacc.Bacc("TRN2", target_bir_lowering=False, num_devices=1)
    arrays, a = {}, {}
    for name in _INS:
        arrays[f"in_{name}"] = v = np.ascontiguousarray(inputs[name])
        a[name] = nc.dram_tensor(f"in_{name}", v.shape, F32, kind="ExternalInput").ap()
    arrays["in_rope"] = v = _rope_table()
    a["rope"] = nc.dram_tensor("in_rope", v.shape, F32, kind="ExternalInput").ap()
    o = [nc.dram_tensor(f"out_{i}", s, F32, kind="ExternalOutput").ap() for i, s in enumerate(_OUTS)]
    build(nc, a, o)
    r = run_bass_kernel_spmd(nc, [arrays], core_ids=[0])
    return tuple(r.results[0][f"out_{i}"] for i in range(len(_OUTS)))
```

```python
from contextlib import ExitStack

import numpy as np

import concourse.bass as bass
from concourse import mybir

F32, I32, U32 = mybir.dt.float32, mybir.dt.int32, mybir.dt.uint32
ALU = mybir.AluOpType
ACT = mybir.ActivationFunctionType
AX = mybir.AxisListType

P = 128
DEPTH, D = 2, 1024
SEQ, STREAMS, FRAMES, PAST = 512, 8, 16, 256
PT = SEQ // P
NT = PT + 1
ROWS = NT * P
KD = D // P
HEADS, KV, HD = 8, 2, 64
GQ = HEADS // KV
IH, ID = 8, 32
SG, SW = 4, 512
NG, NE = 4, 8
EXPERTS, HID = NG * NE, 128
EPS = 1e-6
ATT_SCALE = HD ** -0.5
COLS = 4136
K0, V0, QI0, KI0, WI0 = 512, 640, 768, 1024, 1056
QKV_W = 1064
Q_REP = 272
U0, VS0, GA0, GB0 = 1064, 1576, 2088, 3112
BLK = 512
TOPK_P, TOPK_S = 128, 68
KEYS = [P * (t + 1) for t in range(PT)] + [PAST + FRAMES]
MB_AT = [sum(KEYS[:t]) for t in range(NT)]
MB_W = sum(KEYS)
NEG = -3.3e38
SEL = -3.4e38
OFF = -1e30
SLOTS = 4
SLOT_W = KD * BLK
BR = 128
PAIRS = 2 * ROWS
OVER = (PAIRS - 1) // BR
TURNS = EXPERTS // SLOTS
AHEAD = 3
COLS_T = EXPERTS + OVER
YBUF = 2
AT_TABLE = 1160
AT_OVER = AT_TABLE + 2 * COLS_T
AT_WIDE = AT_OVER + OVER + 1 + 2 * SLOTS
NOWHERE = 1e6
(QU, KU, IU, UU, VU, KCU, VCU, SU) = range(8)
GAU, GBU, PABU = (8, 11), (9, 12), (10, 13)
OUTU = (14, 15)
IDX_TILES = (3, 2, 1, 4)
UNIT_DMAS = {u: 1 for u in range(16)} | {IU: 3, KCU: 4, VCU: 2, PABU[0]: 4, PABU[1]: 4}


def landed(u):
    return 16 * sum(UNIT_DMAS[v] for v in range(u + 1) if v % SLOTS == u % SLOTS)


PROMPT_UNITS = [(t, j, g) for t in range(PT) for j in range(GQ) for g in range(KV)]
STREAM_UNITS = [(PT, j, g) for g in range(KV) for j in range(GQ)]
ATT_UNITS = PROMPT_UNITS + STREAM_UNITS
NPU, NAU = len(PROMPT_UNITS), len(ATT_UNITS)
PREP_AT = {NPU: 0, NPU + GQ: 1}


def over(ap, n, axis, shape):
    return ap.unsqueeze(axis).broadcast_to(shape)


def build(nc, a, o):
    ctx = ExitStack()
    with ctx:
        def sb(name, shape):
            return ctx.enter_context(nc.sbuf_tensor(name, shape, F32))

        def sem(name):
            return ctx.enter_context(nc.semaphore(name))

        ctx.enter_context(nc.allow_non_contiguous_dma("small parameters"))
        x = sb("x", [P, NT, D])
        xt = sb("xt", [P, KD, ROWS])
        qkv = sb("qkv", [P, NT, QKV_W])
        uv = sb("uv", [P, 2, NT, BLK])
        ring = sb("ring", [P, SLOTS, SLOT_W])
        att = sb("att", [P, GQ, ROWS])
        sgt = sb("sgt", [P, SG, ROWS])
        mb = sb("mb", [P, MB_W])
        kt = sb("kt", [P, SEQ])
        scr = sb("scr", [P, 2048])
        ident = sb("ident", [P, P])
        tril = sb("tril", [P, P])
        rope_t = sb("rope_t", [P, NT, HD + ID])
        quad = sb("quad", [P, 2, P])
        pair = sb("pair", [P, 4, P])
        own = sb("own", [P, STREAMS])
        gain = sb("gain", [P, 2, KD])
        rbias = sb("rbias", [P, NG + EXPERTS])
        sbias = sb("sbias", [P, 2, SG])
        corner = sb("corner", [P, SG, FRAMES])
        stat = sb("stat", [P, 64])
        ss, rs = stat[:, 0:5], stat[:, 5:10]
        mx, nmx, den, rden = (stat[:, 10 + 2 * i:12 + 2 * i] for i in range(4))
        moments = stat[:, 18:28].rearrange("p (t c) -> p t c", c=2)
        lrs = stat[:, 28:33]
        half = stat[:, 33:38]
        bns = stat[:, 38:44]
        best = stat[:, 44:52]
        var_e = stat[:, 52:57]
        over_sum = stat[0:1, 57:58]
        over_past = stat[0:1, 58:59].bitcast(I32)
        over_new = stat[0:1, 59:60]

        qit = att[:, :, :].rearrange("p a b -> p (a b)")[:, 0:1024].rearrange("p (j r) -> p j r", j=2)
        kit = att[:, :, :].rearrange("p a b -> p (a b)")[:, 1024:1536]
        kis = att[:, :, :].rearrange("p a b -> p (a b)")[:, 1536:1536 + 2 * KEYS[PT]].rearrange(
            "p (s k) -> p s k", s=2)
        sgt_flat = sgt[:, :, :].rearrange("p a b -> p (a b)")
        qis = sgt_flat[:, 0:2048].rearrange("p (s h q) -> p s h q", s=2, h=IH)
        qt = sgt_flat[:, 0:2048].rearrange("p (j r) -> p j r", j=GQ)
        qts = sgt_flat[:, 0:2048].rearrange("p (s j q) -> p s j q", s=4, j=GQ)

        ki_rep = kt[:, :]
        qis_rep = mb[:, 0:1024].rearrange("p (h c d) -> p h c d", h=IH, c=4)
        kis_rep = mb[:, 1024:1152]
        ks_rep = [sgt_flat[:, 2048:2176], sgt_flat[:, 2176:2304]]

        def score(t):
            return mb[:, MB_AT[t]:MB_AT[t] + KEYS[t]]

        probs = [scr[:, 0:512], scr[:, 512:1024]]
        probs_t = [scr[:, 1024:1536], scr[:, 1536:2048]]
        relu_b = [scr[:, 0:512], scr[:, 512:1024]]
        ln_g, ln_b = scr[:, 1024:1536], scr[:, 1536:2048]
        xn = [scr[:, 0:1024], scr[:, 1024:2048]]
        sgw_t = [scr[:, 0:512].rearrange("p (g i) -> p g i", g=SG),
                 scr[:, 512:1024].rearrange("p (g i) -> p g i", g=SG)]
        fin_gain = uv[:, 0, 0:2, :].rearrange("p t c -> p (t c)")

        def mbv(at, w):
            return mb[:, at:at + w]
        logit = mbv(0, 180).rearrange("p (t c) -> p t c", t=NT)
        w16 = mbv(180, 80).rearrange("p (t c) -> p t c", t=NT)
        m8 = mbv(260, 40).rearrange("p (t c) -> p t c", t=NT)
        r8 = mbv(300, 40).rearrange("p (t c) -> p t c", t=NT)
        hot = mbv(340, 20).rearrange("p (t c) -> p t c", t=NT)
        eg = mbv(360, 20).rearrange("p (t c) -> p t c", t=NT)
        gsum, gw, esum, escale = (mbv(380 + 5 * i, 5) for i in range(4))
        picked = mbv(400, 160).rearrange("p (t g e) -> p t g e", t=NT, g=NG)
        l8 = mbv(560, 40).rearrange("p (t c) -> p t c", t=NT)
        e8 = mbv(600, 40).rearrange("p (t c) -> p t c", t=NT)
        gate = mbv(640, 160).rearrange("p (t e) -> p t e", t=NT)
        w16e = mbv(800, 80).rearrange("p (t c) -> p t c", t=NT)
        m8e = mbv(880, 40).rearrange("p (t c) -> p t c", t=NT)
        r8e = mbv(920, 40).rearrange("p (t c) -> p t c", t=NT)
        wr = kt[:, 0:KD * 36].rearrange("p (k c) -> p k c", k=KD)
        ids = kt[:, 288:288 + BR + 2 * NT]
        pair_at = mbv(960, 30).rearrange("p (w k t) -> p w k t", w=3, k=2)
        code_k = mbv(990, 10).rearrange("p (k t) -> p k t", k=2)
        start, need, scan_a, scan_b, size = (mbv(1000 + 32 * i, 32) for i in range(5))
        table = mbv(AT_TABLE, 2 * COLS_T)[0:BR, :].bitcast(U32).rearrange("p (w b) -> p w b", w=2)
        over_expert = mbv(AT_OVER, OVER)[0:1, :].bitcast(I32)
        over_count = mbv(AT_OVER + OVER, 1)[0:1, :].bitcast(I32)
        now = [[mbv(AT_OVER + OVER + 1 + SLOTS * w + q, 1)[0:BR, :].bitcast(U32) for q in range(SLOTS)] for w in range(2)]
        wide = mbv(AT_WIDE, 2 * COLS_T)[0:BR, :].rearrange("p (w b) -> p w b", w=2)
        pads = mbv(AT_WIDE + 2 * COLS_T, COLS_T)[0:BR, :]
        ones = scr[:, 0:P]
        before = scr[:, 1728:1856]
        (chosen, total, base, rank, whole, block_of, place, code, equal, part) = (
            scr[:, P + 160 * i:P + 160 * (i + 1)].rearrange("p (t e) -> p t e", t=NT) for i in range(10))
        onehot = att[:, :, :].rearrange("p a b -> p (a b)")[:, 0:2 * NT * (BR + COLS_T)].rearrange(
            "p (m c) -> p m c", m=2 * NT)
        begun = sgt_flat[0:1, 0:OVER * EXPERTS].rearrange("p (b e) -> p b e", e=EXPERTS)
        xt_flat = xt[:, :, :].rearrange("p k r -> p (k r)")
        xin_t = [xt_flat[:, KD * BR * z:KD * BR * (z + 1)].rearrange("p (k r) -> p k r", k=KD) for z in range(2)]
        hidden = [xt_flat[:, 2 * KD * BR + BR * z:2 * KD * BR + BR * (z + 1)] for z in range(2)]
        yout = [scr[0:BR, D * z:D * (z + 1)] for z in range(YBUF)]
        xn2 = [uv[:, :, :, :].rearrange("p c t w -> p (c t w)")[:, D * t:D * (t + 1)] for t in range(NT)]
        xin = [xn2[q][0:BR, :] for q in range(SLOTS)]

        banks = [ctx.enter_context(nc.psum_tensor(f"bank{i}", [P, BLK], F32)) for i in range(8)]

        s_const = sem("s_const")
        s_pool = sem("s_pool")
        s_rope = sem("s_rope")
        s_x = sem("s_x")
        s_out = sem("s_out")
        s_fin = sem("s_fin")
        s_fin_ss = sem("s_fin_ss")
        s_fin_rs = sem("s_fin_rs")
        s_fin_x = sem("s_fin_x")
        s_go = {e: sem(f"s_go_{e}") for e in ("pe", "act", "dve", "pool")}
        params, ln_loaded, wr_loaded = sem("params"), sem("ln_loaded"), sem("wr_loaded")
        kv_out, sguv_out = sem("kv_out"), sem("sguv_out")
        x_in = [sem(f"x_in{q}") for q in range(SLOTS)]
        y_out = [sem(f"y_out{z}") for z in range(YBUF)]
        x_over, y_over = sem("x_over"), sem("y_over")
        first = sem("arrived")
        arrived = first
        slot = [sem(f"slot{i}") for i in range(SLOTS)]
        names = ("unit_done rows_sent ss_ready rs_ready xn_ready "
                 "xt_psum xt_done proj_psum proj_free rope_done rep_done kx_psum kx_done qis_done idx_psum "
                 "idx_relu idx_used qk_psum qk_done s_psum p_raw p_exp p_ready pt_psum pt_done "
                 "pv_done o_psum o_done ks_psum ks_done qts_done ln_stat ln_rs ln_done swm_ready "
                 "sw_psum sw_done sg_psum sg_used sgt_psum sgt_done mg_gate mg_proj mg_sig mg_done "
                 "mt_psum mt_done xo_psum xo_done r_psum r_exp r_sub gu_psum silu_done h_done "
                 "xd_out chosen_ready count_psum experts_known onehot_ready table_psum table_ready "
                 "xin_psum xin_ready turn over_free over_sent over_w y_ready y_psum dve_chain act_chain").split()
        (unit_done, rows_sent, ss_ready, rs_ready, xn_ready,
         xt_psum, xt_done, proj_psum, proj_free, rope_done, rep_done, kx_psum, kx_done, qis_done, idx_psum,
         idx_relu, idx_used, qk_psum, qk_done, s_psum, p_raw, p_exp, p_ready, pt_psum, pt_done,
         pv_done, o_psum, o_done, ks_psum, ks_done, qts_done, ln_stat, ln_rs, ln_done, swm_ready,
         sw_psum, sw_done, sg_psum, sg_used, sgt_psum, sgt_done, mg_gate, mg_proj, mg_sig, mg_done,
         mt_psum, mt_done, xo_psum, xo_done, r_psum, r_exp, r_sub, gu_psum, silu_done, h_done,
         xd_out, chosen_ready, count_psum, experts_known, onehot_ready, table_psum, table_ready,
         xin_psum, xin_ready, turn, over_free, over_sent, over_w, y_ready, y_psum, dve_chain, act_chain) = made = [sem(n) for n in names]
        combine_in = [sem(f"combine_in{t}") for t in range(NT)]
        layer_sems = [first, *slot, *made, *combine_in]

        xd = nc.dram_tensor("xd", (ROWS, D), F32, kind="Internal").ap()
        yd = nc.dram_tensor("yd", (2 * ROWS, D), F32, kind="Internal").ap()
        block = ctx.enter_context(nc.Block())

        def pairs(t):
            return ring[:, t % SLOTS, 2048 * (t // SLOTS):2048 * (t // SLOTS) + 2048].rearrange("p (k c) -> p k c", k=2)

        def earlier(eng):
            return eng.value_load(over_past[:, 0:1], min_val=0, max_val=16 * OVER * DEPTH)

        def next_layer(eng, key):
            eng.drain().then_inc(arrived, 1)
            eng.wait_ge(s_go[key], 1)
            eng.sem_clear(s_go[key])

        @block.sync
        def _(sp):
            for t in range(PT):
                sp.dma_start(x[:, t, :], a["x_prompt"][0, t * P:(t + 1) * P, :]).then_inc(s_x, 16)
            sp.dma_start(x[:, PT, :], a["x_sample"].rearrange("b t d -> (b t) d")).then_inc(s_x, 16)
            with sp.Fori(0, DEPTH) as L:
                w_in = a["w_in"][L].rearrange("(p k) c -> p k c", k=KD)

                def load(u, dst, src):
                    sp.dma_start(dst, src).then_inc(slot[u % SLOTS], 16)

                def at(u):
                    return ring[:, u % SLOTS, :]

                def cols(u, c0, w=BLK):
                    load(u, at(u)[:, 0:KD * w].rearrange("p (k c) -> p k c", k=KD), w_in[:, :, c0:c0 + w])

                for u in range(16):
                    if u >= SLOTS:
                        sp.wait_ge(unit_done, u - SLOTS + 1)
                    if u in (QU, KU):
                        cols(u, u * BLK)
                    elif u == IU:
                        cols(u, KI0, QKV_W - KI0)
                        for h in range(2):
                            load(u, at(u)[:, 512 + 256 * h:768 + 256 * h].rearrange("p (b d) -> p b d", b=STREAMS),
                                 a["cache_kidx"][L].rearrange("b (t p) d -> t p b d", p=P)[h])
                    elif u == UU:
                        cols(u, U0)
                    elif u == VU:
                        cols(u, VS0)
                    elif u == KCU:
                        for h in range(2):
                            for g in range(KV):
                                c0 = 512 * (2 * h + g)
                                load(u, at(u)[:, c0:c0 + 512].rearrange("p (b d) -> p b d", b=STREAMS),
                                     a["cache_k"][L].rearrange("b (t p) g d -> t g p b d", p=P)[h, g])
                    elif u == VCU:
                        for hf in range(2):
                            load(u, at(u)[:, 1024 * hf:1024 * hf + 1024].rearrange("p (n c) -> p n c", n=8),
                                 a["cache_v"][L].rearrange("b (t p) g d -> p (b t) (g d)", p=P)[:, 8 * hf:8 * hf + 8, :])
                    elif u == SU:
                        load(u, at(u)[:, 0:512].rearrange("p (g j) -> p g j", g=SG),
                             a["sgu_w"][L].rearrange("g i j -> i g j"))
                    elif u in GAU:
                        cols(u, GA0 + BLK * GAU.index(u))
                    elif u in GBU:
                        cols(u, GB0 + BLK * GBU.index(u))
                    elif u in PABU:
                        c0 = BLK * PABU.index(u)
                        for g in range(KV):
                            load(u, at(u)[64 * g:64 * g + 64, 0:2048].rearrange("p (j c) -> p j c", j=GQ),
                                 a["w_pa"][L].rearrange("(g j p) c -> g p j c", g=KV, p=HD)[g, :, :, c0:c0 + BLK])
                        for hf in range(2):
                            load(u, at(u)[:, 2048 + 1024 * hf:3072 + 1024 * hf].rearrange("p (j c) -> p j c", j=2),
                                 a["w_pb"][L].rearrange("(j p) c -> p j c", p=P)[:, 2 * hf:2 * hf + 2, c0:c0 + BLK])
                    else:
                        c0 = BLK * OUTU.index(u)
                        load(u, at(u).rearrange("p (k c) -> p k c", k=KD),
                             a["w_out"][L].rearrange("(k p) c -> p k c", p=P)[:, :, c0:c0 + BLK])

                def expert(q, row, landed_sem):
                    for n, w in enumerate(("w_eg", "w_eu")):
                        sp.dma_start(ring[:, q, 1024 * n:1024 * n + 1024],
                                     a[w].rearrange("l g e (p k) f -> (l g e) p (k f)", k=KD)[row]
                                     ).then_inc(landed_sem, 16)
                    sp.dma_start(ring[:, q, 2048:3072],
                                 a["w_ed"].rearrange("l g e f d -> (l g e) f d")[row]).then_inc(landed_sem, 16)

                for q in range(SLOTS):
                    sp.wait_ge(unit_done, 13 + q)
                    expert(q, EXPERTS * L + q, slot[q])
                for t in range(NT):
                    sp.wait_ge(xn_ready, NT + t + 1)
                    sp.dma_start(xd[t * P:(t + 1) * P, :], xn2[t]).then_inc(xd_out, 16)
                with sp.Fori(0, TURNS - 1) as i:
                    for q in range(SLOTS):
                        sp.wait_ge(y_psum, SLOTS * i + (q + 1))
                        expert(q, EXPERTS * L + (SLOTS * i + (SLOTS + q)), slot[q])
                sp.wait_ge(experts_known, 1)
                with sp.If(sp.value_load(over_count[:, 0:1], min_val=0, max_val=OVER) != 0):
                    with sp.Fori(0, OVER) as v:
                        sp.wait_ge(y_psum, v + EXPERTS)
                        e = sp.value_load(over_expert[:, bass.ds(v, 1)], min_val=0, max_val=EXPERTS - 1)
                        expert(0, EXPERTS * L + e, over_w)
                    sp.wait_ge(y_over, earlier(sp) + (16 * OVER + 16))
                    sp.sem_inc(over_sent, 1)
                sp.wait_ge(y_psum, EXPERTS)
                for z in range(YBUF):
                    sp.wait_ge(y_out[z], 16 * (EXPERTS // YBUF) * L + (16 * (EXPERTS // YBUF) + 16))
                    sp.sem_inc(turn, 1)
                sp.wait_ge(turn, YBUF)
                for t in range(NT):
                    sp.dma_start(pairs(t), yd.rearrange("(k t p) c -> t p k c", k=2, t=NT)[t]).then_inc(combine_in[t], 16)
                sp.wait_ge(arrived, 4)
                for s in layer_sems:
                    sp.sem_clear(s)
                for key in s_go:
                    sp.sem_inc(s_go[key], 1)
            for t in range(PT):
                sp.wait_ge(s_fin, t + 1)
                sp.dma_start(o[0][0, t * P:(t + 1) * P, :], x[:, t, :]).then_inc(s_out, 16)
            sp.wait_ge(s_fin, NT)
            sp.dma_start(o[1].rearrange("b t d -> (b t) d"), x[:, PT, :]).then_inc(s_out, 16)
            sp.wait_ge(s_out, 16 * NT)

        @block.gpsimd
        def _(pool):
            pool.dma_start(rope_t[:, :, :], a["rope"].rearrange("t p c -> p t c")).then_inc(s_rope, 16)
            for q, done in enumerate((*y_out, y_over)):
                pool.dma_start(yd[q * P:(q + 1) * P, 0:HD + ID], a["rope"][q]).then_inc(done, 16)
            pool.memset(ident[:, :], 0.0)
            pool.memset(tril[:, :], 1.0)
            pool.memset(quad[:, :, :], 0.0)
            pool.memset(pair[:, :, :], 0.0)
            pool.memset(own[:, :], 1.0)
            pool.memset(half, -0.5)
            pool.memset(over_sum, 0.0)
            pool.memset(mb[:, 0:P], 0.0).then_inc(s_pool, 1)
            pool.wait_ge(s_pool, 1)
            pool.affine_select(out=ident[:, :], in_=ident[:, :], compare_op=ALU.not_equal, fill=1.0,
                               base=0, pattern=[[-1, P]], channel_multiplier=1)
            pool.affine_select(out=tril[:, :], in_=tril[:, :], compare_op=ALU.is_ge, fill=0.0,
                               base=0, pattern=[[-1, P]], channel_multiplier=1)
            pool.affine_select(out=own[:, :], in_=own[:, :], compare_op=ALU.is_ge, fill=0.0,
                               base=0, pattern=[[-FRAMES, STREAMS]], channel_multiplier=1).then_inc(s_pool, 1)
            pool.wait_ge(s_pool, 2)
            pool.affine_select(out=own[:, :], in_=own[:, :], compare_op=ALU.is_ge, fill=0.0,
                               base=FRAMES - 1, pattern=[[FRAMES, STREAMS]], channel_multiplier=-1)
            for b in range(STREAMS):
                q = slice(FRAMES * b, FRAMES * (b + 1))
                pool.memset(quad[32 * (b % 4):32 * (b % 4) + 32, b // 4, q], 1.0).then_inc(s_pool, 1)
                pool.wait_ge(s_pool, 3 + 2 * b)
                pool.memset(pair[64 * (b % 2):64 * (b % 2) + 64, b // 2, q], 1.0).then_inc(s_pool, 1)
                pool.wait_ge(s_pool, 4 + 2 * b)
            pool.drain().then_inc(s_const, 1)

            def power(dst, src, scale, ready, n, out_sem):
                pool.wait_ge(ready, n)
                pool.tensor_scalar(dst, src, scale, EPS, ALU.mult, ALU.add).then_inc(s_pool, 1)
                pool.wait_ge(s_pool, 1)
                pool.sem_clear(s_pool)
                pool.tensor_tensor(dst, dst, half, ALU.pow).then_inc(out_sem, 1)

            pool.sem_clear(s_pool)
            with pool.Fori(0, DEPTH) as L:
                pool.dma_start(gain[:, 0, :], a["norm1"][L].rearrange("(p k) -> p k", k=KD)).then_inc(params, 16)
                pool.dma_start(gain[:, 1, :], a["norm2"][L].rearrange("(p k) -> p k", k=KD)).then_inc(params, 16)
                power(rs, ss, 1.0 / D, ss_ready, 1, rs_ready)
                pool.dma_start(rbias[:, 0:NG], a["b_rg"][L].partition_broadcast(P)).then_inc(params, 16)
                pool.dma_start(rbias[:, NG:], a["b_re"][L].partition_broadcast(P)).then_inc(params, 16)
                pool.dma_start(sbias[:, 0, :], a["sgu_b"][L].rearrange("g i -> i g")).then_inc(params, 16)
                for b in range(STREAMS):
                    q = slice(FRAMES * b, FRAMES * (b + 1))
                    pool.dma_start(sbias[q, 1, :], a["sgu_b"][L][:, 0:FRAMES].rearrange("g i -> i g")).then_inc(params, 16)
                    pool.dma_start(corner[q, :, :], a["sgu_w"][L][:, 0:FRAMES, 0:FRAMES].rearrange("g i j -> i g j")).then_inc(params, 16)
                for t in range(NT):
                    pool.wait_ge(rope_done, t + 1)
                    for c0, w, n in ((K0, P, 0), (V0, P, 1), (KI0, ID, 2)):
                        if t < PT:
                            dst = o[2 + n][L][0, t * P:(t + 1) * P]
                            dst = dst if n == 2 else dst.rearrange("t g d -> t (g d)")
                        else:
                            dst = o[5 + n][L]
                            dst = dst.rearrange("b t d -> (b t) d") if n == 2 else dst.rearrange("b t g d -> (b t) (g d)")
                        pool.dma_start(dst, qkv[:, t, c0:c0 + w]).then_inc(kv_out, 16)
                    dst = ki_rep[:, t * P:(t + 1) * P] if t < PT else kis_rep
                    if t == PT:
                        pool.tensor_copy(qis_rep[:, :, :, :],
                                         qkv[:, t, QI0:KI0].rearrange("p (h d) -> p h d", h=IH).unsqueeze(2).broadcast_to([P, IH, 4, ID]))
                    pool.tensor_copy(dst.rearrange("p (c d) -> p c d", c=4),
                                     over(qkv[:, t, KI0:KI0 + ID], 4, 1, [P, 4, ID])).then_inc(rep_done, 1)
                pool.dma_start(ln_g, a["sgu_ln_g"][L].partition_broadcast(P)).then_inc(ln_loaded, 16)
                pool.dma_start(ln_b, a["sgu_ln_b"][L].partition_broadcast(P)).then_inc(ln_loaded, 16)
                pool.wait_ge(qk_psum, 1 + GQ)
                for g in range(KV):
                    if g:
                        power(lrs, moments[:, :, 1], 1.0, ln_stat, 1, ln_rs)
                        pool.wait_ge(ln_done, NT)
                        pool.dma_start(o[8][L].rearrange("b t c -> (b t) c"), uv[:, 1, PT, :]).then_inc(sguv_out, 16)
                        pool.wait_ge(ks_psum, 4)
                    q = qkv[:, PT, 0:512].rearrange("p (j g d) -> p j g d", g=KV, j=GQ)[:, :, g, :]
                    c0 = K0 + HD * g
                    pool.tensor_copy(qkv[:, 0:GQ, Q_REP:Q_REP + P].rearrange("p j (c d) -> p j c d", c=2),
                                     q.unsqueeze(2).broadcast_to([P, GQ, 2, HD]))
                    pool.tensor_copy(ks_rep[g].rearrange("p (c d) -> p c d", c=2),
                                     over(qkv[:, PT, c0:c0 + HD], 2, 1, [P, 2, HD])).then_inc(rep_done, 1)
                pool.wait_ge(kv_out, 48 * NT * L + 48 * NT)
                pool.wait_ge(sguv_out, 16 * L + 16)
                pool.sem_inc(rows_sent, 1)
                pool.wait_ge(s_psum, NAU)
                pool.dma_start(wr[:, :, 0:NG], a["w_rg"][L].rearrange("(p k) c -> p k c", k=KD)).then_inc(wr_loaded, 16)
                pool.dma_start(wr[:, :, NG:], a["w_re"][L].rearrange("(p k) c -> p k c", k=KD)).then_inc(wr_loaded, 16)
                pool.dma_start(ids, a["ids"]).then_inc(wr_loaded, 16)
                power(rs, ss, 1.0 / D, ss_ready, 2, rs_ready)
                pool.wait_ge(table_ready, 1)
                pool.wait_ge(xd_out, 16 * NT)
                pool.wait_ge(r_psum, 1)

                def gather(b, q, landed_sem):
                    pool.tensor_copy(now[0][q], table[:, 0, bass.ds(b, 1)]).then_inc(s_pool, 1)
                    pool.wait_ge(s_pool, 1)
                    pool.sem_clear(s_pool)
                    pool.indirect_dma_start(out=xin[q], out_offset=None, in_=xd,
                                            in_offset=bass.IndirectOffsetOnAxis(ap=now[0][q], axis=0),
                                            bounds_check=ROWS - 1, oob_is_err=False).then_inc(landed_sem, 16)

                def scatter(b, q, z, sent_sem):
                    pool.tensor_copy(now[1][q], table[:, 1, bass.ds(b, 1)]).then_inc(s_pool, 1)
                    pool.wait_ge(s_pool, 1)
                    pool.sem_clear(s_pool)
                    pool.indirect_dma_start(out=yd, in_=yout[z], in_offset=None,
                                            out_offset=bass.IndirectOffsetOnAxis(ap=now[1][q], axis=0),
                                            bounds_check=2 * ROWS - 1, oob_is_err=False).then_inc(sent_sem, 16)

                def turn_rows(i, last):
                    for q in range(SLOTS):
                        b = SLOTS * i + q
                        if not last or q + AHEAD < SLOTS:
                            pool.wait_ge(xin_psum, b + 1)
                            gather(b + AHEAD, (q + AHEAD) % SLOTS, x_in[(q + AHEAD) % SLOTS])
                        pool.wait_ge(y_ready, b + 3)
                        scatter(b, q, q % YBUF, y_out[q % YBUF])

                for b in range(AHEAD):
                    gather(b, b, x_in[b])
                with pool.Fori(0, TURNS - 1) as i:
                    turn_rows(i, False)
                turn_rows(TURNS - 1, True)
                with pool.If(pool.value_load(over_count[:, 0:1], min_val=0, max_val=OVER) != 0):
                    with pool.Fori(0, OVER) as v:
                        pool.wait_ge(xin_psum, v + (EXPERTS + 1))
                        gather(v + EXPERTS, 0, x_over)
                        pool.wait_ge(y_ready, v + (EXPERTS + 3))
                        scatter(v + EXPERTS, 0, 0, y_over)
                next_layer(pool, "pool")
            pool.dma_start(fin_gain, a["final_norm"].partition_broadcast(P)).then_inc(s_rope, 16)
            power(rs, ss, 1.0 / D, s_fin_ss, 1, s_fin_rs)

        @block.tensor
        def _(pe):
            pe.wait_ge(s_const, 1)
            idm = ident[:, :]

            def norm_transposes(phase):
                for t in range(NT):
                    pe.wait_ge(xn_ready, NT * phase + t + 1)
                    for hf in range(2):
                        n = 2 * t + hf
                        if n >= 4:
                            pe.wait_ge(xt_done, 2 * NT * phase + n - 3)
                        for k in range(4):
                            mm = pe.transpose(banks[n % 4][:, k * P:(k + 1) * P],
                                              (xn2[t] if phase else xn[t % 2])[:, 4 * hf + k:D:KD], idm)
                        mm.then_inc(xt_psum, 1)

            with pe.Fori(0, DEPTH) as L:
                def unit(u):
                    return ring[:, u % SLOTS, :]

                def wait_unit(u):
                    pe.wait_ge(slot[u % SLOTS], landed(u))

                def project(u, t, out, w=BLK):
                    rhs = unit(u)[:, 0:KD * w].rearrange("p (k c) -> p k c", k=KD)
                    for k in range(KD):
                        mm = pe.matmul(out, xt[:, k, t * P:(t + 1) * P], rhs[:, k, :],
                                       start=(k == 0), stop=(k == KD - 1))
                    return mm

                jobs = [(u, t) for u in (QU, KU, IU, UU, VU) for t in range(NT)]

                def proj_job(n):
                    u, t = jobs[n]
                    if t == 0:
                        wait_unit(u)
                    if u == QU:
                        pe.wait_ge(xt_done, 2 * t + 2)
                    if n >= 4:
                        pe.wait_ge(proj_free, n - 3)
                    w = QKV_W - KI0 if u == IU else BLK
                    mm = project(u, t, banks[4 + n % 4][:, 0:w], w)
                    mm.then_inc(proj_psum, 1)
                    if t == NT - 1 and u != IU:
                        pe.drain().then_inc(unit_done, 1)

                norm_transposes(0)
                for n in range(3 * NT):
                    proj_job(n)
                pe.wait_ge(xt_done, 2 * NT)
                kidx = unit(IU)[:, 512:1024].rearrange("p (h s c) -> p h s c", h=2, s=2)
                for s in range(2):
                    for h in range(2):
                        mm = pe.transpose(banks[0][:, 256 * s + 128 * h:256 * s + 128 * h + 128],
                                          kidx[:, h, s, :], idm)
                mm.then_inc(kx_psum, 1)
                pe.drain().then_inc(unit_done, 1)
                for n in range(3 * NT, 4 * NT):
                    proj_job(n)
                pe.wait_ge(rope_done, NT)
                pe.wait_ge(rep_done, NT)
                for t in range(PT):
                    mm = pe.transpose(banks[1][:, t * P:(t + 1) * P],
                                      ki_rep[:, t * P:(t + 1) * P], idm)
                mm.then_inc(kx_psum, 1)
                for j in range(2):
                    for t in range(PT):
                        mm = pe.transpose(banks[2 + j][:, t * P:(t + 1) * P],
                                          qkv[:, t, QI0 + P * j:QI0 + P * (j + 1)], idm)
                    mm.then_inc(kx_psum, 1)
                pe.wait_ge(kx_done, 1)
                pe.transpose(banks[0][:, 0:P], kis_rep, idm).then_inc(kx_psum, 1)
                for j in range(2):
                    pe.wait_ge(kx_done, 2 + j)
                    for h in range(4):
                        mm = pe.transpose(banks[1 + j][:, h * P:(h + 1) * P],
                                          qis_rep[:, 4 * j + h, :, :].rearrange("p c d -> p (c d)"), idm)
                    mm.then_inc(kx_psum, 1)
                pe.wait_ge(kx_done, 5)
                pe.wait_ge(qis_done, 2)
                for at, t in enumerate(IDX_TILES):
                    for h in range(IH):
                        m = IH * at + h
                        if m >= 4:
                            pe.wait_ge(idx_relu, m - 3)
                        out = banks[m % 4][:, 0:KEYS[t]]
                        if t < PT:
                            r = slice(ID * (h % 4), ID * (h % 4) + ID)
                            mm = pe.matmul(out, qit[r, h // 4, t * P:(t + 1) * P], kit[r, 0:KEYS[t]],
                                           start=True, stop=True)
                        else:
                            for s in range(2):
                                mm = pe.matmul(out, qis[:, s, h, :], kis[:, s, :], start=(s == 0), stop=(s == 1))
                        mm.then_inc(idx_psum, 1)
                    if at == 0:
                        for n in range(4 * NT, 5 * NT):
                            proj_job(n)
                pe.wait_ge(idx_relu, IH * len(IDX_TILES))
                for t in range(PT):
                    mm = pe.transpose(banks[0][:, t * P:(t + 1) * P], qkv[:, t, K0:K0 + P], idm)
                mm.then_inc(qk_psum, 1)
                pe.wait_ge(proj_free, 5 * NT)
                for j in range(GQ):
                    for t in range(PT):
                        mm = pe.transpose(banks[4 + j][:, t * P:(t + 1) * P], qkv[:, t, j * P:(j + 1) * P], idm)
                    mm.then_inc(qk_psum, 1)
                pe.wait_ge(qk_done, 1 + GQ)

                def stream_layout(g):
                    kc = unit(KCU)[:, 0:2048].rearrange("p (h g s c) -> p h g s c", h=2, g=KV, s=4)
                    for s2 in range(2):
                        if g:
                            pe.wait_ge(ks_done, 3)
                            pe.wait_ge(qts_done, 1)
                        for s in range(2):
                            for h in range(2):
                                mm = pe.transpose(banks[6 + s2][:, 256 * s + 128 * h:256 * s + 128 * h + 128],
                                                  kc[:, h, g, 2 * s2 + s, :], idm)
                        mm.then_inc(ks_psum, 1)
                    pe.wait_ge(ks_done, 3 * g + 1)
                    pe.wait_ge(rep_done, NT + 1 + g)
                    pe.transpose(banks[6][:, 0:P], ks_rep[g], idm).then_inc(ks_psum, 1)
                    pe.wait_ge(ks_done, 3 * g + 2)
                    for j in range(GQ):
                        mm = pe.transpose(banks[7][:, j * P:(j + 1) * P], qkv[:, j, Q_REP:Q_REP + P], idm)
                    mm.then_inc(ks_psum, 1)
                    if g:
                        pe.drain().then_inc(unit_done, 1)
                    pe.wait_ge(ks_done, 3 * g + 3)
                    pe.wait_ge(qts_done, g + 1)

                def logits(n):
                    t, j, g = ATT_UNITS[n]
                    if n in PREP_AT:
                        if g == 0:
                            wait_unit(KCU)
                        stream_layout(g)
                    out = banks[n % 2][:, 0:KEYS[t]]
                    if t < PT:
                        r = slice(HD * g, HD * g + HD)
                        mm = pe.matmul(out, qt[r, j, t * P:(t + 1) * P], kt[r, 0:KEYS[t]], start=True, stop=True)
                    else:
                        for s in range(4):
                            mm = pe.matmul(out, qts[:, s, j, :], qkv[:, s, 0:KEYS[t]], start=(s == 0), stop=(s == 3))
                    mm.then_inc(s_psum, 1)

                def probs_transposes(n):
                    t, j, g = ATT_UNITS[n]
                    pe.wait_ge(p_ready, n + 1)
                    if n >= 2:
                        pe.wait_ge(pt_done, n - 1)
                    blocks = range(t + 1) if t < PT else (0, 1, 3)
                    for i, c in enumerate(blocks):
                        mm = pe.transpose(banks[2 + n % 2][:, i * P:(i + 1) * P],
                                          probs[n % 2][:, c * P:(c + 1) * P], idm)
                    mm.then_inc(pt_psum, 1)

                def values(n):
                    t, j, g = ATT_UNITS[n]
                    pe.wait_ge(pt_done, n + 1)
                    if t >= 2 and (j, g) == (0, 0):
                        pe.wait_ge(o_done, t - 1)
                    o_b = banks[4 + t % 2]
                    v = slice(V0 + HD * g, V0 + HD * g + HD)
                    r = slice(HD * g, HD * g + HD)
                    pt = probs_t[n % 2]
                    if t < PT:
                        for c in range(t + 1):
                            mm = pe.matmul(o_b[r, j * P:(j + 1) * P], qkv[:, c, v], pt[:, c * P:(c + 1) * P],
                                           start=(c == 0), stop=(c == t))
                    else:
                        if n == NPU:
                            wait_unit(VCU)
                        vc = unit(VCU)[:, 0:2048].rearrange("p (b t c) -> p b t c", b=STREAMS, t=2)
                        pe.matmul(o_b[r, j * P:(j + 1) * P], qkv[:, PT, v], pt[:, 2 * P:3 * P], start=True, stop=False)
                        for b in range(STREAMS):
                            for h in range(2):
                                q0 = FRAMES * b
                                mm = pe.matmul(o_b[r, j * P + q0:j * P + q0 + FRAMES], vc[:, b, h, r],
                                               pt[:, h * P + q0:h * P + q0 + FRAMES], start=False,
                                               stop=(b == STREAMS - 1 and h == 1))
                    mm.then_inc(pv_done, 1)
                    if n == NAU - 1 or ATT_UNITS[n + 1][0] != t:
                        pe.drain().then_inc(o_psum, 1)

                logits(0)
                logits(1)
                for n in range(NAU):
                    probs_transposes(n)
                    if n + 2 < NAU:
                        logits(n + 2)
                    if n >= 1:
                        values(n - 1)
                values(NAU - 1)
                pe.drain().then_inc(unit_done, 1)

                for m in range(2):
                    pe.wait_ge(swm_ready, m + 1)
                    if m == 0:
                        src = unit(SU)[:, 0:512]
                    else:
                        src = unit(SU)[:, 1024:1536]
                    for g in range(SG):
                        mm = pe.transpose(banks[6 + m][:, g * P:(g + 1) * P], src[:, g * P:(g + 1) * P], idm)
                    mm.then_inc(sw_psum, 1)
                pe.drain().then_inc(unit_done, 1)
                pe.wait_ge(sw_done, 2)
                for t in range(NT):
                    pe.wait_ge(ln_done, t + 1)
                    if t == 4:
                        pe.wait_ge(sg_used, 1)
                    for g in range(SG):
                        mm = pe.matmul(banks[t % 4][:, g * P:(g + 1) * P], sgw_t[t // PT][:, g, :],
                                       uv[:, 1, t, g * P:(g + 1) * P], start=True, stop=True)
                    mm.then_inc(sg_psum, 1)
                pe.wait_ge(o_done, NT)
                for t in range(NT):
                    pe.wait_ge(sg_used, t + 1)
                    if t == 4:
                        pe.wait_ge(sgt_done, 1)
                    for g in range(SG):
                        mm = pe.transpose(banks[4 + t % 4][:, g * P:(g + 1) * P], uv[:, 0, t, g * P:(g + 1) * P], idm)
                    mm.then_inc(sgt_psum, 1)

                pe.wait_ge(sgt_done, NT)
                for n in range(2 * NT):
                    c, t = divmod(n, NT)
                    b = banks[4 * (n % 2):4 * (n % 2) + 4]
                    if n >= 2:
                        pe.wait_ge(mg_done, n - 1)
                    if t == 0:
                        wait_unit(GAU[c])
                        wait_unit(GBU[c])
                    project(GAU[c], t, b[0][:, :])
                    project(GBU[c], t, b[1][:, :]).then_inc(mg_gate, 1)
                    if t == 0:
                        wait_unit(PABU[c])
                    w = unit(PABU[c]).rearrange("p (n c) -> p n c", n=8)
                    for half_, src in ((0, att), (1, sgt)):
                        for j in range(4):
                            mm = pe.matmul(b[2 + half_][:, :], src[:, j, t * P:(t + 1) * P], w[:, 4 * half_ + j, :],
                                           start=(j == 0), stop=(j == 3))
                    mm.then_inc(mg_proj, 1)
                    if t == NT - 1:
                        pe.drain().then_inc(unit_done, 3)
                pe.wait_ge(mg_done, 2 * NT)
                for n in range(2 * NT):
                    t, hf = divmod(n, 2)
                    if n >= 4:
                        pe.wait_ge(mt_done, n - 3)
                    for k in range(4):
                        mm = pe.transpose(banks[n % 4][:, k * P:(k + 1) * P], uv[:, hf, t, k * P:(k + 1) * P], idm)
                    mm.then_inc(mt_psum, 1)
                for n in range(2 * NT):
                    c, t = divmod(n, NT)
                    if t == 0:
                        wait_unit(OUTU[c])
                    if c == 0:
                        pe.wait_ge(mt_done, 2 * t + 2)
                    if n >= 4:
                        pe.wait_ge(xo_done, n - 3)
                    project(OUTU[c], t, banks[4 + n % 4][:, :]).then_inc(xo_psum, 1)
                    if t == NT - 1:
                        pe.drain().then_inc(unit_done, 1)

                norm_transposes(1)
                pe.wait_ge(xt_done, 4 * NT)
                pe.wait_ge(xo_done, 2 * NT)
                pe.wait_ge(wr_loaded, 48 * L + 48)
                for t in range(NT):
                    for k in range(KD):
                        mm = pe.matmul(banks[4][:, 36 * t:36 * t + 36], xt[:, k, t * P:(t + 1) * P], wr[:, k, :],
                                       start=(k == 0), stop=(k == KD - 1))
                mm.then_inc(r_psum, 1)

                pe.wait_ge(chosen_ready, 1)
                pe.matmul(banks[5][:, 0:NT * EXPERTS], before, scr[:, P:P + NT * EXPERTS], start=True, stop=True)
                pe.matmul(banks[6][:, 0:NT * EXPERTS], ones, scr[:, P:P + NT * EXPERTS], start=True, stop=True).then_inc(count_psum, 1)
                pe.wait_ge(onehot_ready, 1)
                for m in range(2 * NT):
                    mm = pe.matmul(banks[5][0:BR, 0:COLS_T], onehot[:, m, 0:BR], onehot[:, m, BR:BR + COLS_T],
                                   start=(m == 0), stop=(m == 2 * NT - 1))
                mm.then_inc(table_psum, 1)
                pe.wait_ge(table_ready, 1)
                pe.drain().then_inc(xin_psum, 1)

                def rows_in(b, q):
                    for k in range(KD):
                        mm = pe.transpose(banks[k // 4][:, (k % 4) * BR:(k % 4 + 1) * BR],
                                          xin[q][:, k:D:KD], ident[0:BR, 0:BR])
                    mm.then_inc(xin_psum, 1)

                def up(b, q, z):
                    for m in range(2):
                        w = ring[:, q, 1024 * m:1024 * m + 1024].rearrange("p (k f) -> p k f", k=KD)
                        for k in range(KD):
                            mm = pe.matmul(banks[2 + z][:, BR * m:BR * m + BR], w[:, k, :], xin_t[z][:, k, :],
                                           start=(k == 0), stop=(k == KD - 1))
                    mm.then_inc(gu_psum, 1)

                def down(b, q, z):
                    pe.wait_ge(h_done, b + 3)
                    pe.wait_ge(y_ready, b + 1)
                    for c in range(2):
                        mm = pe.matmul(banks[4 + 2 * z + c][0:BR, :], hidden[z][:, :],
                                       ring[:, q, 2048 + BLK * c:2048 + BLK * c + BLK], start=True, stop=True)
                    mm.then_inc(y_psum, 1)

                def rows_step(i, q):
                    pe.wait_ge(x_in[q % SLOTS], 16 * TURNS * L + (16 * i + 16 * (q // SLOTS) + 16))
                    b = SLOTS * i + q
                    if not (isinstance(b, int) and b == 0):
                        pe.wait_ge(xin_ready, 2 * b)
                    rows_in(b, q % SLOTS)

                def up_step(i, q):
                    b, s_ = SLOTS * i + q, q % SLOTS
                    pe.wait_ge(slot[s_], 48 * i + (landed(12 + s_) + 48 * (q // SLOTS) + 48))
                    pe.wait_ge(xin_ready, 2 * b + 2)
                    pe.wait_ge(h_done, b + 1)
                    up(b, s_, q % 2)

                def down_step(i, q):
                    down(SLOTS * i + q, q % SLOTS, q % 2)

                rows_step(0, 0)
                rows_step(0, 1)
                up_step(0, 0)
                with pe.Fori(0, TURNS - 1) as i:
                    for q in range(1, SLOTS + 1):
                        rows_step(i, q + 1)
                        up_step(i, q)
                        down_step(i, q - 1)
                for q in range(1, SLOTS):
                    if q + 1 < SLOTS:
                        rows_step(TURNS - 1, q + 1)
                    up_step(TURNS - 1, q)
                    down_step(TURNS - 1, q - 1)
                down_step(TURNS - 1, SLOTS - 1)
                with pe.If(pe.value_load(over_count[:, 0:1], min_val=0, max_val=OVER) != 0):
                    gathered = earlier(pe)
                    with pe.Fori(0, OVER) as v:
                        b = v + EXPERTS
                        pe.wait_ge(x_over, gathered + (16 * v + 16))
                        pe.wait_ge(xin_ready, 2 * b)
                        rows_in(b, 0)
                        pe.wait_ge(over_w, 48 * v + 48)
                        pe.wait_ge(xin_ready, 2 * b + 2)
                        pe.wait_ge(h_done, b + 2)
                        up(b, 0, 0)
                        pe.wait_ge(y_ready, b + 2)
                        down(b, 0, 0)
                next_layer(pe, "pe")

        @block.scalar
        def _(act):
            with act.Fori(0, DEPTH) as L:
                def proj_out(n):
                    u, t = divmod(n, NT)
                    act.wait_ge(proj_psum, n + 1)
                    b = banks[4 + n % 4]
                    if u == 0:
                        ins = act.activation(qkv[:, t, 0:BLK].rearrange("p (j g d) -> p g j d", g=KV, j=GQ),
                                             b[:, :].rearrange("p (g j d) -> p g j d", g=KV, j=GQ), ACT.Copy)
                    elif u == 1:
                        ins = act.activation(qkv[:, t, BLK * u:BLK * u + BLK], b[:, :], ACT.Copy)
                    elif u == 2:
                        ins = act.activation(qkv[:, t, KI0:QKV_W], b[:, 0:QKV_W - KI0], ACT.Copy)
                    else:
                        ins = act.activation(uv[:, u - 3, t, :], b[:, :], ACT.Gelu_apprx_tanh)
                    ins.then_inc(proj_free, 1)

                for n in range(3 * NT):
                    proj_out(n)
                act.wait_ge(kx_psum, 1)
                act.activation(kis[:, :, 0:PAST], banks[0][:, :].rearrange("p (s k) -> p s k", s=2), ACT.Copy).then_inc(kx_done, 1)
                for n in range(3 * NT, 4 * NT):
                    proj_out(n)
                for i, dst in enumerate((kit, qit[:, 0, :], qit[:, 1, :])):
                    act.wait_ge(kx_psum, i + 2)
                    act.activation(dst, banks[1 + i][:, :], ACT.Copy).then_inc(kx_done, 1)
                act.wait_ge(kx_psum, 5)
                for c in range(4):
                    r = slice(ID * c, ID * c + ID)
                    src = banks[0][r, 0:P].rearrange("p (s q) -> p s q", s=2)[:, :, FRAMES * c:FRAMES * c + FRAMES]
                    ins = act.activation(kis[r, :, PAST:PAST + FRAMES], src, ACT.Copy)
                ins.then_inc(kx_done, 1)
                for at, t in enumerate(IDX_TILES):
                    for h in range(IH):
                        m = IH * at + h
                        act.wait_ge(idx_psum, m + 1)
                        if m >= 2:
                            act.wait_ge(idx_used, m - 1)
                        act.activation(relu_b[m % 2][:, 0:KEYS[t]], banks[m % 4][:, 0:KEYS[t]], ACT.Relu).then_inc(idx_relu, 1)
                    if at == 0:
                        for n in range(4 * NT, 5 * NT):
                            proj_out(n)
                for i, dst in enumerate([kt[:, :]] + [qt[:, j, :] for j in range(GQ)]):
                    act.wait_ge(qk_psum, i + 1)
                    act.activation(dst, banks[0 if i == 0 else 3 + i][:, :], ACT.Copy).then_inc(qk_done, 1)

                def stream_keys(g):
                    for s2 in range(2):
                        act.wait_ge(ks_psum, 4 * g + s2 + 1)
                        act.activation(qkv[:, 2 * s2:2 * s2 + 2, 0:PAST],
                                       banks[6 + s2][:, :].rearrange("p (s k) -> p s k", s=2), ACT.Copy).then_inc(ks_done, 1)
                    act.wait_ge(ks_psum, 4 * g + 3)
                    for c in range(2):
                        r = slice(HD * c, HD * c + HD)
                        src = banks[6][r, 0:P].rearrange("p (s q) -> p s q", s=4)[:, :, FRAMES * c:FRAMES * c + FRAMES]
                        ins = act.activation(qkv[r, 0:4, PAST:PAST + FRAMES], src, ACT.Copy)
                    ins.then_inc(ks_done, 1)

                def probs_out(n):
                    t = ATT_UNITS[n][0]
                    act.wait_ge(pt_psum, n + 1)
                    if n >= 2:
                        act.wait_ge(pv_done, n - 1)
                    w = KEYS[t] if t < PT else 3 * P
                    act.activation(probs_t[n % 2][:, 0:w], banks[2 + n % 2][:, 0:w], ACT.Copy).then_inc(pt_done, 1)

                def tile_out(t):
                    act.wait_ge(o_psum, t + 1)
                    act.activation(att[:, :, t * P:(t + 1) * P],
                                   banks[4 + t % 2][:, :].rearrange("p (j q) -> p j q", j=GQ), ACT.Copy).then_inc(o_done, 1)

                for n in range(NAU):
                    t = ATT_UNITS[n][0]
                    if n in PREP_AT:
                        stream_keys(PREP_AT[n])
                    act.wait_ge(p_raw, n + 1)
                    k = n % 2
                    act.activation(probs[k][:, 0:KEYS[t]], probs[k][:, 0:KEYS[t]], ACT.Exp,
                                   bias=nmx[:, k:k + 1], scale=ATT_SCALE, accum_out=den[:, k:k + 1]).then_inc(p_exp, 1)
                    if n >= 1:
                        probs_out(n - 1)
                    if n >= 2 and ATT_UNITS[n - 2][0] != ATT_UNITS[n - 1][0]:
                        tile_out(ATT_UNITS[n - 2][0])
                probs_out(NAU - 1)
                tile_out(PT)
                for m in range(2):
                    act.wait_ge(sw_psum, m + 1)
                    act.activation(scr[:, 512 * m:512 * m + 512], banks[6 + m][:, :], ACT.Copy).then_inc(sw_done, 1)
                for t in range(NT):
                    act.wait_ge(sgt_psum, t + 1)
                    act.activation(sgt[:, :, t * P:(t + 1) * P],
                                   banks[4 + t % 4][:, :].rearrange("p (g q) -> p g q", g=SG), ACT.Copy).then_inc(sgt_done, 1)
                for n in range(2 * NT):
                    act.wait_ge(mg_gate, n + 1)
                    if n >= 2:
                        act.wait_ge(mg_done, n - 1)
                    for m in range(2):
                        c0 = 1024 * (n % 2) + 512 * m
                        ins = act.activation(scr[:, c0:c0 + 512], banks[4 * (n % 2) + m][:, :], ACT.Sigmoid)
                    ins.then_inc(mg_sig, 1)
                for n in range(2 * NT):
                    t, hf = divmod(n, 2)
                    act.wait_ge(mt_psum, n + 1)
                    act.activation(xt[:, 4 * hf:4 * hf + 4, t * P:(t + 1) * P],
                                   banks[n % 4][:, :].rearrange("p (k q) -> p k q", k=4), ACT.Copy).then_inc(mt_done, 1)
                for m in range(2):
                    act.wait_ge(r_sub, m + 1)
                    v = (eg, e8)[m]
                    act.activation(v, v, ACT.Exp).then_inc(r_exp, 1)
                act.wait_ge(table_ready, 1)
                act.drain().then_inc(y_ready, 2)

                def silu(b, z):
                    act.wait_ge(gu_psum, b + 1)
                    act.activation(hidden[z], banks[2 + z][:, 0:BR], ACT.Silu).then_inc(silu_done, 1)

                def results(b, z):
                    act.wait_ge(y_psum, b + 1)
                    for c in range(2):
                        ins = act.activation(yout[z][:, BLK * c:BLK * c + BLK], banks[4 + 2 * z + c][0:BR, :], ACT.Copy)
                    ins.then_inc(y_ready, 1)

                def turn_out(i, last):
                    for q in range(SLOTS):
                        if not last or q + 1 < SLOTS:
                            silu(SLOTS * i + (q + 1), (q + 1) % 2)
                        act.wait_ge(y_out[q % YBUF], 16 * (EXPERTS // YBUF) * L + (32 * i + 16 * (q // YBUF) + 16))
                        results(SLOTS * i + q, q % 2)

                silu(0, 0)
                with act.Fori(0, TURNS - 1) as i:
                    turn_out(i, False)
                turn_out(TURNS - 1, True)
                with act.If(act.value_load(over_count[:, 0:1], min_val=0, max_val=OVER) != 0):
                    sent = earlier(act)
                    with act.Fori(0, OVER) as v:
                        silu(v + EXPERTS, 0)
                        act.wait_ge(y_out[0], 16 * (EXPERTS // YBUF) * L + (16 * (EXPERTS // YBUF) + 16))
                        act.sem_inc(over_free, 1)
                        act.wait_ge(y_over, sent + (16 * v + 16))
                        results(v + EXPERTS, 0)
                next_layer(act, "act")

        @block.vector
        def _(dve):
            V = nc.vector
            count = [0]

            def then(ins):
                count[0] += 1
                ins.then_inc(dve_chain, 1)
                dve.wait_ge(dve_chain, count[0])

            def square_sums(done):
                for t in range(NT):
                    then(V.tensor_tensor_reduce(out=xn[t % 2], in0=x[:, t, :], in1=x[:, t, :], scale=1.0, scalar=0.0,
                                                op0=ALU.mult, op1=ALU.add, accum_out=ss[:, t:t + 1]))
                V.nop().then_inc(done, 1)

            def norm(phase, L):
                square_sums(ss_ready)
                dve.wait_ge(rs_ready, phase + 1)
                if phase == 0:
                    dve.wait_ge(params, 16 * 21 * L + 16 * 21)

                def rows(t):
                    if phase == 0 and t >= 2:
                        dve.wait_ge(xt_psum, 2 * (t - 1))
                    V.tensor_scalar(xn2[t] if phase else xn[t % 2], x[:, t, :], rs[:, t:t + 1], None, ALU.mult).then_inc(xn_ready, 1)

                rows(0)
                rows(1)
                for t in range(NT):
                    for hf in range(2):
                        n = 2 * t + hf
                        dve.wait_ge(xt_psum, 2 * NT * phase + n + 1)
                        V.tensor_tensor(xt[:, 4 * hf:4 * hf + 4, t * P:(t + 1) * P],
                                        banks[n % 4][:, :].rearrange("p (k q) -> p k q", k=4),
                                        gain[:, phase, 4 * hf:4 * hf + 4].unsqueeze(2).broadcast_to([P, 4, P]),
                                        ALU.mult).then_inc(xt_done, 1)
                    if t + 2 < NT:
                        rows(t + 2)

            def rotate(t, c0, heads, d, table):
                h2 = d // 2
                src = qkv[:, t, c0:c0 + heads * d].rearrange("p (h a i) -> p h a i", a=2, i=h2)
                cos, sin = table[:, 0:h2], table[:, h2:d]
                w = heads * d
                t1 = scr[:, 0:w].rearrange("p (h a i) -> p h a i", a=2, i=h2)
                t2 = scr[:, 1024:1024 + w].rearrange("p (h a i) -> p h a i", a=2, i=h2)
                bc = [P, heads, h2]
                for z in range(2):
                    V.tensor_tensor(t1[:, :, z, :], src[:, :, z, :], over(cos, heads, 1, bc), ALU.mult)
                    ins = V.tensor_tensor(t2[:, :, z, :], src[:, :, 1 - z, :], over(sin, heads, 1, bc), ALU.mult)
                then(ins)
                V.tensor_tensor(src[:, :, 0, :], t1[:, :, 0, :], t2[:, :, 0, :], ALU.subtract)
                then(V.tensor_tensor(src[:, :, 1, :], t1[:, :, 1, :], t2[:, :, 1, :], ALU.add))

            def select(t):
                s = score(t)
                k = TOPK_P if t < PT else TOPK_S
                for r in range(-(-k // 8)):
                    then(V.max(best, s))
                    if k - 8 * r < 8:
                        then(V.memset(best[:, k - 8 * r:8], SEL))
                    then(V.match_replace(out=s, in_to_replace=best, in_values=s, imm_value=SEL))
                then(V.tensor_scalar(s, s, SEL, OFF, ALU.not_equal, ALU.mult))

            def dispatch(L):
                for t in range(NT):
                    ins = V.tensor_tensor(chosen[:, t, :].rearrange("p (g e) -> p g e", g=NG),
                                          over(w16e[:, t, 0:NE], NG, 1, [P, NG, NE]),
                                          hot[:, t, :].unsqueeze(2).broadcast_to([P, NG, NE]), ALU.mult)
                V.memset(ones, 1.0)
                then(V.tensor_scalar(before, tril[:, :], -1.0, 1.0, ALU.mult, ALU.add))
                V.nop().then_inc(chosen_ready, 1)
                dve.wait_ge(count_psum, 1)
                V.tensor_copy(total, banks[6][:, 0:NT * EXPERTS].rearrange("p (t e) -> p t e", t=NT))
                then(V.memset(base[:, 0, :], 0.0))
                for t in range(1, NT):
                    then(V.tensor_tensor(base[:, t, :], base[:, t - 1, :], total[:, t - 1, :], ALU.add))
                then(V.tensor_tensor(size, base[:, NT - 1, :], total[:, NT - 1, :], ALU.add))
                dve.wait_ge(wr_loaded, 48 * L + 48)
                then(V.tensor_scalar(need, size, float(BR), None, ALU.is_gt))
                for j in range(2, -(-ROWS // BR)):
                    then(V.scalar_tensor_tensor(need, size, float(BR * j), need, ALU.is_gt, ALU.add))
                src, dst, step = need, scan_a, 1
                while step < EXPERTS:
                    V.tensor_copy(dst[:, 0:step], src[:, 0:step])
                    then(V.tensor_tensor(dst[:, step:], src[:, step:], src[:, :EXPERTS - step], ALU.add))
                    src, dst, step = dst, (scan_b if dst is scan_a else scan_a), 2 * step
                V.tensor_copy(over_count, src[0:1, EXPERTS - 1:EXPERTS])
                V.tensor_scalar(over_new, src[0:1, EXPERTS - 1:EXPERTS], 0.0, 16.0 * OVER, ALU.is_gt, ALU.mult)
                then(V.tensor_copy(over_past, over_sum))
                V.tensor_tensor(over_sum, over_sum, over_new, ALU.add)
                then(V.tensor_tensor(start, src, need, ALU.subtract))
                then(V.tensor_tensor(begun, over(start[0:1, :], OVER, 1, [1, OVER, EXPERTS]),
                                     ids[0:1, 0:OVER].unsqueeze(2).broadcast_to([1, OVER, EXPERTS]), ALU.is_le))
                then(V.tensor_reduce(wide[0:1, 0, 0:OVER], begun, AX.X, ALU.add))
                then(V.tensor_scalar(over_expert, wide[0:1, 0, 0:OVER], -1.0, None, ALU.add))
                V.nop().then_inc(experts_known, 1)
                then(V.scalar_tensor_tensor(start, start, float(EXPERTS - 1), ids[:, 0:EXPERTS], ALU.add, ALU.subtract))
                then(V.tensor_tensor(rank, banks[5][:, 0:NT * EXPERTS].rearrange("p (t e) -> p t e", t=NT), base, ALU.add))
                then(V.tensor_scalar(whole, rank, float(BR), None, ALU.is_ge))
                for j in range(2, -(-ROWS // BR)):
                    then(V.scalar_tensor_tensor(whole, rank, float(BR * j), whole, ALU.is_ge, ALU.add))
                then(V.scalar_tensor_tensor(block_of, rank, float(BR), over(start, NT, 1, [P, NT, EXPERTS]),
                                            ALU.is_ge, ALU.mult))
                then(V.tensor_tensor(block_of, block_of, whole, ALU.add))
                V.tensor_tensor(block_of, block_of, over(ids[:, 0:EXPERTS], NT, 1, [P, NT, EXPERTS]), ALU.add)
                then(V.scalar_tensor_tensor(place, whole, -float(BR), rank, ALU.mult, ALU.add))
                then(V.scalar_tensor_tensor(code, block_of, float(BR), place, ALU.mult, ALU.add))
                then(V.scalar_tensor_tensor(code, code, 1.0, chosen, ALU.add, ALU.mult))
                V.tensor_reduce(code_k[:, 0, :], code, AX.X, ALU.max)
                then(V.tensor_reduce(code_k[:, 1, :], code, AX.X, ALU.add))
                then(V.tensor_tensor(code_k[:, 1, :], code_k[:, 1, :], code_k[:, 0, :], ALU.subtract))
                for k in range(2):
                    then(V.tensor_tensor(equal, code, code_k[:, k, :].unsqueeze(2).broadcast_to([P, NT, EXPERTS]), ALU.is_equal))
                    for w, what in enumerate((place, block_of, gate)):
                        then(V.tensor_tensor(part, equal, what, ALU.mult))
                        then(V.tensor_reduce(pair_at[:, w, k, :], part, AX.X, ALU.add))
                for m in range(2 * NT):
                    k, t = divmod(m, NT)
                    V.tensor_scalar(onehot[:, m, 0:BR], ids[:, 0:BR], pair_at[:, 0, k, t:t + 1], None, ALU.is_equal)
                    ins = V.tensor_scalar(onehot[:, m, BR:BR + COLS_T], ids[:, 0:COLS_T], pair_at[:, 1, k, t:t + 1],
                                          ids[:, BR + m:BR + m + 1], ALU.is_equal, ALU.mult)
                then(ins)
                V.nop().then_inc(onehot_ready, 1)
                dve.wait_ge(table_psum, 1)
                pair_1 = banks[5][0:BR, 0:COLS_T]
                then(V.tensor_scalar(pads, pair_1, 0.0, NOWHERE, ALU.is_equal, ALU.mult))
                then(V.scalar_tensor_tensor(wide[:, 1, :], pair_1, -1.0, pads, ALU.add, ALU.add))
                then(V.tensor_scalar(wide[:, 0, :], wide[:, 1, :], float(ROWS), -float(ROWS), ALU.is_ge, ALU.mult))
                then(V.tensor_tensor(wide[:, 0, :], wide[:, 0, :], wide[:, 1, :], ALU.add))
                then(V.tensor_copy(table, wide))
                V.nop().then_inc(h_done, 2)
                V.nop().then_inc(table_ready, 1)

            dve.wait_ge(s_const, 1)
            dve.wait_ge(s_rope, 16)
            dve.wait_ge(s_x, 16 * NT)
            with dve.Fori(0, DEPTH) as L:
                count[0] = 0
                norm(0, L)
                for t in range(NT):
                    dve.wait_ge(proj_free, 2 * NT + t + 1)
                    dve.wait_ge(xt_psum, 2 * NT)
                    k_all = HEADS + KV
                    rotate(t, 0, k_all, HD, rope_t[:, t, 0:HD])
                    rotate(t, QI0, IH + 1, ID, rope_t[:, t, HD:HD + ID])
                    V.tensor_scalar(qkv[:, t, WI0:QKV_W], qkv[:, t, WI0:QKV_W], IH ** -0.5, None,
                                    ALU.mult).then_inc(rope_done, 1)
                for j in range(2):
                    dve.wait_ge(kx_psum, 6 + j)
                    for s in range(2):
                        ins = V.tensor_tensor(qis[:, s, 4 * j:4 * j + 4, :],
                                              banks[1 + j][:, :].rearrange("p (h q) -> p h q", h=4),
                                              over(quad[:, s, :], 4, 1, [P, 4, P]), ALU.mult)
                    ins.then_inc(qis_done, 1)
                V.memset(score(0)[:, :], 0.0).then_inc(dve_chain, 1)
                count[0] += 1
                dve.wait_ge(dve_chain, count[0])
                then(V.memset(score(0)[0:64, 64:P], OFF))
                dve.wait_ge(rope_done, NT)
                for at, t in enumerate(IDX_TILES):
                    s = score(t)
                    for h in range(IH):
                        m = IH * at + h
                        dve.wait_ge(idx_relu, m + 1)
                        w = qkv[:, t, WI0 + h:WI0 + h + 1]
                        r = relu_b[m % 2][:, 0:KEYS[t]]
                        if h == 0:
                            ins = V.tensor_scalar(s, r, w, None, ALU.mult)
                        else:
                            ins = V.scalar_tensor_tensor(s, r, w, s, ALU.mult, ALU.add)
                        ins.then_inc(idx_used, 1)
                        dve.wait_ge(idx_used, m + 1)
                    if t < PT:
                        then(V.memset(s[0:64, KEYS[t] - 64:KEYS[t]], NEG))
                    select(t)

                dve.wait_ge(proj_free, 5 * NT)
                for t in range(NT):
                    then(V.bn_stats(bns, uv[:, 1, t, :]))
                    then(V.bn_aggr(moments[:, t, :], bns))
                V.nop().then_inc(ln_stat, 1)
                dve.wait_ge(ln_rs, 1)
                dve.wait_ge(ln_loaded, 32 * L + 32)
                for t in range(NT):
                    v = uv[:, 1, t, :]
                    then(V.tensor_scalar(v, v, moments[:, t, 0:1], lrs[:, t:t + 1], ALU.subtract, ALU.mult))
                    then(V.tensor_tensor(v, v, ln_g, ALU.mult))
                    V.tensor_tensor(v, v, ln_b, ALU.add).then_inc(ln_done, 1)
                dve.wait_ge(ln_done, NT)

                def masked_logits(n):
                    t = ATT_UNITS[n][0]
                    if n in PREP_AT:
                        g = PREP_AT[n]
                        dve.wait_ge(ks_psum, 4 * g + 4)
                        for s in range(4):
                            ins = V.tensor_tensor(qts[:, s, :, :], banks[7][:, :].rearrange("p (j q) -> p j q", j=GQ),
                                                  over(pair[:, s, :], GQ, 1, [P, GQ, P]), ALU.mult)
                        ins.then_inc(qts_done, 1)
                    k = n % 2
                    dve.wait_ge(s_psum, n + 1)
                    if n >= 2:
                        dve.wait_ge(pt_psum, n - 1)
                    then(V.tensor_tensor_reduce(out=probs[k][:, 0:KEYS[t]], in0=banks[n % 2][:, 0:KEYS[t]], in1=score(t),
                                                scale=1.0, scalar=NEG, op0=ALU.add, op1=ALU.max,
                                                accum_out=mx[:, k:k + 1]))
                    V.tensor_scalar(nmx[:, k:k + 1], mx[:, k:k + 1], -ATT_SCALE, None, ALU.mult).then_inc(p_raw, 1)

                def normalise(n):
                    t = ATT_UNITS[n][0]
                    k = n % 2
                    p = probs[k][:, 0:KEYS[t]]
                    dve.wait_ge(p_exp, n + 1)
                    then(V.reciprocal(rden[:, k:k + 1], den[:, k:k + 1]))
                    ins = V.tensor_scalar(p, p, rden[:, k:k + 1], None, ALU.mult)
                    if t == PT:
                        then(ins)
                        ins = V.tensor_tensor(probs[k][:, 3 * P:4 * P].rearrange("p (b i) -> p b i", b=STREAMS),
                                              over(p[:, PAST:PAST + FRAMES], STREAMS, 1, [P, STREAMS, FRAMES]),
                                              own[:, :].unsqueeze(2).broadcast_to([P, STREAMS, FRAMES]), ALU.mult)
                    ins.then_inc(p_ready, 1)

                masked_logits(0)
                for n in range(NAU):
                    if n + 1 < NAU and n + 1 not in PREP_AT:
                        masked_logits(n + 1)
                    normalise(n)
                    if n + 1 in PREP_AT:
                        masked_logits(n + 1)

                dve.wait_ge(slot[SU % SLOTS], landed(SU))
                sw = ring[:, SU % SLOTS, :]
                w4 = sw[:, 0:512].rearrange("p (g j) -> p g j", g=SG)
                low = over(tril[:, :], SG, 1, [P, SG, P])
                V.tensor_tensor(w4, w4, low, ALU.mult).then_inc(swm_ready, 1)
                ws = sw[:, 1024:1536].rearrange("p (g b j) -> p g b j", g=SG, b=STREAMS)
                for g in range(SG):
                    ins = V.tensor_tensor(ws[:, g, :, :], over(corner[:, g, :], STREAMS, 1, [P, STREAMS, FRAMES]),
                                          own[:, :].unsqueeze(2).broadcast_to([P, STREAMS, FRAMES]), ALU.mult)
                then(ins)
                ws4 = sw[:, 1024:1536].rearrange("p (g j) -> p g j", g=SG)
                V.tensor_tensor(ws4, ws4, low, ALU.mult).then_inc(swm_ready, 1)
                for t in range(NT):
                    dve.wait_ge(sg_psum, t + 1)
                    for g in range(SG):
                        u = uv[:, 0, t, g * P:(g + 1) * P]
                        ins = V.scalar_tensor_tensor(u, banks[t % 4][:, g * P:(g + 1) * P],
                                                     sbias[:, t // PT, g:g + 1], u, ALU.add, ALU.mult)
                    ins.then_inc(sg_used, 1)
                for n in range(2 * NT):
                    c, t = divmod(n, NT)
                    dve.wait_ge(mg_sig, n + 1)
                    dve.wait_ge(mg_proj, n + 1)
                    b = banks[4 * (n % 2):4 * (n % 2) + 4]
                    t1 = scr[:, 1024 * (n % 2):1024 * (n % 2) + 512]
                    t2 = scr[:, 1024 * (n % 2) + 512:1024 * (n % 2) + 1024]
                    V.tensor_tensor(t1, t1, b[2][:, :], ALU.mult)
                    then(V.tensor_tensor(t2, t2, b[3][:, :], ALU.mult))
                    if n == 2 * NT - 1:
                        dve.wait_ge(rows_sent, 1)
                    V.tensor_tensor(uv[:, c, t, :], t1, t2, ALU.add).then_inc(mg_done, 1)
                for n in range(2 * NT):
                    c, t = divmod(n, NT)
                    dve.wait_ge(xo_psum, n + 1)
                    xs = x[:, t, BLK * c:BLK * c + BLK]
                    V.tensor_tensor(xs, xs, banks[4 + n % 4][:, :], ALU.add).then_inc(xo_done, 1)
                dve.wait_ge(xo_done, 2 * NT)
                norm(1, L)

                dve.wait_ge(r_psum, 1)
                then(V.tensor_tensor(logit, banks[4][:, 0:36 * NT].rearrange("p (t c) -> p t c", t=NT),
                                     over(rbias[:, :], NT, 1, [P, NT, 36]), ALU.add))
                for w_, r_ in ((w16, r8), (w16e, r8e)):
                    V.memset(w_, NEG)
                    then(V.memset(r_, NEG))
                then(V.tensor_copy(w16[:, :, 0:NG], logit[:, :, 0:NG]))
                for t in range(NT):
                    ins = V.max(m8[:, t, :], w16[:, t, :])
                then(ins)
                V.tensor_tensor(eg, logit[:, :, 0:NG], m8[:, :, 0:1].broadcast_to([P, NT, NG]),
                                ALU.subtract).then_inc(r_sub, 1)
                then(V.tensor_copy(r8[:, :, 0:1], m8[:, :, 0:1]))
                for t in range(NT):
                    ins = V.match_replace(out=w16[:, t, :], in_to_replace=r8[:, t, :], in_values=w16[:, t, :], imm_value=SEL)
                then(ins)
                then(V.tensor_scalar(hot, w16[:, :, 0:NG], SEL, None, ALU.is_equal))
                for t in range(NT):
                    ins = V.tensor_tensor(picked[:, t, :, :], logit[:, t, NG:].rearrange("p (g e) -> p g e", g=NG),
                                          hot[:, t, :].unsqueeze(2).broadcast_to([P, NG, NE]), ALU.mult)
                then(ins)
                then(V.tensor_reduce(l8, picked.rearrange("p t g e -> p t e g"), AX.X, ALU.add))
                then(V.tensor_copy(w16e[:, :, 0:NE], l8))
                for t in range(NT):
                    ins = V.max(m8e[:, t, :], w16e[:, t, :])
                then(ins)
                V.tensor_tensor(e8, l8, m8e[:, :, 0:1].broadcast_to([P, NT, NE]), ALU.subtract).then_inc(r_sub, 1)
                then(V.tensor_copy(r8e[:, :, 0:2], m8e[:, :, 0:2]))
                for t in range(NT):
                    ins = V.match_replace(out=w16e[:, t, :], in_to_replace=r8e[:, t, :], in_values=w16e[:, t, :], imm_value=SEL)
                then(ins)
                then(V.tensor_scalar(w16e[:, :, 0:NE], w16e[:, :, 0:NE], SEL, None, ALU.is_equal))
                dve.wait_ge(r_exp, 2)
                then(V.tensor_reduce(gsum, eg, AX.X, ALU.add))
                then(V.tensor_tensor(e8, e8, w16e[:, :, 0:NE], ALU.mult))
                then(V.tensor_reduce(esum, e8, AX.X, ALU.add))
                then(V.tensor_tensor(escale, gsum, esum, ALU.mult))
                then(V.reciprocal(gw, escale))
                then(V.tensor_tensor(e8, e8, gw.unsqueeze(2).broadcast_to([P, NT, NE]), ALU.mult))
                for t in range(NT):
                    ins = V.tensor_tensor(gate[:, t, :].rearrange("p (g e) -> p g e", g=NG),
                                          over(e8[:, t, :], NG, 1, [P, NG, NE]),
                                          hot[:, t, :].unsqueeze(2).broadcast_to([P, NG, NE]), ALU.mult)
                then(ins)
                dispatch(L)

                def rows_out(b, z):
                    dve.wait_ge(xin_psum, b + 2)
                    for hf in range(2):
                        V.tensor_tensor(xin_t[z][:, 4 * hf:4 * hf + 4, :],
                                        banks[hf][:, 0:4 * BR].rearrange("p (k r) -> p k r", k=4),
                                        gain[:, 1, 4 * hf:4 * hf + 4].unsqueeze(2).broadcast_to([P, 4, BR]),
                                        ALU.mult).then_inc(xin_ready, 1)

                def hidden_rows(b, z):
                    dve.wait_ge(silu_done, b + 1)
                    V.tensor_tensor(hidden[z], hidden[z], banks[2 + z][:, BR:2 * BR], ALU.mult).then_inc(h_done, 1)

                def turn_mid(i, last):
                    for q in range(SLOTS):
                        if not last or q + 1 < SLOTS:
                            rows_out(SLOTS * i + (q + 1), (q + 1) % 2)
                        hidden_rows(SLOTS * i + q, q % 2)

                rows_out(0, 0)
                with dve.Fori(0, TURNS - 1) as i:
                    turn_mid(i, False)
                turn_mid(TURNS - 1, True)
                with dve.If(dve.value_load(over_count[:, 0:1], min_val=0, max_val=OVER) != 0):
                    with dve.Fori(0, OVER) as v:
                        rows_out(v + EXPERTS, 0)
                        hidden_rows(v + EXPERTS, 0)
                for t in range(NT):
                    dve.wait_ge(combine_in[t], 16)
                    for k in range(2):
                        then(V.scalar_tensor_tensor(x[:, t, :], pairs(t)[:, k, :], pair_at[:, 2, k, t:t + 1], x[:, t, :],
                                                    ALU.mult, ALU.add))
                next_layer(dve, "dve")

            count[0] = 0
            square_sums(s_fin_ss)
            dve.wait_ge(s_fin_rs, 1)
            dve.wait_ge(s_rope, 32)
            for t in range(NT):
                dve.wait_ge(s_fin, t)
                V.tensor_scalar(x[:, t, :], x[:, t, :], rs[:, t:t + 1], None, ALU.mult).then_inc(s_fin_x, 1)
                dve.wait_ge(s_fin_x, t + 1)
                V.tensor_tensor(x[:, t, :], x[:, t, :], fin_gain, ALU.mult).then_inc(s_fin, 1)


_INS = ("x_prompt x_sample cache_k cache_v cache_kidx norm1 w_in sgu_ln_g sgu_ln_b sgu_w sgu_b w_pa w_pb w_out "
        "norm2 w_rg b_rg w_re b_re w_eg w_eu w_ed final_norm").split()
_OUTS = [(1, SEQ, D), (STREAMS, FRAMES, D), (DEPTH, 1, SEQ, KV, HD), (DEPTH, 1, SEQ, KV, HD), (DEPTH, 1, SEQ, ID),
         (DEPTH, STREAMS, FRAMES, KV, HD), (DEPTH, STREAMS, FRAMES, KV, HD), (DEPTH, STREAMS, FRAMES, ID),
         (DEPTH, STREAMS, FRAMES, SW)]


def _rope_table():
    pos = np.concatenate([np.arange(SEQ), PAST + np.tile(np.arange(FRAMES), STREAMS)]).astype(np.float32)
    parts = []
    for d in (HD, ID):
        inv = np.float32(10000.0) ** (-np.arange(0, d, 2, dtype=np.float32) / np.float32(d))
        ang = pos[:, None] * inv[None, :].astype(np.float32)
        parts += [np.cos(ang), np.sin(ang)]
    return np.concatenate(parts, axis=1).astype(np.float32).reshape(NT, P, HD + ID)


def _ids():
    pairs = 1 + np.arange(2 * ROWS).reshape(2 * NT, P).T
    return np.concatenate([np.tile(np.arange(BR), (P, 1)), pairs], axis=1).astype(np.float32)


def kernel(**inputs):
    import concourse.bacc as bacc
    from concourse.bass_utils import run_bass_kernel_spmd

    nc = bacc.Bacc("TRN2", target_bir_lowering=False, num_devices=1)
    arrays, a = {}, {}
    for name in _INS:
        arrays[f"in_{name}"] = v = np.ascontiguousarray(inputs[name])
        a[name] = nc.dram_tensor(f"in_{name}", v.shape, F32, kind="ExternalInput").ap()
    for name, v in (("rope", _rope_table()), ("ids", _ids())):
        arrays[f"in_{name}"] = v
        a[name] = nc.dram_tensor(f"in_{name}", v.shape, F32, kind="ExternalInput").ap()
    o = [nc.dram_tensor(f"out_{i}", s, F32, kind="ExternalOutput").ap() for i, s in enumerate(_OUTS)]
    build(nc, a, o)
    r = run_bass_kernel_spmd(nc, [arrays], core_ids=[0])
    return tuple(r.results[0][f"out_{i}"] for i in range(len(_OUTS)))
```

```python
from contextlib import ExitStack

import numpy as np

import concourse.bass as bass
from concourse import mybir

F32, I32, U32 = mybir.dt.float32, mybir.dt.int32, mybir.dt.uint32
ALU = mybir.AluOpType
ACT = mybir.ActivationFunctionType
AX = mybir.AxisListType

P = 128
DEPTH, D = 2, 1024
SEQ, STREAMS, FRAMES, PAST = 512, 8, 16, 256
PT = SEQ // P
NT = PT + 1
ROWS = NT * P
KD = D // P
HEADS, KV, HD = 8, 2, 64
GQ = HEADS // KV
IH, ID = 8, 32
SG, SW = 4, 512
NG, NE = 4, 8
EXPERTS, HID = NG * NE, 128
EPS = 1e-6
ATT_SCALE = HD ** -0.5
COLS = 4136
K0, V0, QI0, KI0, WI0 = 512, 640, 768, 1024, 1056
QKV_W = 1064
SK0 = (0, QI0)
Q_REP = 272
U0, VS0, GA0, GB0 = 1064, 1576, 2088, 3112
BLK = 512
TOPK_P, TOPK_S = 128, 68
KEYS = [P * (t + 1) for t in range(PT)] + [PAST + FRAMES]
MB_AT = [sum(KEYS[:t]) for t in range(NT)]
MB_W = sum(KEYS)
NEG = -3.3e38
SEL = -3.4e38
OFF = -1e30
SLOTS = 4
SLOT_W = KD * BLK
BR = 96
PAIRS = 2 * ROWS
OVER = (PAIRS - 1) // BR
TURNS = EXPERTS // SLOTS
AHEAD = 6
COLS_T = EXPERTS + OVER
NORM2 = ((0, NT - 2), (NT - 2, NT - 1), (NT - 1, NT))
YBUF = 2
AT_TABLE = 1220
AT_OVER = AT_TABLE + 2 * COLS_T
AT_WIDE = AT_OVER + OVER + 1 + 2 * SLOTS
NOWHERE = 1e6
(QU, KU, IU, UU, VU, KCU, VCU, SU) = range(8)
GAU, GBU, PABU = (8, 11), (9, 12), (10, 13)
OUTU = (14, 15)
IDX_TILES = (3, 1, 2, 4)
HEAD_JOBS = range(3 * NT, 3 * NT + 2)
TAIL_JOBS = {1: range(3 * NT + 2, 3 * NT + 5), 3: range(3 * NT + 5, 5 * NT)}
UNIT_DMAS = {u: 1 for u in range(16)} | {IU: 3, KCU: 4, VCU: 2, PABU[0]: 4, PABU[1]: 4}


def landed(u):
    return 16 * sum(UNIT_DMAS[v] for v in range(u + 1) if v % SLOTS == u % SLOTS)


EARLY = 1
PBUF = 4
SBANK = (0, 1, 6)
PROMPT_UNITS = [(t, j, g) for t in range(PT) for j in range(GQ) for g in range(KV)]
STREAM_UNITS = [(PT, j, g) for g in range(KV) for j in range(GQ)]
ATT_UNITS = PROMPT_UNITS + STREAM_UNITS
NPU, NAU = len(PROMPT_UNITS), len(ATT_UNITS)
LOOK = 3
QUERIES_AT = {NPU: 0, NPU + GQ: 1}
GATES_FROM = 6
GATE_STEPS = {GATES_FROM + (KD + 1) * t + k: (t, k) for t in range(EARLY) for k in range(KD + 1)}
KEYS_AT = {GATES_FROM + (KD + 1) * EARLY + i: divmod(i, 3) for i in range(6)}
assert max(KEYS_AT) < NPU - LOOK


def with_values(n):
    return n < NPU or (n - NPU) % GQ == GQ - 1


def over(ap, n, axis, shape):
    return ap.unsqueeze(axis).broadcast_to(shape)


def build(nc, a, o):
    ctx = ExitStack()
    with ctx:
        def sb(name, shape):
            return ctx.enter_context(nc.sbuf_tensor(name, shape, F32))

        def sem(name):
            return ctx.enter_context(nc.semaphore(name))

        ctx.enter_context(nc.allow_non_contiguous_dma("small parameters"))
        x = sb("x", [P, NT, D])
        xt = sb("xt", [P, KD, ROWS])
        qkv = sb("qkv", [P, NT, QKV_W])
        uv = sb("uv", [P, 2, NT, BLK])
        ring = sb("ring", [P, SLOTS, SLOT_W])
        att = sb("att", [P, GQ, ROWS])
        sgt = sb("sgt", [P, SG, ROWS])
        mb = sb("mb", [P, MB_W])
        kt = sb("kt", [P, SEQ])
        scr = sb("scr", [P, 2048])
        ident = sb("ident", [P, P])
        tril = sb("tril", [P, P])
        rope_t = sb("rope_t", [P, NT, HD + ID])
        quad = sb("quad", [P, 2, P])
        pair = sb("pair", [P, 4, P])
        own = sb("own", [P, STREAMS])
        gain = sb("gain", [P, DEPTH, 2, KD])
        rbias = sb("rbias", [P, NG + EXPERTS])
        sbias = sb("sbias", [P, 2, SG])
        corner = sb("corner", [P, SG, FRAMES])
        stat = sb("stat", [P, 92])
        ss, rs = stat[:, 0:5], stat[:, 5:10]
        mx, nmx, den, rden = (stat[:, 60 + PBUF * i:60 + PBUF * (i + 1)] for i in range(4))
        moments = stat[:, 18:28].rearrange("p (t c) -> p t c", c=2)
        lrs = stat[:, 28:33]
        half = stat[:, 33:38]
        bns = stat[:, 38:44]
        bests = [stat[:, c:c + 8] for c in (44, 76, 84)]
        var_e = stat[:, 52:57]
        over_sum = stat[0:1, 57:58]
        over_past = stat[0:1, 58:59].bitcast(I32)
        over_new = stat[0:1, 59:60]

        qit = att[:, :, :].rearrange("p a b -> p (a b)")[:, 0:1024].rearrange("p (j r) -> p j r", j=2)
        kit = att[:, :, :].rearrange("p a b -> p (a b)")[:, 1024:1536]
        kis = att[:, :, :].rearrange("p a b -> p (a b)")[:, 1536:1536 + 2 * KEYS[PT]].rearrange(
            "p (s k) -> p s k", s=2)
        sgt_flat = sgt[:, :, :].rearrange("p a b -> p (a b)")
        qis = sgt_flat[:, 0:2048].rearrange("p (s h q) -> p s h q", s=2, h=IH)
        qt = sgt_flat[:, 0:2048].rearrange("p (j r) -> p j r", j=GQ)
        qts = sgt_flat[:, 0:2048].rearrange("p (s j q) -> p s j q", s=4, j=GQ)

        ki_rep = kt[:, :]
        qis_rep = mb[:, 0:1024].rearrange("p (h c d) -> p h c d", h=IH, c=4)
        kis_rep = mb[:, 1024:1152]
        ks_rep = [sgt_flat[:, 2048:2176], sgt_flat[:, 2176:2304]]

        def score(t):
            return mb[:, MB_AT[t]:MB_AT[t] + KEYS[t]]

        probs = [scr[:, 512 * i:512 * i + 512] for i in range(PBUF)]
        probs_t = [ring[:, VCU % SLOTS, 2048 + 512 * i:2560 + 512 * i] for i in range(PBUF)]
        early_gate = [ring[:, SU % SLOTS, 3072 + 512 * t:3584 + 512 * t] for t in range(EARLY)]
        probs_t4 = ring[:, VCU % SLOTS, 2048:2048 + 512 * PBUF].rearrange("p (j c) -> p j c", j=PBUF)
        relu_b = [scr[:, 0:512], scr[:, 512:1024]]
        ln_g, ln_b = (ring[:, SU % SLOTS, 2048 + 512 * i:2560 + 512 * i] for i in range(2))
        xn = [scr[:, 0:1024], scr[:, 1024:2048]]
        sgw_t = [scr[:, 0:512].rearrange("p (g i) -> p g i", g=SG),
                 scr[:, 512:1024].rearrange("p (g i) -> p g i", g=SG)]
        fin_gain = uv[:, 0, 0:2, :].rearrange("p t c -> p (t c)")

        def mbv(at, w):
            return mb[:, at:at + w]
        logit = mbv(0, 180).rearrange("p (t c) -> p t c", t=NT)
        w16 = mbv(180, 80).rearrange("p (t c) -> p t c", t=NT)
        m8 = mbv(260, 40).rearrange("p (t c) -> p t c", t=NT)
        r8 = mbv(300, 40).rearrange("p (t c) -> p t c", t=NT)
        hot = mbv(340, 20).rearrange("p (t c) -> p t c", t=NT)
        eg = mbv(360, 20).rearrange("p (t c) -> p t c", t=NT)
        gsum, gw, esum, escale = (mbv(380 + 5 * i, 5) for i in range(4))
        picked = mbv(400, 160).rearrange("p (t g e) -> p t g e", t=NT, g=NG)
        l8 = mbv(560, 40).rearrange("p (t c) -> p t c", t=NT)
        e8 = mbv(600, 40).rearrange("p (t c) -> p t c", t=NT)
        gate = mbv(640, 160).rearrange("p (t e) -> p t e", t=NT)
        w16e = mbv(800, 80).rearrange("p (t c) -> p t c", t=NT)
        m8e = mbv(880, 40).rearrange("p (t c) -> p t c", t=NT)
        r8e = mbv(920, 40).rearrange("p (t c) -> p t c", t=NT)
        wr = kt[:, 0:KD * 36].rearrange("p (k c) -> p k c", k=KD)
        ids = kt[:, 288:288 + BR + 2 * NT]
        pair_at = mbv(960, 30).rearrange("p (w k t) -> p w k t", w=3, k=2)
        number_k, rank_k, whole_k, beyond_k, start_k = (
            mbv(1160 + 10 * i, 10).rearrange("p (k t) -> p k t", k=2) for i in range(5))
        start, need, scan_a, scan_b, size = (mbv(1000 + 32 * i, 32) for i in range(5))
        table = mbv(AT_TABLE, 2 * COLS_T)[0:BR, :].bitcast(U32).rearrange("p (w b) -> p w b", w=2)
        over_expert = mbv(AT_OVER, OVER)[0:1, :].bitcast(I32)
        over_count = mbv(AT_OVER + OVER, 1)[0:1, :].bitcast(I32)
        now = [[mbv(AT_OVER + OVER + 1 + SLOTS * w + q, 1)[0:BR, :].bitcast(U32) for q in range(SLOTS)] for w in range(2)]
        wide = mbv(AT_WIDE, 2 * COLS_T)[0:BR, :].rearrange("p (w b) -> p w b", w=2)
        pads = mbv(AT_WIDE + 2 * COLS_T, COLS_T)[0:BR, :]
        ones = scr[:, 0:P]
        before = scr[:, 1728:1856]
        (chosen, total, base, rank, number) = (
            scr[:, P + 160 * i:P + 160 * (i + 1)].rearrange("p (t e) -> p t e", t=NT) for i in range(5))
        mine, part = (scr[:, P + 160 * i:P + 160 * (i + 2)].rearrange("p (k t e) -> p k t e", k=2, t=NT) for i in (5, 7))
        onehot = att[:, :, :].rearrange("p a b -> p (a b)")[:, 0:2 * NT * (BR + COLS_T)].rearrange(
            "p (m c) -> p m c", m=2 * NT)
        begun = sgt_flat[0:1, 0:OVER * EXPERTS].rearrange("p (b e) -> p b e", e=EXPERTS)
        begun_count = sgt_flat[0:1, OVER * EXPERTS:OVER * (EXPERTS + 1)]
        xt_flat = xt[:, :, :].rearrange("p k r -> p (k r)")
        xin_t = [xt_flat[:, KD * BR * z:KD * BR * (z + 1)].rearrange("p (k r) -> p k r", k=KD) for z in range(2)]
        hidden = [xt_flat[:, 2 * KD * BR + BR * z:2 * KD * BR + BR * (z + 1)] for z in range(2)]
        yout = [scr[0:BR, D * z:D * (z + 1)] for z in range(YBUF)]
        expert_up = [ring[:, q, 0:2048] for q in range(SLOTS)] + [sgt_flat[:, 512:2560], xt_flat[:, 2048:4096]]
        expert_down = [ring[:, q, 2048:3072] for q in range(SLOTS)] + [
            att[:, :, :].rearrange("p a b -> p (a b)")[:, 1536:2560], xt_flat[:, 4096:5120]]
        assert 2 * NT * (BR + COLS_T) <= 1536 and OVER * (EXPERTS + 1) <= 512 and 2 * (KD + 1) * BR <= 2048
        xn2 = [uv[:, :, :, :].rearrange("p c t w -> p (c t w)")[:, D * t:D * (t + 1)] for t in range(NT)]
        xin = [xn2[q][0:BR, :] for q in range(SLOTS)]

        banks = [ctx.enter_context(nc.psum_tensor(f"bank{i}", [P, BLK], F32)) for i in range(8)]

        s_const = sem("s_const")
        s_ident = sem("s_ident")
        s_pool = sem("s_pool")
        s_rope = sem("s_rope")
        s_x = [sem(f"s_x{t}") for t in range(NT)]
        s_gain = sem("s_gain")
        s_out = sem("s_out")
        s_fin = sem("s_fin")
        s_squares = sem("s_squares")
        s_roots = sem("s_roots")
        s_fin_x = sem("s_fin_x")
        s_go = {e: sem(f"s_go_{e}") for e in ("pe", "act", "dve", "pool")}
        params, ln_loaded, wr_loaded = sem("params"), sem("ln_loaded"), sem("wr_loaded")
        kv_out, sguv_out = sem("kv_out"), sem("sguv_out")
        x_in = [sem(f"x_in{q}") for q in range(SLOTS)]
        y_out = [sem(f"y_out{z}") for z in range(YBUF)]
        x_over, y_over = sem("x_over"), sem("y_over")
        first = sem("arrived")
        arrived = first
        slot = [sem(f"slot{i}") for i in range(SLOTS)]
        names = ("early_psum early_done idx_used_pool weighted ks_rep_done score_done unit_done rows_sent sq_done x_new rs_ready xn_ready "
                 "xt_psum xt_done proj_psum proj_free rope_done rep_done kx_psum kx_done qis_done idx_psum "
                 "idx_relu idx_used qk_psum qk_done s_psum p_raw p_exp p_ready pt_psum pt_done "
                 "pv_done o_psum o_done ks_psum ks_done qts_done ln_stat ln_rs ln_done swm_ready "
                 "sw_psum sw_done sg_psum sg_used sgt_psum sgt_done mg_gate mg_proj mg_sig mg_done "
                 "mt_psum mt_done xo_psum xo_done r_psum r_exp r_sub gu_psum silu_done h_done "
                 "xd_out chosen_ready count_psum experts_known onehot_ready table_psum table_ready "
                 "xin_psum xin_ready turn over_free over_sent over_w y_ready y_psum dve_chain act_chain").split()
        (early_psum, early_done, idx_used_pool, weighted, ks_rep_done, score_done, unit_done, rows_sent, sq_done, x_new, rs_ready, xn_ready,
         xt_psum, xt_done, proj_psum, proj_free, rope_done, rep_done, kx_psum, kx_done, qis_done, idx_psum,
         idx_relu, idx_used, qk_psum, qk_done, s_psum, p_raw, p_exp, p_ready, pt_psum, pt_done,
         pv_done, o_psum, o_done, ks_psum, ks_done, qts_done, ln_stat, ln_rs, ln_done, swm_ready,
         sw_psum, sw_done, sg_psum, sg_used, sgt_psum, sgt_done, mg_gate, mg_proj, mg_sig, mg_done,
         mt_psum, mt_done, xo_psum, xo_done, r_psum, r_exp, r_sub, gu_psum, silu_done, h_done,
         xd_out, chosen_ready, count_psum, experts_known, onehot_ready, table_psum, table_ready,
         xin_psum, xin_ready, turn, over_free, over_sent, over_w, y_ready, y_psum, dve_chain, act_chain) = made = [sem(n) for n in names]
        combine_in = [sem(f"combine_in{t}") for t in range(NT)]
        extra = [sem(f"extra{i}") for i in range(2)]
        layer_sems = [first, *slot, *made, *combine_in, *extra]
        assert [s.num - first.num for s in layer_sems] == list(range(len(layer_sems)))

        xd = nc.dram_tensor("xd", (ROWS, D), F32, kind="Internal").ap()
        yd = nc.dram_tensor("yd", (2 * ROWS, D), F32, kind="Internal").ap()
        block = ctx.enter_context(nc.Block())

        def pairs(t):
            return ring[:, t % SLOTS, 2048 * (t // SLOTS):2048 * (t // SLOTS) + 2048].rearrange("p (k c) -> p k c", k=2)

        def earlier(eng):
            return eng.value_load(over_past[:, 0:1], min_val=0, max_val=16 * OVER * DEPTH)

        def next_layer(eng, key):
            eng.drain().then_inc(arrived, 1)
            eng.wait_ge(s_go[key], 1)
            eng.sem_clear(s_go[key])

        def idx_use(m):
            if IH <= m < 2 * IH:
                return idx_used_pool, m + 1 - IH
            return idx_used, m + 1 if m < IH else m + 1 - IH

        def key_scores(eng, at):
            t = IDX_TILES[at]
            s = score(t)
            for h in range(IH):
                m = IH * at + h
                eng.wait_ge(idx_relu, m + 1)
                w = qkv[:, t, WI0 + h:WI0 + h + 1]
                r = relu_b[m % 2][:, 0:KEYS[t]]
                if h == 0:
                    ins = eng.tensor_scalar(s, r, w, None, ALU.mult)
                elif eng is nc.vector:
                    ins = eng.scalar_tensor_tensor(s, r, w, s, ALU.mult, ALU.add)
                else:
                    eng.tensor_scalar(r, r, w, None, ALU.mult).then_inc(weighted, 1)
                    eng.wait_ge(weighted, (IH - 1) * (at - 1) + h)
                    ins = eng.tensor_tensor(s, s, r, ALU.add)
                used, n = idx_use(m)
                ins.then_inc(used, 1)
                eng.wait_ge(used, n)

        @block.sync
        def _(sp):
            for l in range(DEPTH):
                sp.dma_start(gain[:, l, 0, :], a["norm1"][l].rearrange("(p k) -> p k", k=KD)).then_inc(s_gain, 16)
                sp.dma_start(gain[:, l, 1, :], a["norm2"][l].rearrange("(p k) -> p k", k=KD)).then_inc(s_gain, 16)
            for t in range(PT):
                sp.dma_start(x[:, t, :], a["x_prompt"][0, t * P:(t + 1) * P, :]).then_inc(s_x[t], 16)
            sp.dma_start(x[:, PT, :], a["x_sample"].rearrange("b t d -> (b t) d")).then_inc(s_x[PT], 16)
            with sp.Fori(0, DEPTH) as L:
                w_in = a["w_in"][L].rearrange("(p k) c -> p k c", k=KD)

                def load(u, dst, src):
                    sp.dma_start(dst, src).then_inc(slot[u % SLOTS], 16)

                def at(u):
                    return ring[:, u % SLOTS, :]

                def cols(u, c0, w=BLK):
                    load(u, at(u)[:, 0:KD * w].rearrange("p (k c) -> p k c", k=KD), w_in[:, :, c0:c0 + w])

                for u in range(16):
                    if u >= SLOTS:
                        sp.wait_ge(unit_done, u - SLOTS + 1)
                    if u in (QU, KU):
                        cols(u, u * BLK)
                    elif u == IU:
                        cols(u, KI0, QKV_W - KI0)
                        for h in range(2):
                            load(u, at(u)[:, 512 + 256 * h:768 + 256 * h].rearrange("p (b d) -> p b d", b=STREAMS),
                                 a["cache_kidx"][L].rearrange("b (t p) d -> t p b d", p=P)[h])
                    elif u == UU:
                        cols(u, U0)
                    elif u == VU:
                        cols(u, VS0)
                    elif u == KCU:
                        for h in range(2):
                            for g in range(KV):
                                c0 = 512 * (2 * h + g)
                                load(u, at(u)[:, c0:c0 + 512].rearrange("p (b d) -> p b d", b=STREAMS),
                                     a["cache_k"][L].rearrange("b (t p) g d -> t g p b d", p=P)[h, g])
                    elif u == VCU:
                        for hf in range(2):
                            load(u, at(u)[:, 1024 * hf:1024 * hf + 1024].rearrange("p (n c) -> p n c", n=8),
                                 a["cache_v"][L].rearrange("b (t p) g d -> p (b t) (g d)", p=P)[:, 8 * hf:8 * hf + 8, :])
                    elif u == SU:
                        load(u, at(u)[:, 0:512].rearrange("p (g j) -> p g j", g=SG),
                             a["sgu_w"][L].rearrange("g i j -> i g j"))
                    elif u in GAU:
                        if u == GAU[1]:
                            sp.wait_ge(mg_done, EARLY)
                        cols(u, GA0 + BLK * GAU.index(u))
                    elif u in GBU:
                        cols(u, GB0 + BLK * GBU.index(u))
                    elif u in PABU:
                        c0 = BLK * PABU.index(u)
                        for g in range(KV):
                            load(u, at(u)[64 * g:64 * g + 64, 0:2048].rearrange("p (j c) -> p j c", j=GQ),
                                 a["w_pa"][L].rearrange("(g j p) c -> g p j c", g=KV, p=HD)[g, :, :, c0:c0 + BLK])
                        for hf in range(2):
                            load(u, at(u)[:, 2048 + 1024 * hf:3072 + 1024 * hf].rearrange("p (j c) -> p j c", j=2),
                                 a["w_pb"][L].rearrange("(j p) c -> p j c", p=P)[:, 2 * hf:2 * hf + 2, c0:c0 + BLK])
                    else:
                        c0 = BLK * OUTU.index(u)
                        load(u, at(u).rearrange("p (k c) -> p k c", k=KD),
                             a["w_out"][L].rearrange("(k p) c -> p k c", p=P)[:, :, c0:c0 + BLK])

                def expert(q, row, landed_sem):
                    for n, w in enumerate(("w_eg", "w_eu")):
                        sp.dma_start(expert_up[q][:, 1024 * n:1024 * n + 1024],
                                     a[w].rearrange("l g e (p k) f -> (l g e) p (k f)", k=KD)[row]
                                     ).then_inc(landed_sem, 16)
                    sp.dma_start(expert_down[q],
                                 a["w_ed"].rearrange("l g e f d -> (l g e) f d")[row]).then_inc(landed_sem, 16)

                for q in range(SLOTS):
                    sp.wait_ge(unit_done, 13 + q)
                    expert(q, EXPERTS * L + (q + 2), slot[q])
                    if q == 1:
                        expert(SLOTS, EXPERTS * L, extra[0])
                for t in range(NT):
                    sp.wait_ge(xn_ready, NT + t + 1)
                    sp.dma_start(xd[t * P:(t + 1) * P, :], xn2[t]).then_inc(xd_out, 16)
                sp.wait_ge(r_psum, 1)
                expert(SLOTS + 1, EXPERTS * L + 1, extra[1])
                with sp.Fori(0, TURNS - 2) as i:
                    for q in range(SLOTS):
                        sp.wait_ge(y_psum, SLOTS * i + (q + 3))
                        expert(q, EXPERTS * L + (SLOTS * i + (SLOTS + q + 2)), slot[q])
                for q in range(SLOTS - 2):
                    sp.wait_ge(y_psum, SLOTS * (TURNS - 2) + q + 3)
                    expert(q, EXPERTS * L + (SLOTS * (TURNS - 1) + q + 2), slot[q])
                sp.wait_ge(experts_known, 1)
                with sp.If(sp.value_load(over_count[:, 0:1], min_val=0, max_val=OVER) != 0):
                    with sp.Fori(0, OVER) as v:
                        sp.wait_ge(y_psum, v + EXPERTS)
                        e = sp.value_load(over_expert[:, bass.ds(v, 1)], min_val=0, max_val=EXPERTS - 1)
                        expert(0, EXPERTS * L + e, over_w)
                    sp.wait_ge(y_over, earlier(sp) + (16 * OVER + 16))
                    sp.sem_inc(over_sent, 1)
                sp.wait_ge(y_psum, EXPERTS)
                for z in range(YBUF):
                    sp.wait_ge(y_out[z], 16 * (EXPERTS // YBUF) * L + (16 * (EXPERTS // YBUF) + 16))
                    sp.sem_inc(turn, 1)
                sp.wait_ge(turn, YBUF)
                for t in range(NT):
                    sp.dma_start(pairs(t), yd.rearrange("(k t p) c -> t p k c", k=2, t=NT)[t]).then_inc(combine_in[t], 16)
                sp.wait_ge(arrived, 4)
                sp.sem_clear(range(layer_sems[0].num, layer_sems[-1].num + 1))
                for key in s_go:
                    sp.sem_inc(s_go[key], 1)
            for t in range(PT):
                sp.wait_ge(s_fin, t + 1)
                sp.dma_start(o[0][0, t * P:(t + 1) * P, :], x[:, t, :]).then_inc(s_out, 16)
            sp.wait_ge(s_fin, NT)
            sp.dma_start(o[1].rearrange("b t d -> (b t) d"), x[:, PT, :]).then_inc(s_out, 16)
            sp.wait_ge(s_out, 16 * NT)

        @block.gpsimd
        def _(pool):
            def power(dst, src, scale, ready, n, out_sem, w=NT):
                pool.wait_ge(ready, n)
                pool.tensor_scalar(dst, src, scale, EPS, ALU.mult, ALU.add).then_inc(s_pool, 1)
                pool.wait_ge(s_pool, 1)
                pool.sem_clear(s_pool)
                pool.tensor_tensor(dst, dst, half[:, 0:w], ALU.pow).then_inc(out_sem, 1)

            pool.memset(ident[:, :], 0.0)
            pool.memset(half, -0.5).then_inc(s_pool, 1)
            pool.wait_ge(s_pool, 1)
            pool.sem_clear(s_pool)
            pool.affine_select(out=ident[:, :], in_=ident[:, :], compare_op=ALU.not_equal, fill=1.0,
                               base=0, pattern=[[-1, P]], channel_multiplier=1).then_inc(s_ident, 1)
            power(rs, ss, 1.0 / D, s_squares, NT, s_roots)
            pool.dma_start(rope_t[:, :, :], a["rope"].rearrange("t p c -> p t c")).then_inc(s_rope, 16)
            for q, done in enumerate((*y_out, y_over)):
                pool.dma_start(yd[q * P:(q + 1) * P, 0:HD + ID], a["rope"][q]).then_inc(done, 16)
            pool.memset(tril[:, :], 1.0)
            pool.memset(quad[:, :, :], 0.0)
            pool.memset(pair[:, :, :], 0.0)
            pool.memset(own[:, :], 1.0)
            pool.memset(over_sum, 0.0)
            pool.memset(mb[:, 0:P], 0.0).then_inc(s_pool, 1)
            pool.wait_ge(s_pool, 1)
            pool.affine_select(out=tril[:, :], in_=tril[:, :], compare_op=ALU.is_ge, fill=0.0,
                               base=0, pattern=[[-1, P]], channel_multiplier=1)
            pool.affine_select(out=own[:, :], in_=own[:, :], compare_op=ALU.is_ge, fill=0.0,
                               base=0, pattern=[[-FRAMES, STREAMS]], channel_multiplier=1).then_inc(s_pool, 1)
            pool.wait_ge(s_pool, 2)
            pool.affine_select(out=own[:, :], in_=own[:, :], compare_op=ALU.is_ge, fill=0.0,
                               base=FRAMES - 1, pattern=[[FRAMES, STREAMS]], channel_multiplier=-1).then_inc(s_pool, 1)
            pool.wait_ge(s_pool, 3)
            for b in range(STREAMS):
                q = slice(FRAMES * b, FRAMES * (b + 1))
                pool.memset(quad[32 * (b % 4):32 * (b % 4) + 32, b // 4, q], 1.0).then_inc(s_pool, 1)
                pool.wait_ge(s_pool, 4 + 2 * b)
                pool.memset(pair[64 * (b % 2):64 * (b % 2) + 64, b // 2, q], 1.0).then_inc(s_pool, 1)
                pool.wait_ge(s_pool, 5 + 2 * b)
            pool.sem_inc(s_const, 1)

            pool.sem_clear(s_pool)
            with pool.Fori(0, DEPTH) as L:
                pool.dma_start(rbias[:, 0:NG], a["b_rg"][L].partition_broadcast(P)).then_inc(params, 16)
                pool.dma_start(rbias[:, NG:], a["b_re"][L].partition_broadcast(P)).then_inc(params, 16)
                pool.dma_start(sbias[:, 0, :], a["sgu_b"][L].rearrange("g i -> i g")).then_inc(params, 16)
                for b in range(STREAMS):
                    q = slice(FRAMES * b, FRAMES * (b + 1))
                    pool.dma_start(sbias[q, 1, :], a["sgu_b"][L][:, 0:FRAMES].rearrange("g i -> i g")).then_inc(params, 16)
                    pool.dma_start(corner[q, :, :], a["sgu_w"][L][:, 0:FRAMES, 0:FRAMES].rearrange("g i j -> i g j")).then_inc(params, 16)
                for t in range(NT):
                    pool.wait_ge(rope_done, t + 1)
                    for c0, w, n in ((K0, P, 0), (V0, P, 1), (KI0, ID, 2)):
                        if t < PT:
                            dst = o[2 + n][L][0, t * P:(t + 1) * P]
                            dst = dst if n == 2 else dst.rearrange("t g d -> t (g d)")
                        else:
                            dst = o[5 + n][L]
                            dst = dst.rearrange("b t d -> (b t) d") if n == 2 else dst.rearrange("b t g d -> (b t) (g d)")
                        pool.dma_start(dst, qkv[:, t, c0:c0 + w]).then_inc(kv_out, 16)
                    dst = ki_rep[:, t * P:(t + 1) * P] if t < PT else kis_rep
                    if t == PT:
                        pool.tensor_copy(qis_rep[:, :, :, :],
                                         qkv[:, t, QI0:KI0].rearrange("p (h d) -> p h d", h=IH).unsqueeze(2).broadcast_to([P, IH, 4, ID]))
                    pool.tensor_copy(dst.rearrange("p (c d) -> p c d", c=4),
                                     over(qkv[:, t, KI0:KI0 + ID], 4, 1, [P, 4, ID])).then_inc(rep_done, 1)
                key_scores(pool, 1)
                pool.sem_inc(score_done, 1)
                pool.wait_ge(unit_done, SU - SLOTS + 1)
                pool.dma_start(ln_g, a["sgu_ln_g"][L].partition_broadcast(P)).then_inc(ln_loaded, 16)
                pool.dma_start(ln_b, a["sgu_ln_b"][L].partition_broadcast(P)).then_inc(ln_loaded, 16)
                pool.wait_ge(qk_psum, 1 + GQ)
                for g in range(KV):
                    c0 = K0 + HD * g
                    pool.tensor_copy(ks_rep[g].rearrange("p (c d) -> p c d", c=2),
                                     over(qkv[:, PT, c0:c0 + HD], 2, 1, [P, 2, HD])).then_inc(ks_rep_done, 1)
                for g in range(KV):
                    if g:
                        power(lrs, moments[:, :, 1], 1.0, ln_stat, 1, ln_rs)
                        pool.wait_ge(ln_rs, 1)
                        for step in range(3):
                            for t in range(NT):
                                v = uv[:, 1, t, :]
                                if step == 0:
                                    ins = pool.tensor_scalar(v, v, moments[:, t, 0:1], lrs[:, t:t + 1], ALU.subtract, ALU.mult)
                                else:
                                    pool.wait_ge(ln_done, NT * (step - 1) + t + 1)
                                    pool.wait_ge(ln_loaded, 32 * L + 32)
                                    ins = pool.tensor_tensor(v, v, (ln_g, ln_b)[step - 1], (ALU.mult, ALU.add)[step - 1])
                                ins.then_inc(ln_done, 1)
                        pool.wait_ge(ln_done, 3 * NT)
                        pool.dma_start(o[8][L].rearrange("b t c -> (b t) c"), uv[:, 1, PT, :]).then_inc(sguv_out, 16)
                        pool.wait_ge(ks_psum, 7)
                    q = qkv[:, PT, 0:512].rearrange("p (j g d) -> p j g d", g=KV, j=GQ)[:, :, g, :]
                    pool.tensor_copy(qkv[:, 0:GQ, Q_REP:Q_REP + P].rearrange("p j (c d) -> p j c d", c=2),
                                     q.unsqueeze(2).broadcast_to([P, GQ, 2, HD])).then_inc(rep_done, 1)
                pool.wait_ge(kv_out, 48 * NT * L + 48 * NT)
                pool.wait_ge(sguv_out, 16 * L + 16)
                pool.sem_inc(rows_sent, 1)
                pool.wait_ge(s_psum, NAU)
                pool.dma_start(wr[:, :, 0:NG], a["w_rg"][L].rearrange("(p k) c -> p k c", k=KD)).then_inc(wr_loaded, 16)
                pool.dma_start(wr[:, :, NG:], a["w_re"][L].rearrange("(p k) c -> p k c", k=KD)).then_inc(wr_loaded, 16)
                pool.dma_start(ids, a["ids"]).then_inc(wr_loaded, 16)
                for t0, t1 in NORM2:
                    power(rs[:, t0:t1], ss[:, t0:t1], 1.0 / D, sq_done, t1, rs_ready, t1 - t0)
                pool.wait_ge(table_ready, 1)
                pool.wait_ge(xd_out, 16 * NT)
                pool.wait_ge(r_psum, 1)

                def gather(b, q, landed_sem):
                    pool.tensor_copy(now[0][q], table[:, 0, bass.ds(b, 1)]).then_inc(s_pool, 1)
                    pool.wait_ge(s_pool, 1)
                    pool.sem_clear(s_pool)
                    pool.indirect_dma_start(out=xin[q], out_offset=None, in_=xd,
                                            in_offset=bass.IndirectOffsetOnAxis(ap=now[0][q], axis=0),
                                            bounds_check=ROWS - 1, oob_is_err=False).then_inc(landed_sem, 16)

                def scatter(b, q, z, sent_sem):
                    pool.tensor_copy(now[1][q], table[:, 1, bass.ds(b, 1)]).then_inc(s_pool, 1)
                    pool.wait_ge(s_pool, 1)
                    pool.sem_clear(s_pool)
                    pool.indirect_dma_start(out=yd, in_=yout[z], in_offset=None,
                                            out_offset=bass.IndirectOffsetOnAxis(ap=now[1][q], axis=0),
                                            bounds_check=2 * ROWS - 1, oob_is_err=False).then_inc(sent_sem, 16)

                def next_rows(b, q):
                    pool.wait_ge(xin_psum, b - 2)
                    gather(b, q, x_in[q])

                def turn_rows(i, last):
                    for q in range(SLOTS):
                        b = SLOTS * i + q
                        pool.wait_ge(y_ready, b + 3)
                        scatter(b, q, q % YBUF, y_out[q % YBUF])
                        if not last or b + AHEAD < EXPERTS:
                            next_rows(b + AHEAD, (q + AHEAD) % SLOTS)

                for b in range(SLOTS):
                    gather(b, b, x_in[b])
                for b in range(SLOTS, AHEAD):
                    next_rows(b, b % SLOTS)
                whole_turns = (EXPERTS - AHEAD) // SLOTS
                with pool.Fori(0, whole_turns) as i:
                    turn_rows(i, False)
                for i in range(whole_turns, TURNS):
                    turn_rows(i, True)
                with pool.If(pool.value_load(over_count[:, 0:1], min_val=0, max_val=OVER) != 0):
                    with pool.Fori(0, OVER) as v:
                        pool.wait_ge(xin_psum, v + (EXPERTS + 1))
                        gather(v + EXPERTS, 0, x_over)
                        pool.wait_ge(y_ready, v + (EXPERTS + 3))
                        scatter(v + EXPERTS, 0, 0, y_over)
                power(rs, ss, 1.0 / D, sq_done, 2 * NT, rs_ready)
                next_layer(pool, "pool")
            pool.dma_start(fin_gain, a["final_norm"].partition_broadcast(P)).then_inc(s_rope, 16)

        @block.tensor
        def _(pe):
            pe.wait_ge(s_ident, 1)
            idm = ident[:, :]

            def norm_transposes(phase, tiles):
                for t in tiles:
                    pe.wait_ge(xn_ready, NT * phase + t + 1)
                    for hf in range(2):
                        n = 2 * t + hf
                        if n >= 4:
                            pe.wait_ge(xt_done, 2 * NT * phase + n - 3)
                        for k in range(4):
                            mm = pe.transpose(banks[n % 4][:, k * P:(k + 1) * P],
                                              (xn2[t] if phase else xn[t % 2])[:, 4 * hf + k:D:KD], idm)
                        mm.then_inc(xt_psum, 1)

            with pe.Fori(0, DEPTH) as L:
                def unit(u):
                    return ring[:, u % SLOTS, :]

                def wait_unit(u):
                    pe.wait_ge(slot[u % SLOTS], landed(u))

                def project(u, t, out, w=BLK):
                    rhs = unit(u)[:, 0:KD * w].rearrange("p (k c) -> p k c", k=KD)
                    for k in range(KD):
                        mm = pe.matmul(out, xt[:, k, t * P:(t + 1) * P], rhs[:, k, :],
                                       start=(k == 0), stop=(k == KD - 1))
                    return mm

                jobs = [(u, t) for u in (QU, KU, IU, UU, VU) for t in range(NT)]

                def proj_job(n):
                    u, t = jobs[n]
                    if t == 0:
                        wait_unit(u)
                    if u == QU:
                        pe.wait_ge(xt_done, 2 * t + 2)
                    if n >= 4:
                        pe.wait_ge(proj_free, n - 3)
                    w = QKV_W - KI0 if u == IU else BLK
                    mm = project(u, t, banks[4 + n % 4][:, 0:w], w)
                    mm.then_inc(proj_psum, 1)
                    if t == NT - 1 and u != IU:
                        pe.drain().then_inc(unit_done, 1)

                norm_transposes(0, range(NT))
                for n in range(3 * NT):
                    proj_job(n)
                pe.wait_ge(xt_done, 2 * NT)
                kidx = unit(IU)[:, 512:1024].rearrange("p (h s c) -> p h s c", h=2, s=2)
                for s in range(2):
                    for h in range(2):
                        mm = pe.transpose(banks[0][:, 256 * s + 128 * h:256 * s + 128 * h + 128],
                                          kidx[:, h, s, :], idm)
                mm.then_inc(kx_psum, 1)
                pe.drain().then_inc(unit_done, 1)
                for n in HEAD_JOBS:
                    proj_job(n)
                pe.wait_ge(rope_done, NT)
                pe.wait_ge(rep_done, NT)
                for t in range(PT):
                    mm = pe.transpose(banks[1][:, t * P:(t + 1) * P],
                                      ki_rep[:, t * P:(t + 1) * P], idm)
                mm.then_inc(kx_psum, 1)
                for j in range(2):
                    for t in range(PT):
                        mm = pe.transpose(banks[2 + j][:, t * P:(t + 1) * P],
                                          qkv[:, t, QI0 + P * j:QI0 + P * (j + 1)], idm)
                    mm.then_inc(kx_psum, 1)
                pe.wait_ge(kx_done, 1)
                pe.transpose(banks[0][:, 0:P], kis_rep, idm).then_inc(kx_psum, 1)
                for j in range(2):
                    pe.wait_ge(kx_done, 2 + j)
                    for h in range(4):
                        mm = pe.transpose(banks[1 + j][:, h * P:(h + 1) * P],
                                          qis_rep[:, 4 * j + h, :, :].rearrange("p c d -> p (c d)"), idm)
                    mm.then_inc(kx_psum, 1)
                pe.wait_ge(kx_done, 5)
                pe.wait_ge(qis_done, 2)
                for at, t in enumerate(IDX_TILES):
                    for h in range(IH):
                        m = IH * at + h
                        if m >= 4:
                            pe.wait_ge(idx_relu, m - 3)
                        out = banks[m % 4][:, 0:KEYS[t]]
                        if t < PT:
                            r = slice(ID * (h % 4), ID * (h % 4) + ID)
                            mm = pe.matmul(out, qit[r, h // 4, t * P:(t + 1) * P], kit[r, 0:KEYS[t]],
                                           start=True, stop=True)
                        else:
                            for s in range(2):
                                mm = pe.matmul(out, qis[:, s, h, :], kis[:, s, :], start=(s == 0), stop=(s == 1))
                        mm.then_inc(idx_psum, 1)
                    for n in TAIL_JOBS.get(at, ()):
                        proj_job(n)
                pe.wait_ge(idx_relu, IH * len(IDX_TILES))
                for t in range(PT):
                    mm = pe.transpose(banks[0][:, t * P:(t + 1) * P], qkv[:, t, K0:K0 + P], idm)
                mm.then_inc(qk_psum, 1)
                pe.wait_ge(proj_free, 5 * NT)
                for j in range(GQ):
                    for t in range(PT):
                        mm = pe.transpose(banks[4 + j][:, t * P:(t + 1) * P], qkv[:, t, j * P:(j + 1) * P], idm)
                    mm.then_inc(qk_psum, 1)
                pe.wait_ge(qk_done, 1 + GQ)

                def stream_keys(g, step):
                    if g == 0 and step == 0:
                        wait_unit(KCU)
                        pe.wait_ge(early_done, EARLY)
                    if g or step:
                        pe.wait_ge(ks_done, 3 * g + step)
                    if step < 2:
                        kc = unit(KCU)[:, 0:2048].rearrange("p (h g s c) -> p h g s c", h=2, g=KV, s=4)
                        for s in range(2):
                            for h in range(2):
                                mm = pe.transpose(banks[7][:, 256 * s + 128 * h:256 * s + 128 * h + 128],
                                                  kc[:, h, g, 2 * step + s, :], idm)
                    else:
                        pe.wait_ge(ks_rep_done, g + 1)
                        mm = pe.transpose(banks[7][:, 0:P], ks_rep[g], idm)
                    mm.then_inc(ks_psum, 1)

                def stream_queries(g):
                    pe.wait_ge(ks_done, 6)
                    pe.wait_ge(rep_done, NT + 1 + g)
                    if g:
                        pe.wait_ge(qts_done, 4 * g)
                    for j in range(GQ):
                        mm = pe.transpose(banks[7][:, j * P:(j + 1) * P], qkv[:, j, Q_REP:Q_REP + P], idm)
                    mm.then_inc(ks_psum, 1)
                    if g:
                        pe.drain().then_inc(unit_done, 1)

                def logits(n):
                    t, j, g = ATT_UNITS[n]
                    if n in QUERIES_AT:
                        stream_queries(g)
                    if n >= len(SBANK):
                        pe.wait_ge(p_raw, n - len(SBANK) + 1)
                    out = banks[SBANK[n % len(SBANK)]][:, 0:KEYS[t]]
                    if t < PT:
                        r = slice(HD * g, HD * g + HD)
                        mm = pe.matmul(out, qt[r, j, t * P:(t + 1) * P], kt[r, 0:KEYS[t]], start=True, stop=True)
                    else:
                        for s in range(4):
                            if n in QUERIES_AT:
                                pe.wait_ge(qts_done, 4 * g + s + 1)
                            mm = pe.matmul(out, qts[:, s, j, :], qkv[:, s, SK0[g]:SK0[g] + KEYS[t]],
                                           start=(s == 0), stop=(s == 3))
                    mm.then_inc(s_psum, 1)

                def probs_transposes(n):
                    t, j, g = ATT_UNITS[n]
                    pe.wait_ge(p_ready, n + 1)
                    if n >= 2:
                        pe.wait_ge(pt_done, n - 1)
                    blocks = range(t + 1) if t < PT else (0, 1, 3)
                    for i, c in enumerate(blocks):
                        mm = pe.transpose(banks[2 + n % 2][:, i * P:(i + 1) * P],
                                          probs[n % PBUF][:, c * P:(c + 1) * P], idm)
                    mm.then_inc(pt_psum, 1)

                def values(n):
                    t, j, g = ATT_UNITS[n]
                    pe.wait_ge(pt_done, n + 1)
                    if t >= 2 and g == 0 and (t == PT or j == 0):
                        pe.wait_ge(o_done, t - 1)
                    o_b = banks[4 + t % 2]
                    v = slice(V0 + HD * g, V0 + HD * g + HD)
                    r = slice(HD * g, HD * g + HD)
                    if t < PT:
                        pt = probs_t[n % PBUF]
                        for c in range(t + 1):
                            mm = pe.matmul(o_b[r, j * P:(j + 1) * P], qkv[:, c, v], pt[:, c * P:(c + 1) * P],
                                           start=(c == 0), stop=(c == t))
                    else:
                        if n == NPU + GQ - 1:
                            wait_unit(VCU)
                        vc = unit(VCU)[:, 0:2048].rearrange("p (b t c) -> p b t c", b=STREAMS, t=2)
                        o4 = o_b[r, :].rearrange("p (j q) -> p j q", j=GQ)
                        pe.matmul(o4, qkv[:, PT, v], probs_t4[:, :, 2 * P:3 * P], start=True, stop=False)
                        for b in range(STREAMS):
                            for h in range(2):
                                q0 = FRAMES * b
                                mm = pe.matmul(o4[:, :, q0:q0 + FRAMES], vc[:, b, h, r],
                                               probs_t4[:, :, h * P + q0:h * P + q0 + FRAMES], start=False,
                                               stop=(b == STREAMS - 1 and h == 1))
                    mm.then_inc(pv_done, 1)
                    if n == NAU - 1 or ATT_UNITS[n + 1][0] != t:
                        pe.drain().then_inc(o_psum, 1)

                def gate_step(t, k):
                    if t == 0 and k == 0:
                        wait_unit(GAU[0])
                    if t and k == 0:
                        pe.wait_ge(early_done, t)
                    if k < KD:
                        mm = pe.matmul(banks[7][:, :], xt[:, k, t * P:(t + 1) * P],
                                       unit(GAU[0])[:, k * BLK:(k + 1) * BLK], start=(k == 0), stop=(k == KD - 1))
                        if k == KD - 1:
                            mm.then_inc(early_psum, 1)

                for n in range(LOOK):
                    logits(n)
                for n in range(NAU):
                    if n in KEYS_AT:
                        stream_keys(*KEYS_AT[n])
                    probs_transposes(n)
                    if n + LOOK < NAU:
                        logits(n + LOOK)
                    if n in GATE_STEPS:
                        gate_step(*GATE_STEPS[n])
                    if n >= 1 and with_values(n - 1):
                        values(n - 1)
                values(NAU - 1)
                pe.drain().then_inc(unit_done, 1)

                for m in range(2):
                    pe.wait_ge(swm_ready, m + 1)
                    if m == 0:
                        src = unit(SU)[:, 0:512]
                    else:
                        src = unit(SU)[:, 1024:1536]
                    for g in range(SG):
                        mm = pe.transpose(banks[6 + m][:, g * P:(g + 1) * P], src[:, g * P:(g + 1) * P], idm)
                    mm.then_inc(sw_psum, 1)
                pe.drain().then_inc(unit_done, 1)
                pe.wait_ge(sw_done, 2)
                for t in range(NT):
                    pe.wait_ge(ln_done, 2 * NT + t + 1)
                    if t == 4:
                        pe.wait_ge(sg_used, 1)
                    for g in range(SG):
                        mm = pe.matmul(banks[t % 4][:, g * P:(g + 1) * P], sgw_t[t // PT][:, g, :],
                                       uv[:, 1, t, g * P:(g + 1) * P], start=True, stop=True)
                    mm.then_inc(sg_psum, 1)
                pe.wait_ge(o_done, NT)
                for t in range(NT):
                    pe.wait_ge(sg_used, t + 1)
                    if t == 4:
                        pe.wait_ge(sgt_done, 1)
                    for g in range(SG):
                        mm = pe.transpose(banks[4 + t % 4][:, g * P:(g + 1) * P], uv[:, 0, t, g * P:(g + 1) * P], idm)
                    mm.then_inc(sgt_psum, 1)

                pe.wait_ge(sgt_done, NT)
                for n in range(2 * NT):
                    c, t = divmod(n, NT)
                    b = banks[4 * (n % 2):4 * (n % 2) + 4]
                    if n >= 2:
                        pe.wait_ge(mg_done, n - 1)
                    if t == 0:
                        wait_unit(GAU[c])
                        wait_unit(GBU[c])
                    if n >= EARLY:
                        mm = project(GAU[c], t, b[0][:, :])
                    if t == NT - 1:
                        mm.then_inc(unit_done, 1)
                    project(GBU[c], t, b[1][:, :]).then_inc(mg_gate, 1)
                    if t == NT - 1:
                        pe.drain().then_inc(unit_done, 1)
                    if t == 0:
                        wait_unit(PABU[c])
                    w = unit(PABU[c]).rearrange("p (n c) -> p n c", n=8)
                    for half_, src in ((0, att), (1, sgt)):
                        for j in range(4):
                            mm = pe.matmul(b[2 + half_][:, :], src[:, j, t * P:(t + 1) * P], w[:, 4 * half_ + j, :],
                                           start=(j == 0), stop=(j == 3))
                    mm.then_inc(mg_proj, 1)
                    if t == NT - 1:
                        pe.drain().then_inc(unit_done, 1)
                pe.wait_ge(mg_done, 2 * NT)
                for n in range(2 * NT):
                    t, hf = divmod(n, 2)
                    if n >= 4:
                        pe.wait_ge(mt_done, n - 3)
                    for k in range(4):
                        mm = pe.transpose(banks[n % 4][:, k * P:(k + 1) * P], uv[:, hf, t, k * P:(k + 1) * P], idm)
                    mm.then_inc(mt_psum, 1)
                for n in range(2 * NT):
                    c, t = divmod(n, NT)
                    if t == 0:
                        wait_unit(OUTU[c])
                    if c == 0:
                        pe.wait_ge(mt_done, 2 * t + 2)
                    if n >= 4:
                        pe.wait_ge(xo_done, n - 3)
                    project(OUTU[c], t, banks[4 + n % 4][:, :]).then_inc(xo_psum, 1)
                    if t == NT - 1:
                        pe.drain().then_inc(unit_done, 1)
                    if n == 2 * NT - 2:
                        norm_transposes(1, range(*NORM2[0]))

                def route(tiles):
                    for t in tiles:
                        pe.wait_ge(xt_done, 2 * NT + 2 * t + 2)
                        for k in range(KD):
                            mm = pe.matmul(banks[4][:, 36 * t:36 * t + 36], xt[:, k, t * P:(t + 1) * P], wr[:, k, :],
                                           start=(k == 0), stop=(k == KD - 1))
                    return mm

                pe.wait_ge(xo_done, 2 * NT - 1)
                pe.wait_ge(wr_loaded, 48 * L + 48)
                route(range(*NORM2[0]))
                norm_transposes(1, range(*NORM2[1]))
                route(range(*NORM2[1]))
                norm_transposes(1, range(*NORM2[2]))
                route(range(*NORM2[2])).then_inc(r_psum, 1)

                pe.wait_ge(chosen_ready, 1)
                pe.matmul(banks[5][:, 0:NT * EXPERTS], before, scr[:, P:P + NT * EXPERTS], start=True, stop=True)
                pe.matmul(banks[6][:, 0:NT * EXPERTS], ones, scr[:, P:P + NT * EXPERTS], start=True, stop=True).then_inc(count_psum, 1)
                for m in range(2 * NT):
                    pe.wait_ge(onehot_ready, m + 1)
                    mm = pe.matmul(banks[5][0:BR, 0:COLS_T], onehot[:, m, 0:BR], onehot[:, m, BR:BR + COLS_T],
                                   start=(m == 0), stop=(m == 2 * NT - 1))
                mm.then_inc(table_psum, 1)
                pe.wait_ge(table_ready, 1)
                pe.drain().then_inc(xin_psum, 1)

                def rows_in(b, q):
                    for k in range(KD):
                        mm = pe.transpose(banks[k // 4][:, (k % 4) * BR:(k % 4 + 1) * BR],
                                          xin[q][:, k:D:KD], ident[0:BR, 0:BR])
                    mm.then_inc(xin_psum, 1)

                def up(b, q, z):
                    for m in range(2):
                        w = expert_up[q][:, 1024 * m:1024 * m + 1024].rearrange("p (k f) -> p k f", k=KD)
                        for k in range(KD):
                            mm = pe.matmul(banks[2 + z][:, BR * m:BR * m + BR], w[:, k, :], xin_t[z][:, k, :],
                                           start=(k == 0), stop=(k == KD - 1))
                    mm.then_inc(gu_psum, 1)

                def down(b, q, z):
                    pe.wait_ge(h_done, b + 3)
                    pe.wait_ge(y_ready, b + 1)
                    for c in range(2):
                        mm = pe.matmul(banks[4 + 2 * z + c][0:BR, :], hidden[z][:, :],
                                       expert_down[q][:, BLK * c:BLK * c + BLK], start=True, stop=True)
                    mm.then_inc(y_psum, 1)

                def rows_step(i, q):
                    pe.wait_ge(x_in[q % SLOTS], 16 * TURNS * L + (16 * i + 16 * (q // SLOTS) + 16))
                    b = SLOTS * i + q
                    if not (isinstance(b, int) and b == 0):
                        pe.wait_ge(xin_ready, 2 * b)
                    rows_in(b, q % SLOTS)

                def where(i, q):
                    return SLOTS + q if isinstance(i, int) and i == 0 and q < 2 else (q - 2) % SLOTS

                def up_step(i, q):
                    b, place = SLOTS * i + q, where(i, q)
                    if place < SLOTS:
                        turn_no = (q - 2) // SLOTS
                        pe.wait_ge(slot[place], 48 * i + (landed(12 + place) + 48 * turn_no + 48))
                    else:
                        pe.wait_ge(extra[place - SLOTS], 48)
                    pe.wait_ge(xin_ready, 2 * b + 2)
                    pe.wait_ge(h_done, b + 1)
                    up(b, place, q % 2)

                def down_step(i, q):
                    down(SLOTS * i + q, where(i, q), q % 2)

                rows_step(0, 0)
                rows_step(0, 1)
                up_step(0, 0)

                def turn_blocks(i):
                    for q in range(1, SLOTS + 1):
                        rows_step(i, q + 1)
                        up_step(i, q)
                        down_step(i, q - 1)

                turn_blocks(0)
                with pe.Fori(1, TURNS - 1) as i:
                    turn_blocks(i)
                for q in range(1, SLOTS):
                    if q + 1 < SLOTS:
                        rows_step(TURNS - 1, q + 1)
                    up_step(TURNS - 1, q)
                    down_step(TURNS - 1, q - 1)
                down_step(TURNS - 1, SLOTS - 1)
                with pe.If(pe.value_load(over_count[:, 0:1], min_val=0, max_val=OVER) != 0):
                    gathered = earlier(pe)
                    with pe.Fori(0, OVER) as v:
                        b = v + EXPERTS
                        pe.wait_ge(x_over, gathered + (16 * v + 16))
                        pe.wait_ge(xin_ready, 2 * b)
                        rows_in(b, 0)
                        pe.wait_ge(over_w, 48 * v + 48)
                        pe.wait_ge(xin_ready, 2 * b + 2)
                        pe.wait_ge(h_done, b + 2)
                        up(b, 0, 0)
                        pe.wait_ge(y_ready, b + 2)
                        down(b, 0, 0)
                next_layer(pe, "pe")

        @block.scalar
        def _(act):
            def squares(t, junk, done):
                act.activation(junk, x[:, t, :], ACT.Square, accum_out=ss[:, t:t + 1]).then_inc(done, 1)

            def rows(phase, t):
                if phase == 0 and t >= 2:
                    act.wait_ge(xt_psum, 2 * (t - 1))
                act.activation(xn2[t] if phase else xn[t % 2], x[:, t, :], ACT.Copy,
                               scale=rs[:, t:t + 1]).then_inc(xn_ready, 1)

            for t in range(NT):
                act.wait_ge(s_x[t], 16)
                squares(t, xt_flat[:, D * t:D * (t + 1)], s_squares)
            act.wait_ge(s_roots, 1)
            with act.Fori(0, DEPTH) as L:
                for t in range(NT):
                    rows(0, t)

                def proj_out(n):
                    u, t = divmod(n, NT)
                    act.wait_ge(proj_psum, n + 1)
                    b = banks[4 + n % 4]
                    if u == 0:
                        ins = act.activation(qkv[:, t, 0:BLK].rearrange("p (j g d) -> p g j d", g=KV, j=GQ),
                                             b[:, :].rearrange("p (g j d) -> p g j d", g=KV, j=GQ), ACT.Copy)
                    elif u == 1:
                        ins = act.activation(qkv[:, t, BLK * u:BLK * u + BLK], b[:, :], ACT.Copy)
                    elif u == 2:
                        ins = act.activation(qkv[:, t, KI0:QKV_W], b[:, 0:QKV_W - KI0], ACT.Copy)
                    else:
                        ins = act.activation(uv[:, u - 3, t, :], b[:, :], ACT.Gelu_apprx_tanh)
                    ins.then_inc(proj_free, 1)

                for n in range(3 * NT):
                    proj_out(n)
                act.wait_ge(kx_psum, 1)
                act.activation(kis[:, :, 0:PAST], banks[0][:, :].rearrange("p (s k) -> p s k", s=2), ACT.Copy).then_inc(kx_done, 1)
                for n in HEAD_JOBS:
                    proj_out(n)
                for i, dst in enumerate((kit, qit[:, 0, :], qit[:, 1, :])):
                    act.wait_ge(kx_psum, i + 2)
                    act.activation(dst, banks[1 + i][:, :], ACT.Copy).then_inc(kx_done, 1)
                act.wait_ge(kx_psum, 5)
                for c in range(4):
                    r = slice(ID * c, ID * c + ID)
                    src = banks[0][r, 0:P].rearrange("p (s q) -> p s q", s=2)[:, :, FRAMES * c:FRAMES * c + FRAMES]
                    ins = act.activation(kis[r, :, PAST:PAST + FRAMES], src, ACT.Copy)
                ins.then_inc(kx_done, 1)
                for at, t in enumerate(IDX_TILES):
                    for h in range(IH):
                        m = IH * at + h
                        act.wait_ge(idx_psum, m + 1)
                        if m >= 2:
                            act.wait_ge(*idx_use(m - 2))
                        act.activation(relu_b[m % 2][:, 0:KEYS[t]], banks[m % 4][:, 0:KEYS[t]], ACT.Relu).then_inc(idx_relu, 1)
                    for n in TAIL_JOBS.get(at, ()):
                        proj_out(n)
                for i, dst in enumerate([kt[:, :]] + [qt[:, j, :] for j in range(GQ)]):
                    act.wait_ge(qk_psum, i + 1)
                    act.activation(dst, banks[0 if i == 0 else 3 + i][:, :], ACT.Copy).then_inc(qk_done, 1)

                def stream_keys(g, step):
                    act.wait_ge(ks_psum, 3 * g + step + 1)
                    act.wait_ge(kv_out, 48 * NT * L + 48 * NT)
                    if step < 2:
                        ins = act.activation(qkv[:, 2 * step:2 * step + 2, SK0[g]:SK0[g] + PAST],
                                             banks[7][:, :].rearrange("p (s k) -> p s k", s=2), ACT.Copy)
                    else:
                        for c in range(2):
                            r = slice(HD * c, HD * c + HD)
                            src = banks[7][r, 0:P].rearrange("p (s q) -> p s q", s=4)[:, :, FRAMES * c:FRAMES * c + FRAMES]
                            ins = act.activation(qkv[r, 0:4, SK0[g] + PAST:SK0[g] + PAST + FRAMES], src, ACT.Copy)
                    ins.then_inc(ks_done, 1)

                def exps(n):
                    t, k = ATT_UNITS[n][0], n % PBUF
                    act.wait_ge(p_raw, n + 1)
                    act.activation(probs[k][:, 0:KEYS[t]], probs[k][:, 0:KEYS[t]], ACT.Exp,
                                   bias=nmx[:, k:k + 1], scale=ATT_SCALE, accum_out=den[:, k:k + 1]).then_inc(p_exp, 1)

                def probs_out(n):
                    t = ATT_UNITS[n][0]
                    act.wait_ge(pt_psum, n + 1)
                    if n >= PBUF:
                        act.wait_ge(pv_done, n - PBUF + 1 if n < NPU + GQ else NPU + 1)
                    w = KEYS[t] if t < PT else 3 * P
                    act.activation(probs_t[n % PBUF][:, 0:w], banks[2 + n % 2][:, 0:w], ACT.Copy).then_inc(pt_done, 1)

                def tile_out(t):
                    act.wait_ge(o_psum, t + 1)
                    act.activation(att[:, :, t * P:(t + 1) * P],
                                   banks[4 + t % 2][:, :].rearrange("p (j q) -> p j q", j=GQ), ACT.Copy).then_inc(o_done, 1)

                exps(0)
                for n in range(NAU):
                    if n in GATE_STEPS and GATE_STEPS[n][1] == KD:
                        t = GATE_STEPS[n][0]
                        act.wait_ge(early_psum, t + 1)
                        act.activation(early_gate[t], banks[7][:, :], ACT.Sigmoid).then_inc(early_done, 1)
                    if n in KEYS_AT:
                        stream_keys(*KEYS_AT[n])
                    if n + 1 < NAU:
                        exps(n + 1)
                    if n >= 1:
                        probs_out(n - 1)
                    if n >= 2 and ATT_UNITS[n - 2][0] != ATT_UNITS[n - 1][0]:
                        tile_out(ATT_UNITS[n - 2][0])
                probs_out(NAU - 1)
                tile_out(PT)
                for m in range(2):
                    act.wait_ge(sw_psum, m + 1)
                    act.activation(scr[:, 512 * m:512 * m + 512], banks[6 + m][:, :], ACT.Copy).then_inc(sw_done, 1)
                for t in range(NT):
                    act.wait_ge(sgt_psum, t + 1)
                    act.activation(sgt[:, :, t * P:(t + 1) * P],
                                   banks[4 + t % 4][:, :].rearrange("p (g q) -> p g q", g=SG), ACT.Copy).then_inc(sgt_done, 1)
                for n in range(2 * NT):
                    act.wait_ge(mg_gate, n + 1)
                    if n >= 2:
                        act.wait_ge(mg_done, n - 1)
                    for m in range(1 if n < EARLY else 0, 2):
                        c0 = 1024 * (n % 2) + 512 * m
                        ins = act.activation(scr[:, c0:c0 + 512], banks[4 * (n % 2) + m][:, :], ACT.Sigmoid)
                    ins.then_inc(mg_sig, 1)
                for n in range(2 * NT):
                    t, hf = divmod(n, 2)
                    act.wait_ge(mt_psum, n + 1)
                    act.activation(xt[:, 4 * hf:4 * hf + 4, t * P:(t + 1) * P],
                                   banks[n % 4][:, :].rearrange("p (k q) -> p k q", k=4), ACT.Copy).then_inc(mt_done, 1)
                for i, (t0, t1) in enumerate(NORM2):
                    for t in range(t0, t1):
                        act.wait_ge(xo_done, NT + t + 1)
                        squares(t, xn2[t], sq_done)
                    act.wait_ge(rs_ready, i + 1)
                    for t in range(t0, t1):
                        rows(1, t)
                for m in range(2):
                    act.wait_ge(r_sub, m + 1)
                    v = (eg, e8)[m]
                    act.activation(v, v, ACT.Exp).then_inc(r_exp, 1)
                act.wait_ge(table_ready, 1)
                act.drain().then_inc(y_ready, 2)

                def silu(b, z):
                    act.wait_ge(gu_psum, b + 1)
                    act.activation(hidden[z], banks[2 + z][:, 0:BR], ACT.Silu).then_inc(silu_done, 1)

                def results(b, z):
                    act.wait_ge(y_psum, b + 1)
                    for c in range(2):
                        ins = act.activation(yout[z][:, BLK * c:BLK * c + BLK], banks[4 + 2 * z + c][0:BR, :], ACT.Copy)
                    ins.then_inc(y_ready, 1)

                def turn_out(i, last):
                    for q in range(SLOTS):
                        if not last or q + 1 < SLOTS:
                            silu(SLOTS * i + (q + 1), (q + 1) % 2)
                        act.wait_ge(y_out[q % YBUF], 16 * (EXPERTS // YBUF) * L + (32 * i + 16 * (q // YBUF) + 16))
                        results(SLOTS * i + q, q % 2)

                silu(0, 0)
                with act.Fori(0, TURNS - 1) as i:
                    turn_out(i, False)
                turn_out(TURNS - 1, True)
                with act.If(act.value_load(over_count[:, 0:1], min_val=0, max_val=OVER) != 0):
                    sent = earlier(act)
                    with act.Fori(0, OVER) as v:
                        silu(v + EXPERTS, 0)
                        act.wait_ge(y_out[0], 16 * (EXPERTS // YBUF) * L + (16 * (EXPERTS // YBUF) + 16))
                        act.sem_inc(over_free, 1)
                        act.wait_ge(y_over, sent + (16 * v + 16))
                        results(v + EXPERTS, 0)
                for t in range(NT):
                    act.wait_ge(x_new, t + 1)
                    squares(t, xt_flat[:, D * t:D * (t + 1)], sq_done)
                next_layer(act, "act")
            for t in range(NT):
                act.activation(x[:, t, :], x[:, t, :], ACT.Copy, scale=rs[:, t:t + 1]).then_inc(s_fin_x, 1)

        @block.vector
        def _(dve):
            V = nc.vector
            count = [0]

            def then(ins):
                count[0] += 1
                ins.then_inc(dve_chain, 1)
                dve.wait_ge(dve_chain, count[0])

            def rows_transposed(phase, t, L):
                for hf in range(2):
                    n = 2 * t + hf
                    dve.wait_ge(xt_psum, 2 * NT * phase + n + 1)
                    V.tensor_tensor(xt[:, 4 * hf:4 * hf + 4, t * P:(t + 1) * P],
                                    banks[n % 4][:, :].rearrange("p (k q) -> p k q", k=4),
                                    gain[:, bass.ds(L, 1), phase, 4 * hf:4 * hf + 4].rearrange("p l k -> p (l k)").unsqueeze(2).broadcast_to([P, 4, P]),
                                    ALU.mult).then_inc(xt_done, 1)

            def rotate(t, c0, heads, d, table):
                h2 = d // 2
                src = qkv[:, t, c0:c0 + heads * d].rearrange("p (h a i) -> p h a i", a=2, i=h2)
                cos, sin = table[:, 0:h2], table[:, h2:d]
                w = heads * d
                t1 = scr[:, 0:w].rearrange("p (h a i) -> p h a i", a=2, i=h2)
                t2 = scr[:, 1024:1024 + w].rearrange("p (h a i) -> p h a i", a=2, i=h2)
                bc = [P, heads, h2]
                for z in range(2):
                    V.tensor_tensor(t1[:, :, z, :], src[:, :, z, :], over(cos, heads, 1, bc), ALU.mult)
                    ins = V.tensor_tensor(t2[:, :, z, :], src[:, :, 1 - z, :], over(sin, heads, 1, bc), ALU.mult)
                then(ins)
                V.tensor_tensor(src[:, :, 0, :], t1[:, :, 0, :], t2[:, :, 0, :], ALU.subtract)
                then(V.tensor_tensor(src[:, :, 1, :], t1[:, :, 1, :], t2[:, :, 1, :], ALU.add))

            def select(tiles):
                last = {t: count[0] for t in tiles}

                def step(t, make, *args, **kwargs):
                    dve.wait_ge(dve_chain, last[t])
                    make(*args, **kwargs).then_inc(dve_chain, 1)
                    count[0] += 1
                    last[t] = count[0]

                for r in range(TOPK_P // 8):
                    turn = [(t, score(t), bests[i], TOPK_P if t < PT else TOPK_S) for i, t in enumerate(tiles)]
                    turn = [u for u in turn if 8 * r < u[3]]
                    for t, s, best, k in turn:
                        step(t, V.max, best, s)
                    for t, s, best, k in turn:
                        if k - 8 * r < 8:
                            step(t, V.memset, best[:, k - 8 * r:8], SEL)
                    for t, s, best, k in turn:
                        step(t, V.match_replace, out=s, in_to_replace=best, in_values=s, imm_value=SEL)
                for t in tiles:
                    step(t, V.tensor_scalar, score(t), score(t), SEL, OFF, ALU.not_equal, ALU.mult)
                dve.wait_ge(dve_chain, count[0])

            def gates():
                dve.wait_ge(r_exp, 2)
                then(V.tensor_reduce(gsum, eg, AX.X, ALU.add))
                then(V.tensor_tensor(e8, e8, w16e[:, :, 0:NE], ALU.mult))
                then(V.tensor_reduce(esum, e8, AX.X, ALU.add))
                then(V.tensor_tensor(escale, gsum, esum, ALU.mult))
                then(V.reciprocal(gw, escale))
                then(V.tensor_tensor(e8, e8, gw.unsqueeze(2).broadcast_to([P, NT, NE]), ALU.mult))
                for t in range(NT):
                    ins = V.tensor_tensor(gate[:, t, :].rearrange("p (g e) -> p g e", g=NG),
                                          over(e8[:, t, :], NG, 1, [P, NG, NE]),
                                          hot[:, t, :].unsqueeze(2).broadcast_to([P, NG, NE]), ALU.mult)
                then(ins)

            def dispatch(L):
                for t in range(NT):
                    ins = V.tensor_tensor(chosen[:, t, :].rearrange("p (g e) -> p g e", g=NG),
                                          over(w16e[:, t, 0:NE], NG, 1, [P, NG, NE]),
                                          hot[:, t, :].unsqueeze(2).broadcast_to([P, NG, NE]), ALU.mult)
                then(ins)
                V.nop().then_inc(chosen_ready, 1)
                dve.wait_ge(wr_loaded, 48 * L + 48)
                then(V.tensor_tensor(number, chosen, over(ids[:, 1:EXPERTS + 1], NT, 1, [P, NT, EXPERTS]), ALU.mult))
                V.tensor_reduce(number_k[:, 0, :], number, AX.X, ALU.max)
                then(V.tensor_reduce(number_k[:, 1, :], number, AX.X, ALU.add))
                then(V.tensor_tensor(number_k[:, 1, :], number_k[:, 1, :], number_k[:, 0, :], ALU.subtract))
                each = [P, 2, NT, EXPERTS]
                then(V.tensor_tensor(mine, number.unsqueeze(1).broadcast_to(each),
                                     number_k.unsqueeze(3).broadcast_to(each), ALU.is_equal))
                dve.wait_ge(count_psum, 1)
                V.tensor_copy(total, banks[6][:, 0:NT * EXPERTS].rearrange("p (t e) -> p t e", t=NT))
                then(V.memset(base[:, 0, :], 0.0))
                for t in range(1, NT):
                    then(V.tensor_tensor(base[:, t, :], base[:, t - 1, :], total[:, t - 1, :], ALU.add))
                V.tensor_tensor(rank, banks[5][:, 0:NT * EXPERTS].rearrange("p (t e) -> p t e", t=NT), base, ALU.add)
                then(V.tensor_tensor(size, base[:, NT - 1, :], total[:, NT - 1, :], ALU.add))
                V.tensor_tensor(part, mine, rank.unsqueeze(1).broadcast_to(each), ALU.mult)
                then(V.tensor_scalar(need, size, float(BR), None, ALU.is_gt))
                then(V.tensor_reduce(rank_k, part, AX.X, ALU.add))
                V.tensor_scalar(beyond_k, rank_k, float(BR), None, ALU.is_ge)
                then(V.tensor_scalar(whole_k, rank_k, float(BR), None, ALU.is_ge))
                for j in range(2, -(-ROWS // BR)):
                    V.scalar_tensor_tensor(need, size, float(BR * j), need, ALU.is_gt, ALU.add)
                    then(V.scalar_tensor_tensor(whole_k, rank_k, float(BR * j), whole_k, ALU.is_ge, ALU.add))
                src, dst, step = need, scan_a, 1
                while step < EXPERTS:
                    V.tensor_copy(dst[:, 0:step], src[:, 0:step])
                    then(V.tensor_tensor(dst[:, step:], src[:, step:], src[:, :EXPERTS - step], ALU.add))
                    src, dst, step = dst, (scan_b if dst is scan_a else scan_a), 2 * step
                then(V.tensor_tensor(start, src, need, ALU.subtract))
                then(V.tensor_tensor(part, mine, start.unsqueeze(1).unsqueeze(1).broadcast_to(each), ALU.mult))
                then(V.tensor_reduce(start_k, part, AX.X, ALU.add))
                V.scalar_tensor_tensor(pair_at[:, 0, :, :], whole_k, -float(BR), rank_k, ALU.mult, ALU.add)
                then(V.tensor_tensor(start_k, start_k, number_k, ALU.subtract))
                then(V.scalar_tensor_tensor(start_k, start_k, float(EXPERTS), beyond_k, ALU.add, ALU.mult))
                then(V.tensor_tensor(start_k, start_k, whole_k, ALU.add))
                then(V.scalar_tensor_tensor(pair_at[:, 1, :, :], number_k, -1.0, start_k, ALU.add, ALU.add))
                for m in range(2 * NT):
                    k, t = divmod(m, NT)
                    V.tensor_scalar(onehot[:, m, 0:BR], ids[:, 0:BR], pair_at[:, 0, k, t:t + 1], None, ALU.is_equal)
                    V.tensor_scalar(onehot[:, m, BR:BR + COLS_T], ids[:, 0:COLS_T], pair_at[:, 1, k, t:t + 1],
                                    ids[:, BR + m:BR + m + 1], ALU.is_equal, ALU.mult).then_inc(onehot_ready, 1)
                V.tensor_copy(over_count, src[0:1, EXPERTS - 1:EXPERTS])
                V.tensor_scalar(over_new, src[0:1, EXPERTS - 1:EXPERTS], 0.0, 16.0 * OVER, ALU.is_gt, ALU.mult)
                then(V.tensor_copy(over_past, over_sum))
                V.tensor_tensor(over_sum, over_sum, over_new, ALU.add)
                then(V.tensor_tensor(begun, over(start[0:1, :], OVER, 1, [1, OVER, EXPERTS]),
                                     ids[0:1, 0:OVER].unsqueeze(2).broadcast_to([1, OVER, EXPERTS]), ALU.is_le))
                then(V.tensor_reduce(begun_count, begun, AX.X, ALU.add))
                then(V.tensor_scalar(over_expert, begun_count, -1.0, None, ALU.add))
                V.nop().then_inc(experts_known, 1)
                dve.wait_ge(table_psum, 1)
                pair_1 = banks[5][0:BR, 0:COLS_T]
                then(V.tensor_scalar(pads, pair_1, 0.0, NOWHERE, ALU.is_equal, ALU.mult))
                then(V.scalar_tensor_tensor(wide[:, 1, :], pair_1, -1.0, pads, ALU.add, ALU.add))
                then(V.tensor_scalar(wide[:, 0, :], wide[:, 1, :], float(ROWS), -float(ROWS), ALU.is_ge, ALU.mult))
                then(V.tensor_tensor(wide[:, 0, :], wide[:, 0, :], wide[:, 1, :], ALU.add))
                then(V.tensor_copy(table, wide))
                V.nop().then_inc(h_done, 2)
                V.nop().then_inc(table_ready, 1)
                gates()
                each = [P, 2, NT, EXPERTS]
                then(V.tensor_tensor(part, mine, gate.unsqueeze(1).broadcast_to(each), ALU.mult))
                then(V.tensor_reduce(pair_at[:, 2, :, :], part, AX.X, ALU.add))

            dve.wait_ge(s_gain, 32 * DEPTH)
            with dve.Fori(0, DEPTH) as L:
                count[0] = 0
                for t in range(NT):
                    rows_transposed(0, t, L)
                dve.wait_ge(s_rope, 16)
                dve.wait_ge(s_const, 1)
                for t in range(NT):
                    dve.wait_ge(proj_free, 2 * NT + t + 1)
                    dve.wait_ge(xt_psum, 2 * NT)
                    k_all = HEADS + KV
                    rotate(t, 0, k_all, HD, rope_t[:, t, 0:HD])
                    rotate(t, QI0, IH + 1, ID, rope_t[:, t, HD:HD + ID])
                    V.tensor_scalar(qkv[:, t, WI0:QKV_W], qkv[:, t, WI0:QKV_W], IH ** -0.5, None,
                                    ALU.mult).then_inc(rope_done, 1)
                for j in range(2):
                    dve.wait_ge(kx_psum, 6 + j)
                    for s in range(2):
                        ins = V.tensor_tensor(qis[:, s, 4 * j:4 * j + 4, :],
                                              banks[1 + j][:, :].rearrange("p (h q) -> p h q", h=4),
                                              over(quad[:, s, :], 4, 1, [P, 4, P]), ALU.mult)
                    ins.then_inc(qis_done, 1)
                V.memset(score(0)[:, :], 0.0).then_inc(dve_chain, 1)
                count[0] += 1
                dve.wait_ge(dve_chain, count[0])
                then(V.memset(score(0)[0:64, 64:P], OFF))
                dve.wait_ge(rope_done, NT)
                key_scores(nc.vector, 0)
                then(V.memset(score(IDX_TILES[0])[0:64, KEYS[IDX_TILES[0]] - 64:], NEG))
                select(IDX_TILES[:1])
                key_scores(nc.vector, 2)
                key_scores(nc.vector, 3)
                dve.wait_ge(score_done, 1)
                for t in IDX_TILES[1:]:
                    if t < PT:
                        ins = V.memset(score(t)[0:64, KEYS[t] - 64:], NEG)
                then(ins)
                select(IDX_TILES[1:])

                def ln_step(i):
                    t, what = divmod(i, 2)
                    if i == 0:
                        dve.wait_ge(proj_free, 5 * NT)
                    if what == 0:
                        then(V.bn_stats(bns, uv[:, 1, t, :]))
                    else:
                        then(V.bn_aggr(moments[:, t, :], bns))
                    if i == 2 * NT - 1:
                        V.nop().then_inc(ln_stat, 1)

                def masked_logits(n):
                    t = ATT_UNITS[n][0]
                    if n in QUERIES_AT:
                        g = QUERIES_AT[n]
                        dve.wait_ge(ks_psum, 7 + g)
                        for s in range(4):
                            V.tensor_tensor(qts[:, s, :, :], banks[7][:, :].rearrange("p (j q) -> p j q", j=GQ),
                                            over(pair[:, s, :], GQ, 1, [P, GQ, P]), ALU.mult).then_inc(qts_done, 1)
                    k = n % PBUF
                    dve.wait_ge(s_psum, n + 1)
                    if n >= PBUF:
                        dve.wait_ge(pt_psum, n - PBUF + 1)
                    then(V.tensor_tensor_reduce(out=probs[k][:, 0:KEYS[t]], in0=banks[SBANK[n % len(SBANK)]][:, 0:KEYS[t]], in1=score(t),
                                                scale=1.0, scalar=NEG, op0=ALU.add, op1=ALU.max,
                                                accum_out=mx[:, k:k + 1]))
                    V.tensor_scalar(nmx[:, k:k + 1], mx[:, k:k + 1], -ATT_SCALE, None, ALU.mult).then_inc(p_raw, 1)

                def normalise(n):
                    t = ATT_UNITS[n][0]
                    k = n % PBUF
                    p = probs[k][:, 0:KEYS[t]]
                    dve.wait_ge(p_exp, n + 1)
                    then(V.reciprocal(rden[:, k:k + 1], den[:, k:k + 1]))
                    ins = V.tensor_scalar(p, p, rden[:, k:k + 1], None, ALU.mult)
                    if t == PT:
                        then(ins)
                        ins = V.tensor_tensor(probs[k][:, 3 * P:4 * P].rearrange("p (b i) -> p b i", b=STREAMS),
                                              over(p[:, PAST:PAST + FRAMES], STREAMS, 1, [P, STREAMS, FRAMES]),
                                              own[:, :].unsqueeze(2).broadcast_to([P, STREAMS, FRAMES]), ALU.mult)
                    ins.then_inc(p_ready, 1)

                masked_logits(0)
                masked_logits(1)
                for n in range(NAU):
                    normalise(n)
                    if n + 2 < NAU:
                        masked_logits(n + 2)
                    if n < 2 * NT:
                        ln_step(n)

                dve.wait_ge(params, 16 * 19 * L + 16 * 19)
                dve.wait_ge(slot[SU % SLOTS], landed(SU))
                sw = ring[:, SU % SLOTS, :]
                w4 = sw[:, 0:512].rearrange("p (g j) -> p g j", g=SG)
                low = over(tril[:, :], SG, 1, [P, SG, P])
                V.tensor_tensor(w4, w4, low, ALU.mult).then_inc(swm_ready, 1)
                ws = sw[:, 1024:1536].rearrange("p (g b j) -> p g b j", g=SG, b=STREAMS)
                for g in range(SG):
                    ins = V.tensor_tensor(ws[:, g, :, :], over(corner[:, g, :], STREAMS, 1, [P, STREAMS, FRAMES]),
                                          own[:, :].unsqueeze(2).broadcast_to([P, STREAMS, FRAMES]), ALU.mult)
                then(ins)
                ws4 = sw[:, 1024:1536].rearrange("p (g j) -> p g j", g=SG)
                V.tensor_tensor(ws4, ws4, low, ALU.mult).then_inc(swm_ready, 1)
                for t in range(NT):
                    dve.wait_ge(sg_psum, t + 1)
                    for g in range(SG):
                        u = uv[:, 0, t, g * P:(g + 1) * P]
                        ins = V.scalar_tensor_tensor(u, banks[t % 4][:, g * P:(g + 1) * P],
                                                     sbias[:, t // PT, g:g + 1], u, ALU.add, ALU.mult)
                    ins.then_inc(sg_used, 1)
                for n in range(2 * NT):
                    c, t = divmod(n, NT)
                    dve.wait_ge(mg_sig, n + 1)
                    dve.wait_ge(mg_proj, n + 1)
                    b = banks[4 * (n % 2):4 * (n % 2) + 4]
                    t1 = scr[:, 1024 * (n % 2):1024 * (n % 2) + 512]
                    t2 = scr[:, 1024 * (n % 2) + 512:1024 * (n % 2) + 1024]
                    V.tensor_tensor(t1, early_gate[n] if n < EARLY else t1, b[2][:, :], ALU.mult)
                    then(V.tensor_tensor(t2, t2, b[3][:, :], ALU.mult))
                    if n == 2 * NT - 1:
                        dve.wait_ge(rows_sent, 1)
                    V.tensor_tensor(uv[:, c, t, :], t1, t2, ALU.add).then_inc(mg_done, 1)
                def residual(n):
                    c, t = divmod(n, NT)
                    dve.wait_ge(xo_psum, n + 1)
                    xs = x[:, t, BLK * c:BLK * c + BLK]
                    V.tensor_tensor(xs, xs, banks[4 + n % 4][:, :], ALU.add).then_inc(xo_done, 1)

                for n in range(2 * NT - 1):
                    residual(n)
                for t in range(NT - 2):
                    rows_transposed(1, t, L)
                residual(2 * NT - 1)
                rows_transposed(1, NT - 2, L)
                rows_transposed(1, NT - 1, L)
                for w_, r_ in ((w16, r8), (w16e, r8e)):
                    V.memset(w_, NEG)
                    V.memset(r_, NEG)
                V.memset(ones, 1.0)
                then(V.tensor_scalar(before, tril[:, :], -1.0, 1.0, ALU.mult, ALU.add))

                dve.wait_ge(r_psum, 1)
                then(V.tensor_tensor(logit, banks[4][:, 0:36 * NT].rearrange("p (t c) -> p t c", t=NT),
                                     over(rbias[:, :], NT, 1, [P, NT, 36]), ALU.add))
                then(V.tensor_copy(w16[:, :, 0:NG], logit[:, :, 0:NG]))
                for t in range(NT):
                    ins = V.max(m8[:, t, :], w16[:, t, :])
                then(ins)
                V.tensor_tensor(eg, logit[:, :, 0:NG], m8[:, :, 0:1].broadcast_to([P, NT, NG]),
                                ALU.subtract).then_inc(r_sub, 1)
                then(V.tensor_copy(r8[:, :, 0:1], m8[:, :, 0:1]))
                for t in range(NT):
                    ins = V.match_replace(out=w16[:, t, :], in_to_replace=r8[:, t, :], in_values=w16[:, t, :], imm_value=SEL)
                then(ins)
                then(V.tensor_scalar(hot, w16[:, :, 0:NG], SEL, None, ALU.is_equal))
                for t in range(NT):
                    ins = V.tensor_tensor(picked[:, t, :, :], logit[:, t, NG:].rearrange("p (g e) -> p g e", g=NG),
                                          hot[:, t, :].unsqueeze(2).broadcast_to([P, NG, NE]), ALU.mult)
                then(ins)
                then(V.tensor_reduce(l8, picked.rearrange("p t g e -> p t e g"), AX.X, ALU.add))
                then(V.tensor_copy(w16e[:, :, 0:NE], l8))
                for t in range(NT):
                    ins = V.max(m8e[:, t, :], w16e[:, t, :])
                then(ins)
                V.tensor_tensor(e8, l8, m8e[:, :, 0:1].broadcast_to([P, NT, NE]), ALU.subtract).then_inc(r_sub, 1)
                then(V.tensor_copy(r8e[:, :, 0:2], m8e[:, :, 0:2]))
                for t in range(NT):
                    ins = V.match_replace(out=w16e[:, t, :], in_to_replace=r8e[:, t, :], in_values=w16e[:, t, :], imm_value=SEL)
                then(ins)
                then(V.tensor_scalar(w16e[:, :, 0:NE], w16e[:, :, 0:NE], SEL, None, ALU.is_equal))
                dispatch(L)

                def rows_out(b, z):
                    dve.wait_ge(xin_psum, b + 2)
                    for hf in range(2):
                        V.tensor_tensor(xin_t[z][:, 4 * hf:4 * hf + 4, :],
                                        banks[hf][:, 0:4 * BR].rearrange("p (k r) -> p k r", k=4),
                                        gain[:, bass.ds(L, 1), 1, 4 * hf:4 * hf + 4].rearrange("p l k -> p (l k)").unsqueeze(2).broadcast_to([P, 4, BR]),
                                        ALU.mult).then_inc(xin_ready, 1)

                def hidden_rows(b, z):
                    dve.wait_ge(silu_done, b + 1)
                    V.tensor_tensor(hidden[z], hidden[z], banks[2 + z][:, BR:2 * BR], ALU.mult).then_inc(h_done, 1)

                def turn_mid(i, last):
                    for q in range(SLOTS):
                        if not last or q + 1 < SLOTS:
                            rows_out(SLOTS * i + (q + 1), (q + 1) % 2)
                        hidden_rows(SLOTS * i + q, q % 2)

                rows_out(0, 0)
                with dve.Fori(0, TURNS - 1) as i:
                    turn_mid(i, False)
                turn_mid(TURNS - 1, True)
                with dve.If(dve.value_load(over_count[:, 0:1], min_val=0, max_val=OVER) != 0):
                    with dve.Fori(0, OVER) as v:
                        rows_out(v + EXPERTS, 0)
                        hidden_rows(v + EXPERTS, 0)
                for t in range(NT):
                    dve.wait_ge(combine_in[t], 16)
                    for k in range(2):
                        ins = V.scalar_tensor_tensor(x[:, t, :], pairs(t)[:, k, :], pair_at[:, 2, k, t:t + 1], x[:, t, :],
                                                     ALU.mult, ALU.add)
                        if k == 0:
                            then(ins)
                    ins.then_inc(x_new, 1)
                next_layer(dve, "dve")

            count[0] = 0
            dve.wait_ge(s_rope, 32)
            for t in range(NT):
                dve.wait_ge(s_fin_x, t + 1)
                V.tensor_tensor(x[:, t, :], x[:, t, :], fin_gain, ALU.mult).then_inc(s_fin, 1)


_INS = ("x_prompt x_sample cache_k cache_v cache_kidx norm1 w_in sgu_ln_g sgu_ln_b sgu_w sgu_b w_pa w_pb w_out "
        "norm2 w_rg b_rg w_re b_re w_eg w_eu w_ed final_norm").split()
_OUTS = [(1, SEQ, D), (STREAMS, FRAMES, D), (DEPTH, 1, SEQ, KV, HD), (DEPTH, 1, SEQ, KV, HD), (DEPTH, 1, SEQ, ID),
         (DEPTH, STREAMS, FRAMES, KV, HD), (DEPTH, STREAMS, FRAMES, KV, HD), (DEPTH, STREAMS, FRAMES, ID),
         (DEPTH, STREAMS, FRAMES, SW)]


def _rope_table():
    pos = np.concatenate([np.arange(SEQ), PAST + np.tile(np.arange(FRAMES), STREAMS)]).astype(np.float32)
    parts = []
    for d in (HD, ID):
        inv = np.float32(10000.0) ** (-np.arange(0, d, 2, dtype=np.float32) / np.float32(d))
        ang = pos[:, None] * inv[None, :].astype(np.float32)
        parts += [np.cos(ang), np.sin(ang)]
    return np.concatenate(parts, axis=1).astype(np.float32).reshape(NT, P, HD + ID)


def _ids():
    pairs = 1 + np.arange(2 * ROWS).reshape(2 * NT, P).T
    return np.concatenate([np.tile(np.arange(BR), (P, 1)), pairs], axis=1).astype(np.float32)


def kernel(**inputs):
    import concourse.bacc as bacc
    from concourse.bass_utils import run_bass_kernel_spmd

    nc = bacc.Bacc("TRN2", target_bir_lowering=False, num_devices=1)
    arrays, a = {}, {}
    for name in _INS:
        arrays[f"in_{name}"] = v = np.ascontiguousarray(inputs[name])
        a[name] = nc.dram_tensor(f"in_{name}", v.shape, F32, kind="ExternalInput").ap()
    for name, v in (("rope", _rope_table()), ("ids", _ids())):
        arrays[f"in_{name}"] = v
        a[name] = nc.dram_tensor(f"in_{name}", v.shape, F32, kind="ExternalInput").ap()
    o = [nc.dram_tensor(f"out_{i}", s, F32, kind="ExternalOutput").ap() for i, s in enumerate(_OUTS)]
    build(nc, a, o)
    r = run_bass_kernel_spmd(nc, [arrays], core_ids=[0])
    return tuple(r.results[0][f"out_{i}"] for i in range(len(_OUTS)))
```
